# Optimizing a Trainium2 kernel written in Bass

```python
import jax, jax.numpy as jnp
from jax import lax
import numpy as np

D_MODEL = 2048
BATCH = 1
SEQ = 256
DEPTH = 1
DEC_BATCH = 8
DEC_SEQ = 4
PAST_LEN = 2048
PAGE_SIZE = 128

N_META = 16
D_CONV = D_MODEL
CONV_W = 3
GLA_HEADS = 4
GLA_DK = D_MODEL // 2 // GLA_HEADS
GLA_DV = D_MODEL // GLA_HEADS
GLA_HK = GLA_HEADS * GLA_DK
GLA_HV = GLA_HEADS * GLA_DV
GATE_RANK = 16
GATE_NORM = 16.0
CHUNK = 64
D_FF = 4 * D_MODEL
ALPHA = (2 * DEPTH) ** 0.25
BETA = (8 * DEPTH) ** -0.25
EPS = 1e-5
SPLITS = (D_CONV, D_CONV, D_CONV, GLA_HK, GLA_HK, GLA_HV, GLA_HV, GATE_RANK, D_MODEL, D_MODEL)
D_IN_PROJ = D_CONV * 3 + GLA_HK * 2 + GLA_HV * 2 + GATE_RANK + D_MODEL * 2

kernel_name = 'gated_conv_gla_hybrid_step'

def layer_norm(x, w, b):
    xf = x.astype(jnp.float32)
    mu = jnp.mean(xf, axis=-1, keepdims=True)
    var = jnp.mean(jnp.square(xf - mu), axis=-1, keepdims=True)
    y = (xf - mu) * lax.rsqrt(var + EPS)
    return (y * w.astype(jnp.float32) + b.astype(jnp.float32)).astype(x.dtype)

def short_conv(u, state, w):
    L = u.shape[1]
    full = jnp.concatenate([state.astype(u.dtype), u], axis=1)
    y = full[:, 0:L] * w[0]
    for j in range(1, CONV_W):
        y = y + full[:, j:j + L] * w[j]
    return y, full[:, L:]

def gla_chunk(s, inp):
    q, k, v, gk = inp
    c = q.shape[2]
    b = jnp.cumsum(gk, axis=2)
    causal = jnp.tril(jnp.ones((c, c), dtype=bool))
    diff = b[:, :, :, None, :] - b[:, :, None, :, :]
    decay = jnp.exp(jnp.where(causal[None, None, :, :, None], diff, -jnp.inf))
    a = jnp.einsum('nhtd,nhsd,nhtsd->nhts', q, k, decay)
    o = jnp.einsum('nhts,nhsv->nhtv', a, v) + jnp.einsum('nhtd,nhdv->nhtv', q * jnp.exp(b), s)
    b_last = b[:, :, -1:, :]
    s_new = jnp.exp(b_last[:, :, 0, :])[..., None] * s + jnp.einsum('nhsd,nhsv->nhdv', k * jnp.exp(b_last - b), v)
    return s_new, o

def gla_sequence(q, k, v, gk, s0, n_lead):
    s = s0.astype(jnp.float32)
    outs = []
    L = q.shape[2]
    lead = n_lead + (L - n_lead) % CHUNK
    bounds = [0, n_lead, lead] if n_lead else [0, lead]
    for lo, hi in zip(bounds[:-1], bounds[1:]):
        if hi > lo:
            s, o = gla_chunk(s, (q[:, :, lo:hi], k[:, :, lo:hi], v[:, :, lo:hi], gk[:, :, lo:hi]))
            outs.append(o)
    n_chunks = (L - lead) // CHUNK
    if n_chunks:
        N, H = q.shape[0], q.shape[1]
        def to_chunks(a):
            return jnp.moveaxis(a[:, :, lead:].reshape(N, H, n_chunks, CHUNK, a.shape[-1]), 2, 0)
        s, o = lax.scan(gla_chunk, s, (to_chunks(q), to_chunks(k), to_chunks(v), to_chunks(gk)))
        outs.append(jnp.moveaxis(o, 0, 2).reshape(N, H, n_chunks * CHUNK, o.shape[-1]))
    return jnp.concatenate(outs, axis=2), s

def token_mixer(u, conv_state, gla_state, n_lead, w_in, conv_w, w_a2, b_a2, gn_w, w_o):
    N, L, _ = u.shape
    idx, acc = [], 0
    for sz in SPLITS[:-1]:
        acc += sz
        idx.append(acc)
    proj = u @ w_in
    cb, cc, cx, q, k, v, g, a1, ga, gb = jnp.split(proj, idx, axis=-1)
    conv_out, conv_new = short_conv(cc * cx, conv_state, conv_w)
    y_a = cb * conv_out
    gk = jax.nn.log_sigmoid((a1 @ w_a2 + b_a2).astype(jnp.float32)) / GATE_NORM
    def heads(a, d):
        return a.reshape(N, L, GLA_HEADS, d).transpose(0, 2, 1, 3).astype(jnp.float32)
    o, gla_new = gla_sequence(heads(q, GLA_DK) * (GLA_DK ** -0.5), heads(k, GLA_DK),
                              heads(v, GLA_DV), heads(gk, GLA_DK), gla_state, n_lead)
    o = o * lax.rsqrt(jnp.mean(jnp.square(o), axis=-1, keepdims=True) + EPS) * gn_w.astype(jnp.float32)
    o = o.transpose(0, 2, 1, 3).reshape(N, L, GLA_HV).astype(u.dtype)
    y_b = o * jax.nn.silu(g)
    m = jax.nn.sigmoid(ga) * y_a + jax.nn.sigmoid(gb) * y_b
    return m @ w_o, conv_new, gla_new

def trunk(h, conv_states, gla_states, n_lead, ln_in_w, ln_in_b, w_in, conv_w, w_a2, b_a2, gn_w,
          w_o, ln1_w, ln1_b, w1, w2, ln2_w, ln2_b):
    h = layer_norm(h, ln_in_w, ln_in_b)
    conv_new, gla_new = [], []
    for l in range(DEPTH):
        mix, cs, gs = token_mixer(h, conv_states[l], gla_states[l], n_lead, w_in[l], conv_w[l],
                                  w_a2[l], b_a2[l], gn_w[l], w_o[l])
        h = layer_norm(ALPHA * h + mix, ln1_w[l], ln1_b[l])
        f = jnp.square(jax.nn.relu(h @ w1[l])) @ w2[l]
        h = layer_norm(ALPHA * h + f, ln2_w[l], ln2_b[l])
        conv_new.append(cs)
        gla_new.append(gs)
    return h, jnp.stack(conv_new), jnp.stack(gla_new)

def setup_inputs(seed: int = 0) -> dict:
    key = jax.random.key(seed)
    ks = jax.random.split(key, 20)
    f32 = jnp.float32
    n = lambda k, shape, s: jax.random.normal(k, shape, f32) * s
    return {
        'x_prompt': n(ks[0], (BATCH, SEQ, D_MODEL), 1.0),
        'x_sample': n(ks[1], (DEC_BATCH, DEC_SEQ, D_MODEL), 1.0),
        'state_conv': n(ks[2], (DEPTH, DEC_BATCH, CONV_W - 1, D_CONV), 1.0),
        'state_gla': n(ks[3], (DEPTH, DEC_BATCH, GLA_HEADS, GLA_DK, GLA_DV), 1.0),
        'meta': n(ks[4], (N_META, D_MODEL), 1.0),
        'ln_in_w': 1.0 + n(ks[5], (D_MODEL,), 0.02),
        'ln_in_b': n(ks[6], (D_MODEL,), 0.02),
        'w_in': n(ks[7], (DEPTH, D_MODEL, D_IN_PROJ), D_MODEL ** -0.5),
        'conv_w': n(ks[8], (DEPTH, CONV_W, D_CONV), CONV_W ** -0.5),
        'w_a2': n(ks[9], (DEPTH, GATE_RANK, GLA_HK), GATE_RANK ** -0.5),
        'b_a2': n(ks[10], (DEPTH, GLA_HK), 0.1),
        'gn_w': 1.0 + n(ks[11], (DEPTH, GLA_DV), 0.02),
        'w_o': n(ks[12], (DEPTH, D_MODEL, D_MODEL), BETA * D_MODEL ** -0.5),
        'ln1_w': 1.0 + n(ks[13], (DEPTH, D_MODEL), 0.02),
        'ln1_b': n(ks[14], (DEPTH, D_MODEL), 0.02),
        'w1': n(ks[15], (DEPTH, D_MODEL, D_FF), D_MODEL ** -0.5),
        'w2': n(ks[16], (DEPTH, D_FF, D_MODEL), BETA * D_FF ** -0.5),
        'ln2_w': 1.0 + n(ks[17], (DEPTH, D_MODEL), 0.02),
        'ln2_b': n(ks[18], (DEPTH, D_MODEL), 0.02),
    }

def reference(x_prompt, x_sample, state_conv, state_gla, meta, ln_in_w, ln_in_b, w_in, conv_w,
              w_a2, b_a2, gn_w, w_o, ln1_w, ln1_b, w1, w2, ln2_w, ln2_b):
    params = (ln_in_w, ln_in_b, w_in, conv_w, w_a2, b_a2, gn_w, w_o, ln1_w, ln1_b, w1, w2, ln2_w, ln2_b)
    nb = x_prompt.shape[0]
    h = jnp.concatenate([jnp.broadcast_to(meta.astype(x_prompt.dtype), (nb, N_META, D_MODEL)), x_prompt], axis=1)
    conv0 = jnp.zeros((DEPTH, nb, CONV_W - 1, D_CONV), x_prompt.dtype)
    gla0 = jnp.zeros((DEPTH, nb, GLA_HEADS, GLA_DK, GLA_DV), jnp.float32)
    hp, conv_p, gla_p = trunk(h, conv0, gla0, N_META, *params)
    y_prompt = hp[:, N_META:]
    y_sample, conv_s, gla_s = trunk(x_sample, state_conv, state_gla, 0, *params)
    return (y_prompt, y_sample, conv_p, gla_p, conv_s, gla_s)


_drawn_inputs = setup_inputs


def setup_inputs(seed=0):
    import zlib

    import numpy as np

    out = dict(_drawn_inputs(seed))
    spreads = {}
    factors = {'gn_w': 8.0, 'ln1_b': 2.674, 'ln2_w': 2.819, 'ln2_b': 2.841}
    for name, (base, spread) in spreads.items():
        noise = np.random.default_rng([zlib.crc32(name.encode()), seed]).standard_normal(out[name].shape)
        drawn = base * np.exp(spread * noise) if base else spread * noise
        out[name] = __import__('jax').numpy.asarray(drawn.astype(out[name].dtype))
    for name, factor in factors.items():
        out[name] = (out[name] * factor).astype(out[name].dtype)
    return out
```

```python
from contextlib import ExitStack

import concourse.bass as bass
from concourse import mybir

F32 = mybir.dt.float32
F32R = mybir.dt.float32r
BF16 = mybir.dt.bfloat16
ALU = mybir.AluOpType
ACT = mybir.ActivationFunctionType
AX_X = mybir.AxisListType.X

P = 128
D = 2048
KT = D // P
META, SEQ = 16, 256
NSEQ, DSEQ = 8, 4
DEC = NSEQ * DSEQ
PROMPT = META + SEQ
T = PROMPT + DEC
N = T - META
HEADS, DK, DV = 4, 256, 512
DT = DK // P
RANK = 16
FF = 4 * D
CW = 3
EPS = 1e-5
ALPHA = 2.0 ** 0.25
GW = 512
NB = GW // P
UK = 2
UNITS = KT // UK
SLOTS = 4
HG = 8
CHUNK = 128
TT = 96
NTT = N // TT
FB = FF // D
CB, CC, CX, WQ, WK = 0, D, 2 * D, 3 * D, 3 * D + D // 2
WV = 4 * D
WG, WA, WGA, WGB = 5 * D, 6 * D, 6 * D + RANK, 7 * D + RANK
P_INW, P_INB, P_LW, P_LB, P_BA, P_GN, P_CW = 0, 16, 32, 48, 64, 72, 76
P_ALL = P_CW + CW * KT
LEVELS = [1, 2, 4, 8, 16, 32, 64]
USES = [
    ["z0", "lev_a0", "v0", "lev_b0", "o0", "o1", "o0T", "o1T", "tail"],
    ["z1", "lev_a1", "v1", "lev_b1", "s0", "d0", "d1", "d2", "s1", "d3", "d4", "d5", "s2", "d6", "d7", "o2T"],
    ["lev_a2", "v2", "lev_b2", "s0", "d0", "d1", "d2", "s1", "d3", "d4", "d5", "s2", "d6", "d7"],
    ["kT", "vst", "kst", "o2"],
]
BEFORE = [1, 1, 1, 0]
S0_SLOTS = 3
PIECE_SEQS = {5: [0, 1, 2], 6: [3, 4, 5], 7: [6, 7]}


def build(nc, x_prompt, x_sample, state_conv, state_gla, meta, ln_in_w, ln_in_b, w_in, conv_w,
          w_a2, b_a2, gn_w, w_o, ln1_w, ln1_b, w1, w2, ln2_w, ln2_b,
          y_prompt, y_sample, conv_prompt, gla_prompt, conv_sample, gla_sample):
    w_in, w_o, w1, w2 = w_in[0], w_o[0], w1[0], w2[0]
    with ExitStack() as ctx:
        scope = [ctx]

        def sb(name, shape, dt=F32):
            return scope[-1].enter_context(nc.sbuf_tensor(name, shape, dt))

        def sem(name):
            return ctx.enter_context(nc.semaphore(name))

        raw = sb("raw", [P, SLOTS, UK, GW])
        w_hi = sb("w_hi", [P, SLOTS, UK, GW], F32R)
        w_lo = sb("w_lo", [P, SLOTS, UK, GW], F32R)
        x_hi = sb("x_hi", [P, KT, T], F32R)
        x_lo = sb("x_lo", [P, KT, T], F32R)
        mix = sb("mix", [P, KT, N])
        ident = sb("ident", [P, P])
        ones = sb("ones", [P, P])
        params = sb("params", [P, P_ALL])
        stats = sb("stats", [P, NTT, KT // NB, 6])
        mv = sb("mv", [P, NTT, 2])
        rstd = sb("rstd", [P, NTT])
        nbias = sb("nbias", [P, NTT])
        stage = sb("stage", [P, NB, N])
        consts = ExitStack()
        scope.append(consts)
        mask = sb("mask", [P, 8, P], BF16)
        mask2 = sb("mask2", [P, 5, 48], BF16)
        segmask = sb("segmask", [P, NSEQ])
        carry = sb("carry", [P, T], BF16)
        a1T = sb("a1T", [RANK, T])
        stT = sb("stT", [P, KT, NSEQ * 2])
        wa2 = sb("wa2", [RANK, HEADS * DK])
        q_dec = sb("q_dec", [P, DT, NSEQ + 2, 48])

        def phase(alloc):
            with ExitStack() as inner:
                scope.append(inner)
                got = alloc()
                scope.pop()
            return got

        def start_buffers():
            return (sb("xrow", [P, 3, D]), sb("wa1", [P, KT, P]), sb("wa1_hi", [P, KT, P], F32R),
                    sb("wa1_lo", [P, KT, P], F32R), sb("hf", [P, 2, T]), sb("prow", [P, P]), sb("strow", [16, D]),
                    sb("stats_in", [P, 3, 4, 6]), sb("seg0", [P, NSEQ]))

        xrow, wa1, wa1_hi, wa1_lo, hf, prow, strow, stats_in, seg0 = phase(start_buffers)

        def head_buffers():
            return dict(
                lev=sb("lev", [P, 4, DT, T]), eb=sb("eb", [P, DT, T]), kh=sb("kh", [P, DT, T]),
                bT=sb("bT", [P, DT, T]), qh=sb("qh", [P, DT, CHUNK]), prod=sb("prod", [P, 4, CHUNK]),
                ktok=sb("ktok", [P, 2, DT, P]), kst=sb("kst", [P, DT, 96], F32R), vst=sb("vst", [P, NB, 96], F32R),
                V=sb("V", [P, NB, T]), F=sb("F", [P, NB, N]), kt2=sb("kt2", [16, DT, P]),
                kstk=sb("kstk", [96, DT, P]), kms=sb("kms", [96, 2, DT, P], F32R), tmpA=sb("tmpA", [P, CHUNK]),
                wa2h=sb("wa2h", [RANK, DK]),
                onT=sb("onT", [P, NB, N]), QK=sb("QK", [P, NB, T]), A=sb("A", [P, NB, T]), B=sb("B", [P, NB, T]),
                vtok=sb("vtok", [P, 3, DV]), vstk=sb("vstk", [96, DV], F32R), att=sb("att", [P, 3, CHUNK]),
                S=sb("S", [P, DT, DV]), S0=sb("S0", [P, S0_SLOTS, DT, DV]), uD=sb("uD", [P, NB, NSEQ, 6]),
                tails=sb("tails", [P, NB, 18]), ebl=sb("ebl", [P, DT, 11]),
                ss=sb("ss", [P, 3]), rs=sb("rs", [P, 3]))

        hb = phase(head_buffers)
        scope.pop()
        consts.close()
        lev, eb, kh, bT, qh, prod, ktok, kst, vst = (hb[k] for k in "lev eb kh bT qh prod ktok kst vst".split())
        V, Fs, kt2, kstk, kms, tmpA, wa2h, onT, QK = (hb[k] for k in "V F kt2 kstk kms tmpA wa2h onT QK".split())
        A, B, vtok, vstk, att, S, S0, uD = (hb[k] for k in "A B vtok vstk att S S0 uD".split())
        tails, ebl, ss, rs = (hb[k] for k in "tails ebl ss rs".split())
        junk = prod[:, :, :].rearrange("p a b -> p (a b)")
        tailrow = ktok[0:18, :, :, :].rearrange("p a b c -> p (a b c)")

        def tail_buffers():
            return (sb("f_hi", [P, KT, N], F32R), sb("f_lo", [P, KT, N], F32R),
                    sb("pair", [P, 2, NB, N]), sb("diag", [P, 2, NTT, TT]), sb("yrow", [P, NTT, D]),
                    sb("ln_w_row", [P, D]), sb("ln_b_row", [P, D]))

        f_hi, f_lo, pair, diag, yrow, ln_w_row, ln_b_row = phase(tail_buffers)

        bank = [ctx.enter_context(nc.psum_tensor(f"bank{n}", [P, 512], F32)) for n in range(NB)]
        gbank = [ctx.enter_context(nc.psum_tensor(f"gbank{n}", [P, 512], F32)) for n in range(4)]

        raw_landed = [sem(f"raw_landed{s}") for s in range(SLOTS)]
        k_landed = [sem(f"k_landed{s}") for s in range(SLOTS)]
        hi_ready = sem("hi_ready")
        lo_ready = sem("lo_ready")
        units_used = sem("units_used")
        bank_full = sem("bank_full")
        bank_free = [sem(f"bank_free{n}") for n in range(NB)]
        g_full = [sem(f"g_full{n}") for n in range(4)]
        g_free = [sem(f"g_free{n}") for n in range(4)]
        x_landed = [sem(f"x_landed{i}") for i in range(3)]
        prow_landed = sem("prow_landed")
        st_landed = sem("st_landed")
        wa_landed = sem("wa_landed")
        wa1_landed = sem("wa1_landed")
        row_stats = sem("row_stats")
        row_sqrt = sem("row_sqrt")
        row_scale = sem("row_scale")
        row_done = sem("row_done")
        const_ready = sem("const_ready")
        ident_ready = sem("ident_ready")
        hf_ready = sem("hf_ready")
        x_hi_ready = sem("x_hi_ready")
        x_lo_ready = sem("x_lo_ready")
        wa1_split = sem("wa1_split")
        pool_seq = sem("pool_seq")
        pool_head = sem("pool_head")
        pool_step = sem("pool_step")
        dve_step = sem("dve_step")
        act_step = sem("act_step")
        z_ready = sem("z_ready")
        ln_ready = sem("ln_ready")
        b_ready = sem("b_ready")
        dist_ready = sem("dist_ready")
        exp_ready = sem("exp_ready")
        eb_ready = sem("eb_ready")
        kd_ready = sem("kd_ready")
        kdecay_ready = sem("kdecay_ready")
        lev_ready = sem("lev_ready")
        wa2h_ready = sem("wa2h_ready")
        qk_pool = sem("qk_pool")
        ebl_ready = sem("ebl_ready")
        vst_ready = sem("vst_ready")
        kms_ready = sem("kms_ready")
        tails_ready = sem("tails_ready")
        u_ready = sem("u_ready")
        uD_ready = sem("uD_ready")
        conv_done = sem("conv_done")
        cb_used = sem("cb_used")
        ga_used = sem("ga_used")
        silu_ready = sem("silu_ready")
        gated_ready = sem("gated_ready")
        ss_ready = sem("ss_ready")
        ms_ready = sem("ms_ready")
        sq_ready = sem("sq_ready")
        rs_ready = sem("rs_ready")
        att_ready = sem("att_ready")
        sc1_ready = sem("sc1_ready")
        s0_landed = [sem(f"s0_landed{s}") for s in range(S0_SLOTS)]
        s0_stored = [sem(f"s0_stored{s}") for s in range(S0_SLOTS)]
        s0_updated = sem("s0_updated")
        S_final = sem("S_final")
        S_stored = sem("S_stored")
        m_ready = sem("m_ready")
        tail_stored = sem("tail_stored")
        fhi_ready = sem("fhi_ready")
        f_ready = sem("f_ready")
        stage_full = sem("stage_full")
        stage_copied = sem("stage_copied")
        diag_ready = sem("diag_ready")
        norm_ready = sem("norm_ready")
        aff_ready = sem("aff_ready")
        x1hi_ready = sem("x1hi_ready")
        x1_ready = sem("x1_ready")
        acc_ready = sem("acc_ready")
        relu_ready = sem("relu_ready")
        sq2_ready = sem("sq2_ready")
        yrow_copied = sem("yrow_copied")
        lnrow_landed = sem("lnrow_landed")
        yn_ready = sem("yn_ready")
        yw_ready = sem("yw_ready")
        yb_ready = sem("yb_ready")
        out_stored = sem("out_stored")

        waits_alone = sem("waits_alone")

        X_BANKS = KT

        def banks_full(g, n):
            return X_BANKS + NB * g + n + 1

        def bank_frees(g):
            return X_BANKS // NB + g + 1

        def landed(g, i):
            return 16 * (2 * g + 1 + i // SLOTS)

        def g_index(h, k, use):
            return BEFORE[k] + len(USES[k]) * h + USES[k].index(use)

        def g_filled(h, k, use):
            return g_index(h, k, use) + 1

        def g_emptied(h, k, use):
            return g_index(h, k, use) + 1 + (k == 3)

        def g_available(h, k, use):
            return g_index(h, k, use) + (k == 3)

        G_END = [BEFORE[k] + len(USES[k]) * HEADS for k in range(4)]
        WO_G, FF_G = HG * HEADS, HG * HEADS + NB
        LAST_B = FB - 1

        def w1_group(b, j):
            return FF_G + 2 * NB * b + j

        def w2_group(b, j):
            return FF_G + 2 * NB * b + NB + j

        END_G = w2_group(LAST_B, NB - 1)

        def alone(engine):
            engine.sem_inc(waits_alone, 1)

        def split_hi(act, g, i, with_k=None):
            s = i % SLOTS
            act.wait_ge(raw_landed[s], landed(g, i))
            if with_k is not None:
                act.wait_ge(k_landed[s], 16 * (2 * with_k + 1 + i // SLOTS))
            if i >= SLOTS:
                act.wait_ge(units_used, (UNITS - 1) * g + i - SLOTS + 1)
            elif not (isinstance(g, int) and g == 0):
                if i < SLOTS - 1:
                    act.wait_ge(units_used, (UNITS - 1) * (g - 1) + i + SLOTS + 1)
                else:
                    act.wait_ge(bank_full, banks_full(g - 1, NB - 1))
            nc.scalar.activation(w_hi[:, s, :, :], raw[:, s, :, :], ACT.Copy).then_inc(hi_ready, 1)

        def split_lo(dve, g, i):
            s = i % SLOTS
            dve.wait_ge(hi_ready, UNITS * g + i + 1)
            nc.vector.tensor_tensor(w_lo[:, s, :, :], raw[:, s, :, :], w_hi[:, s, :, :].bitcast(F32),
                                    ALU.subtract).then_inc(lo_ready, 1)

        def dense_group(pe, g, a_hi, a_lo, cols, operand=None, between=None):
            for i in range(UNITS):
                s = i % SLOTS
                pe.wait_ge(lo_ready, SLOTS + UNITS * g + i + 1)
                if operand is not None:
                    pe.wait_ge(operand[0], operand[1](i))
                for n in range(NB):
                    if i == 0:
                        pe.wait_ge(bank_free[n], bank_frees(g - 1))
                    c0, c1 = cols[n]
                    out = bank[n][:, 0:c1 - c0]
                    for kk in range(UK):
                        kt = UK * i + kk
                        wh, wl = w_hi[:, s, kk, n * P:(n + 1) * P], w_lo[:, s, kk, n * P:(n + 1) * P]
                        nc.tensor.matmul(out, wh, a_hi[:, kt, c0:c1], start=(kt == 0), stop=False)
                        nc.tensor.matmul(out, wh, a_lo[:, kt, c0:c1], start=False, stop=False)
                        last = nc.tensor.matmul(out, wl, a_hi[:, kt, c0:c1], start=False, stop=(kt == KT - 1))
                    if i == UNITS - 1:
                        last.then_inc(bank_full, 1)
                if i < UNITS - 1:
                    last.then_inc(units_used, 1)
                if i == SLOTS - 1 and between is not None:
                    between()

        ALL, OUT, MIX = [(0, T)] * NB, [(META, T)] * NB, [(0, N)] * NB
        GROUP_COLS = [ALL, ALL, ALL, ALL, OUT, OUT, OUT, OUT]

        def transpose(out, in_, rows):
            return nc.tensor.transpose(out, in_, ident[0:rows, 0:rows])

        def row_transposes(pe, first, done=None):
            pe.wait_ge(stage_full, done)
            for t in range(NTT):
                pe.wait_ge(g_free[t], first(t))
                for n in range(NB):
                    last = transpose(gbank[t][0:TT, n * P:(n + 1) * P], stage[:, n, t * TT:(t + 1) * TT], P)
                last.then_inc(g_full[t], 1)

        block = ctx.enter_context(nc.Block())

        @block.sync
        def _(sp):
            sp.dma_start(xrow[0:META, 0, :], meta).then_inc(x_landed[0], 16)
            sp.dma_start(xrow[META:P, 0, :], x_prompt[0, 0:P - META, :]).then_inc(x_landed[0], 16)
            sp.dma_start(xrow[:, 1, :], x_prompt[0, P - META:2 * P - META, :]).then_inc(x_landed[1], 16)
            sp.dma_start(xrow[0:META, 2, :], x_prompt[0, 2 * P - META:SEQ, :]).then_inc(x_landed[2], 16)
            sp.dma_start(xrow[META:META + DEC, 2, :], x_sample.rearrange("a b d -> (a b) d")).then_inc(x_landed[2], 16)
            sp.dma_start(wa1[:, :, :], w_in[:, WA:WA + P].rearrange("(k p) c -> p k c", p=P)).then_inc(wa1_landed, 16)

            def load_unit(u, slot, src):
                sp.wait_ge(lo_ready, u + 1)
                alone(sp)
                sp.dma_start(raw[:, slot, :, :], src.rearrange("(k p) c -> p k c", p=P))\
                    .then_inc(raw_landed[slot], 16)

            def load_group(g, w, row0, col):
                for i in range(UNITS):
                    load_unit(UNITS * g + i, i % SLOTS, w[bass.ds(row0 + i * UK * P, UK * P), bass.ds(col, GW)])

            with sp.Fori(0, HEADS) as h:
                for j, first in enumerate([CC, None, WV, CX, CB, WGA, WG, WGB]):
                    if first is not None:
                        load_group(HG * h + j, w_in, 0, first + h * GW)
                        continue
                    for i in range(UNITS):
                        s, rows = i % SLOTS, slice(i * UK * P, (i + 1) * UK * P)
                        sp.wait_ge(lo_ready, UNITS * (HG * h + j) + i + 1)
                        sp.dma_start(raw[:, s, :, 0:DK], w_in[rows, bass.ds(WQ + h * DK, DK)]
                                     .rearrange("(k p) c -> p k c", p=P)).then_inc(raw_landed[s], 16)
                        sp.dma_start(raw[:, s, :, DK:GW], w_in[rows, bass.ds(WK + h * DK, DK)]
                                     .rearrange("(k p) c -> p k c", p=P)).then_inc(k_landed[s], 16)
            with sp.Fori(0, NB) as j:
                load_group(WO_G + j, w_o, 0, j * GW)
            with sp.Fori(0, FB) as b:
                with sp.Fori(0, NB) as j:
                    load_group(w1_group(b, j), w1, 0, b * D + j * GW)
                with sp.Fori(0, NB) as j:
                    load_group(w2_group(b, j), w2, b * D, j * GW)
            for t in range(NTT):
                for half in range(2):
                    c = slice(half * D // 2, (half + 1) * D // 2)
                    sp.wait_ge(yb_ready, 2 * t + half + 1)
                    a, e = t * TT, (t + 1) * TT
                    n_prompt = min(e, SEQ) - a
                    sp.dma_start(y_prompt[0, a:a + n_prompt, c], yrow[0:n_prompt, t, c]).then_inc(out_stored, 16)
                    if n_prompt < TT:
                        sp.dma_start(y_sample.rearrange("a b d -> (a b) d")[:, c],
                                     yrow[n_prompt:TT, t, c]).then_inc(out_stored, 16)
            sp.wait_ge(out_stored, 16 * 2 * (NTT + 1))
            for s in range(S0_SLOTS):
                sp.wait_ge(s0_stored[s], 1 + 16 * HEADS * len(range(s, NSEQ, S0_SLOTS)))
            sp.wait_ge(S_stored, 1 + 16 * HEADS)
            sp.wait_ge(tail_stored, 1 + 32 * HEADS)

        @block.tensor
        def _(pe):
            pe.wait_ge(ident_ready, 1)
            pe.wait_ge(prow_landed, 16 * 7)
            transpose(gbank[0][:, 0:P_ALL], prow[0:P_ALL, :], P_ALL).then_inc(g_full[0], 1)
            pe.wait_ge(st_landed, 16)
            for k in range(KT):
                last = transpose(gbank[1][:, 16 * k:16 * k + 16], strow[:, k * P:(k + 1) * P], 16)
            last.then_inc(g_full[1], 1)
            for k in range(KT):
                n = k % NB
                if k >= NB:
                    pe.wait_ge(bank_free[n], k // NB)
                for i, rows in enumerate([P, P, T - 2 * P]):
                    if k == 0:
                        pe.wait_ge(row_done, i + 1)
                    last = transpose(bank[n][:, i * P:i * P + rows], xrow[0:rows, i, k * P:(k + 1) * P], rows)
                last.then_inc(bank_full, 1)
            pe.wait_ge(wa1_split, 2)
            for k in range(KT):
                pe.wait_ge(x_lo_ready, k + 1)
                out = gbank[2][:, 0:T]
                nc.tensor.matmul(out, wa1_hi[:, k, :], x_hi[:, k, :], start=(k == 0), stop=False)
                nc.tensor.matmul(out, wa1_hi[:, k, :], x_lo[:, k, :], start=False, stop=False)
                last = nc.tensor.matmul(out, wa1_lo[:, k, :], x_hi[:, k, :], start=False, stop=(k == KT - 1))
            last.then_inc(g_full[2], 1)

            def level(h, k, c, c0, w, entries, use):
                pe.wait_ge(g_free[k], g_available(h, k, use))
                for m, buf in enumerate(entries):
                    out = gbank[k][0:w, m * w:(m + 1) * w]
                    for d in range(DT):
                        ks = QK[:, DT + d, c0:c0 + w] if buf is None else lev[:, buf, d, c0:c0 + w]
                        qs = QK[:, d, c0:c0 + w] if buf is None else ks
                        last = nc.tensor.matmul(out, ks, qs, start=(d == 0), stop=(d == DT - 1))
                return last

            def state_update(h, use, keys, vals):
                for d in range(DT):
                    pe.wait_ge(g_free[1 + d], g_available(h, 1 + d, use))
                    nc.tensor.matmul(gbank[1 + d][:, :], keys[:, d, :], vals, start=True, stop=True)\
                        .then_inc(g_full[1 + d], 1)

            def seq_read(h, i, first=False):
                s = i % S0_SLOTS
                pe.wait_ge(s0_landed[s], 16 * (len(range(s, NSEQ, S0_SLOTS)) * h + i // S0_SLOTS + 1))
                for d in range(DT):
                    nc.tensor.matmul(gbank[3][0:48, :], q_dec[:, d, 1 + i, :], S0[:, s, d, :],
                                     start=(first and d == 0), stop=False)

            def seq_write(h, i):
                pe.wait_ge(kms_ready, NSEQ * h + i + 1)
                state_update(h, f"d{i}", kms[:, i % 2, :, :], vstk[:, :])

            with pe.Fori(0, HEADS) as h:
                for j in range(HG):
                    dense_group(pe, HG * h + j, x_hi, x_lo, GROUP_COLS[j])
                    if j == 0:
                        pe.wait_ge(wa2h_ready, h + 1)
                        for d in range(DT):
                            pe.wait_ge(g_free[d], g_available(h, d, f"z{d}"))
                            nc.tensor.matmul(gbank[d][:, 0:T], wa2h[:, d * P:(d + 1) * P], a1T[:, :],
                                             start=True, stop=True).then_inc(g_full[d], 1)
                    if j == 2:
                        pe.wait_ge(lev_ready, 7 * h + 3)
                        for c in range(2):
                            level(h, c, c, c * CHUNK, CHUNK, [None, 0, 1, 2], f"lev_a{c}").then_inc(g_full[c], 1)
                        level(h, 2, 2, 2 * CHUNK, 48, [None, 0, 1, 2], "lev_a2").then_inc(g_full[2], 1)
                        pe.wait_ge(qk_pool, 5 * h + 4)
                        pe.wait_ge(g_free[3], g_available(h, 3, "kT"))
                        for c in range(2):
                            for d in range(DT):
                                m = c * DT + d
                                last = transpose(gbank[3][:, m * P:(m + 1) * P],
                                                 kh[:, d, c * CHUNK:(c + 1) * CHUNK], P)
                        last.then_inc(g_full[3], 1)
                    if j == 3:
                        for c, w in enumerate([CHUNK, CHUNK, 48]):
                            pe.wait_ge(g_free[c], g_available(h, c, f"v{c}"))
                            alone(pe)
                            for n in range(NB):
                                last = transpose(gbank[c][0:w, n * P:(n + 1) * P], V[:, n, c * CHUNK:c * CHUNK + w], P)
                            last.then_inc(g_full[c], 1)
                        pe.wait_ge(vst_ready, 3 * h + 3)
                        pe.wait_ge(g_free[3], g_available(h, 3, "vst"))
                        for n in range(NB):
                            last = transpose(gbank[3][0:96, n * P:(n + 1) * P], vst[:, n, :].bitcast(F32), P)
                        last.then_inc(g_full[3], 1)
                    if j == 4:
                        pe.wait_ge(lev_ready, 7 * h + 7)
                        for c in range(2):
                            level(h, c, c, c * CHUNK, CHUNK, [3, 0, 1, 2], f"lev_b{c}").then_inc(g_full[c], 1)
                        level(h, 2, 2, 2 * CHUNK, 48, [3], "lev_b2")
                        for d in range(DT):
                            last = transpose(gbank[2][0:16, P + d * P:P + (d + 1) * P],
                                             kh[:, d, 2 * CHUNK:PROMPT], P)
                        last.then_inc(g_full[2], 1)
                        pe.wait_ge(qk_pool, 5 * h + 5)
                        pe.wait_ge(g_free[3], g_available(h, 3, "kst"))
                        for d in range(DT):
                            last = transpose(gbank[3][0:96, d * P:(d + 1) * P], kst[:, d, :].bitcast(F32), P)
                        last.then_inc(g_full[3], 1)
                    if j == 5:
                        pe.wait_ge(att_ready, 3 * h + 3)
                        pe.wait_ge(g_free[0], g_available(h, 0, "o0"))
                        nc.tensor.matmul(gbank[0][:, :], att[:, 0, :], vtok[:, 0, :], start=True, stop=True)\
                            .then_inc(g_full[0], 1)
                        state_update(h, "s0", ktok[:, 0, :, :], vtok[:, 0, :])
                        pe.wait_ge(g_free[3], g_available(h, 3, "o2"))
                    if j == 6:
                        pe.wait_ge(g_free[0], g_available(h, 0, "o1"))
                        nc.tensor.matmul(gbank[0][:, :], att[:, 1, :], vtok[:, 1, :], start=True, stop=False)
                        for d in range(DT):
                            last = nc.tensor.matmul(gbank[0][:, :], qh[:, d, :], S[:, d, :], start=False,
                                                    stop=(d == DT - 1))
                        last.then_inc(g_full[0], 1)
                        state_update(h, "s1", ktok[:, 1, :, :], vtok[:, 1, :])
                    if j == 7:
                        pe.wait_ge(g_free[0], g_available(h, 0, "o0T"))
                        for n in range(NB):
                            last = transpose(gbank[0][:, n * P:(n + 1) * P], vtok[:, 0, n * P:(n + 1) * P], P)
                        last.then_inc(g_full[0], 1)
                        for i in PIECE_SEQS[7]:
                            seq_read(h, i)
                        for d in range(DT):
                            nc.tensor.matmul(gbank[3][0:48, :], q_dec[:, d, 0, :], S[:, d, :], start=False, stop=False)
                        nc.tensor.matmul(gbank[3][0:48, :], att[0:48, 2, 0:48], vtok[0:48, 2, :],
                                         start=False, stop=True).then_inc(g_full[3], 1)
                        state_update(h, "s2", kt2, vtok[0:16, 2, :])
                        pe.wait_ge(g_free[0], g_available(h, 0, "o1T"))
                        for n in range(NB):
                            last = transpose(gbank[0][:, n * P:(n + 1) * P], vtok[:, 1, n * P:(n + 1) * P], P)
                        last.then_inc(g_full[0], 1)
                        for i in PIECE_SEQS[7]:
                            seq_write(h, i)
                        pe.wait_ge(tails_ready, h + 1)
                        pe.wait_ge(g_free[0], g_available(h, 0, "tail"))
                        for n in range(NB):
                            last = transpose(gbank[0][0:18, n * P:(n + 1) * P], tails[:, n, :], P)
                        last.then_inc(g_full[0], 1)
                        pe.wait_ge(g_free[1], g_available(h, 1, "o2T"))
                        pe.wait_ge(g_free[3], g_emptied(h, 3, "o2"))
                        alone(pe)
                        for n in range(NB):
                            last = transpose(gbank[1][:, n * 48:(n + 1) * 48], vtok[0:48, 2, n * P:(n + 1) * P], 48)
                        last.then_inc(g_full[1], 1)
                    elif j >= 5:
                        for i in PIECE_SEQS[j]:
                            seq_read(h, i, first=(i == 0))
                            seq_write(h, i)

            mix_part = (f_ready, lambda i: i // 2 + 1)
            dense_group(pe, WO_G, f_hi, f_lo, MIX, mix_part)
            with pe.Fori(1, NB) as j:
                dense_group(pe, WO_G + j, f_hi, f_lo, MIX, mix_part,
                            between=lambda: row_transposes(pe, lambda t: G_END[t] + j - 1, j))
            row_transposes(pe, lambda t: G_END[t] + NB - 1, NB)
            for m, k in enumerate([3, 0]):
                pe.wait_ge(diag_ready, m + 1)
                pe.wait_ge(g_free[k], G_END[3] + 1 if k == 3 else G_END[0] + NB)
                for t in range(NTT):
                    last = nc.tensor.matmul(gbank[k][:, t * TT:(t + 1) * TT], ones[0:TT, :], diag[0:TT, m, t, :],
                                            start=True, stop=True)
                last.then_inc(g_full[k], 1)

            def up(b):
                with pe.Fori(0, NB) as j:
                    dense_group(pe, w1_group(b, j), x_hi, x_lo, OUT, (x1_ready, lambda i: i // 2 + 1))

            def down_part(b):
                return (f_ready, lambda i: HEADS + NB * b + i // 2 + 1)

            with pe.Fori(0, LAST_B) as b:
                up(b)
                with pe.Fori(0, NB) as j:
                    dense_group(pe, w2_group(b, j), f_hi, f_lo, MIX, down_part(b))
            up(LAST_B)
            dense_group(pe, w2_group(LAST_B, 0), f_hi, f_lo, MIX, down_part(LAST_B))
            used = [NB + 1, NB, NB]
            with pe.Fori(1, NB) as j:
                dense_group(pe, w2_group(LAST_B, j), f_hi, f_lo, MIX, down_part(LAST_B),
                            between=lambda: row_transposes(pe, lambda t: G_END[t] + used[t] + j - 1, NB + j))
            row_transposes(pe, lambda t: G_END[t] + used[t] + NB - 1, 2 * NB)

        @block.scalar
        def _(act):
            act.dma_start(wa2[:, :], w_a2[0]).then_inc(wa_landed, 16)
            act.dma_start(strow[:, :], state_conv[0].rearrange("a b d -> (a b) d")).then_inc(st_landed, 16)
            for i in range(SLOTS):
                split_hi(act, 0, i)
            act.wait_ge(wa1_landed, 16)
            nc.scalar.activation(wa1_hi[:, :, :], wa1[:, :, :], ACT.Copy).then_inc(wa1_split, 1)
            for i, rows in enumerate([P, P, T - 2 * P]):
                act.wait_ge(row_stats, i + 1)
                nc.scalar.activation(rstd[0:rows, i:i + 1], rstd[0:rows, i:i + 1], ACT.Sqrt).then_inc(row_sqrt, 1)
                act.wait_ge(row_scale, i + 1)
                nc.scalar.activation(xrow[0:rows, i, :], xrow[0:rows, i, :], ACT.Identity,
                                     bias=nbias[0:rows, i:i + 1], scale=rstd[0:rows, i:i + 1]).then_inc(row_done, 1)
            act.wait_ge(g_full[0], 1)
            nc.scalar.activation(params[:, :], gbank[0][:, 0:P_ALL], ACT.Copy).then_inc(g_free[0], 1)
            act.wait_ge(g_full[1], 1)
            nc.scalar.activation(stT[:, :, :], gbank[1][:, 0:16 * KT], ACT.Copy).then_inc(g_free[1], 1)
            act.wait_ge(g_free[0], 1)
            for k in range(KT):
                act.wait_ge(bank_full, k + 1)
                if k >= 2:
                    act.wait_ge(x_lo_ready, k - 1)
                nc.scalar.activation(hf[:, k % 2, :], bank[k % NB][:, 0:T], ACT.Identity,
                                     bias=params[:, P_INB + k:P_INB + k + 1],
                                     scale=params[:, P_INW + k:P_INW + k + 1]).then_inc(bank_free[k % NB], 1)
            act.wait_ge(g_full[2], 1)
            nc.scalar.activation(a1T[:, :], gbank[2][0:RANK, 0:T], ACT.Copy).then_inc(g_free[2], 1)

            def evacuate(g, dst, func, w, scale=1.0):
                for n in range(NB):
                    act.wait_ge(bank_full, banks_full(g, n))
                    nc.scalar.activation(dst(n), bank[n][:, 0:w], func,
                                         scale=(scale if n < DT else 1.0)).then_inc(bank_free[n], 1)

            def normalise(h, c, k, use, rows):
                act.wait_ge(g_full[k], g_filled(h, k, use))
                nc.scalar.activation(junk[0:rows, :], gbank[k][0:rows, :], ACT.Square,
                                     accum_out=ss[0:rows, c:c + 1]).then_inc(ss_ready, 1)
                act.wait_ge(ms_ready, 3 * h + c + 1)
                nc.scalar.activation(rs[0:rows, c:c + 1], rs[0:rows, c:c + 1], ACT.Sqrt).then_inc(sq_ready, 1)
                act.wait_ge(rs_ready, 3 * h + c + 1)
                act.wait_ge(g_full[2], g_filled(h, 2, f"s{c}"))
                nc.scalar.activation(vtok[0:rows, c, :], gbank[k][0:rows, :], ACT.Copy,
                                     scale=rs[0:rows, c:c + 1]).then_inc(g_free[k], 1)

            def rows_back(h, k, use, w, skip, at):
                act.wait_ge(g_full[k], g_filled(h, k, use))
                for n in range(NB):
                    last = nc.scalar.activation(onT[:, n, at:at + w - skip], gbank[k][:, n * w + skip:(n + 1) * w],
                                                ACT.Copy, scale=params[:, P_GN + n:P_GN + n + 1])
                last.then_inc(g_free[k], 1)

            def store_state(h, i):
                s = i % S0_SLOTS
                act.wait_ge(g_free[2], g_emptied(h, 2, f"d{i}"))
                act.dma_start(gla_sample[0, i, bass.ds(h, 1), :, :].rearrange("o (d p) v -> p (o d) v", p=P),
                              S0[:, s, :, :]).then_inc(s0_stored[s], 16)

            with act.Fori(0, HEADS) as h:
                for j in range(HG):
                    g = HG * h + j
                    for i in range(SLOTS, UNITS):
                        split_hi(act, g, i, with_k=(h if j == 1 else None))
                        if j == 1 and i < 6:
                            for m in range(2):
                                lv = 2 * (i - SLOTS) + m
                                act.wait_ge(dist_ready, 7 * h + lv + 1)
                                nc.scalar.activation(lev[:, lv, :, :], lev[:, lv, :, :], ACT.Exp,
                                                     scale=1.0 / 16).then_inc(exp_ready, 1)
                        if j == 1 and i == 6:
                            nc.scalar.activation(eb[:, :, :], bT[:, :, :], ACT.Exp, scale=1.0 / 16).then_inc(eb_ready, 1)
                            act.wait_ge(kd_ready, h + 1)
                            nc.scalar.activation(kh[:, :, :], kh[:, :, :], ACT.Exp, scale=1.0 / 16)\
                                .then_inc(kdecay_ready, 1)
                        if j == 3 and i < 7:
                            lv = i - SLOTS
                            act.wait_ge(dist_ready, 7 * h + 4 + lv + 1)
                            nc.scalar.activation(lev[:, lv, :, 0:2 * CHUNK], lev[:, lv, :, 0:2 * CHUNK], ACT.Exp,
                                                 scale=1.0 / 16).then_inc(exp_ready, 1)
                    for i in range(SLOTS - 1):
                        split_hi(act, g + 1, i, with_k=(h if j == 0 else None))
                    if j == 0:
                        evacuate(g, lambda n: A[:, n, :], ACT.Copy, T)
                    if j == 1:
                        evacuate(g, lambda n: QK[:, n, :], ACT.Copy, T, scale=float(DK) ** -0.5)
                    if j == 2:
                        evacuate(g, lambda n: V[:, n, :], ACT.Copy, T)
                    if j == 3:
                        evacuate(g, lambda n: B[:, n, :], ACT.Copy, T)
                    if j == 4:
                        act.wait_ge(vst_ready, 3 * h + 3)
                        evacuate(g, lambda n: V[:, n, 0:N], ACT.Copy, N)
                    if j == 5:
                        act.wait_ge(conv_done, h + 1)
                        act.wait_ge(tails_ready, h + 1)
                        evacuate(g, lambda n: A[:, n, 0:N], ACT.Sigmoid, N)
                    if j == 6:
                        for n in range(NB):
                            act.wait_ge(bank_full, banks_full(g, n))
                            nc.scalar.activation(Fs[:, n, :], bank[n][:, 0:N], ACT.Sigmoid)
                            nc.scalar.activation(QK[:, n, 0:N], bank[n][:, 0:N], ACT.Copy).then_inc(bank_free[n], 1)
                    if j == 7:
                        act.wait_ge(ga_used, h + 1)
                        evacuate(g, lambda n: A[:, n, 0:N], ACT.Sigmoid, N)
                    split_hi(act, g + 1, SLOTS - 1, with_k=(h if j == 0 else None))
                    if j == 0:
                        for d in range(DT):
                            act.wait_ge(g_full[d], g_filled(h, d, f"z{d}"))
                            nc.scalar.activation(lev[:, 2, d, :], gbank[d][:, 0:T], ACT.Identity,
                                                 bias=params[:, bass.ds(P_BA + DT * h + d, 1)]).then_inc(g_free[d], 1)
                        act.wait_ge(g_free[1], g_emptied(h, 1, "z1"))
                        nc.scalar.activation(lev[:, 3, :, :], lev[:, 2, :, :], ACT.Abs).then_inc(act_step, 1)
                        act.wait_ge(act_step, 3 * h + 1)
                        nc.scalar.activation(lev[:, 3, :, :], lev[:, 3, :, :], ACT.Exp, scale=-1.0).then_inc(act_step, 1)
                        act.wait_ge(act_step, 3 * h + 2)
                        nc.scalar.activation(lev[:, 3, :, :], lev[:, 3, :, :], ACT.Ln, bias=ones[:, 0:1])\
                            .then_inc(act_step, 1)
                    if j == 2:
                        act.wait_ge(tail_stored, 32 * h + 1)
                        act.wait_ge(g_full[3], g_filled(h, 3, "kT"))
                        nc.scalar.activation(ktok[:, :, :, :], gbank[3][:, :], ACT.Copy).then_inc(g_free[3], 1)
                    if j == 3:
                        for c, w in enumerate([CHUNK, CHUNK, 48]):
                            act.wait_ge(g_full[c], g_filled(h, c, f"v{c}"))
                            nc.scalar.activation(vtok[0:w, c, :], gbank[c][0:w, :], ACT.Copy).then_inc(g_free[c], 1)
                        act.wait_ge(g_full[3], g_filled(h, 3, "vst"))
                        nc.scalar.activation(vstk[:, :], gbank[3][0:96, :], ACT.Copy).then_inc(g_free[3], 1)
                    if j == 4:
                        act.wait_ge(g_full[3], g_filled(h, 3, "kst"))
                        nc.scalar.activation(kstk[:, :, :], gbank[3][0:96, 0:DK], ACT.Copy).then_inc(g_free[3], 1)
                    if j in (5, 6):
                        normalise(h, j - 5, 0, f"o{j - 5}", CHUNK)
                        for i in PIECE_SEQS[j]:
                            store_state(h, i)
                    if j == 7:
                        rows_back(h, 0, "o0T", CHUNK, META, 0)
                        normalise(h, 2, 3, "o2", 48)
                        rows_back(h, 0, "o1T", CHUNK, 0, CHUNK - META)
                        act.wait_ge(g_full[0], g_filled(h, 0, "tail"))
                        nc.scalar.activation(tailrow, gbank[0][0:18, :], ACT.Copy).then_inc(g_free[0], 1)
                        rows_back(h, 1, "o2T", 48, 0, 2 * CHUNK - META)
                        act.wait_ge(gated_ready, h + 1)
                        for i in PIECE_SEQS[j]:
                            store_state(h, i)
                        act.dma_start(gla_prompt[0, 0, bass.ds(h, 1), :, :].rearrange("o (d p) v -> p (o d) v", p=P),
                                      S[:, :, :]).then_inc(S_stored, 16)
                        act.wait_ge(g_free[0], g_emptied(h, 0, "tail"))
                        act.dma_start(conv_prompt[0, 0, :, bass.ds(h * GW, GW)], tailrow[0:2]).then_inc(tail_stored, 16)
                        act.dma_start(conv_sample[0].rearrange("i c d -> (i c) d")[:, bass.ds(h * GW, GW)],
                                      tailrow[2:18]).then_inc(tail_stored, 16)

            def group_splits(g, has_next=True):
                for i in range(SLOTS, UNITS):
                    split_hi(act, g, i)
                if has_next:
                    for i in range(SLOTS - 1):
                        split_hi(act, g + 1, i)

            for k in range(HEADS):
                act.wait_ge(m_ready, HEADS)
                nc.scalar.activation(f_hi[:, NB * k:NB * (k + 1), :], mix[:, NB * k:NB * (k + 1), :], ACT.Copy)\
                    .then_inc(fhi_ready, 1)
            with act.Fori(0, NB) as j:
                group_splits(WO_G + j)
                split_hi(act, WO_G + j + 1, SLOTS - 1)
            act.wait_ge(row_stats, 4)
            nc.scalar.activation(rstd[0:TT, :], rstd[0:TT, :], ACT.Sqrt).then_inc(row_sqrt, 1)
            for k in range(NB):
                p = pair[:, k % 2, :, :]
                act.wait_ge(norm_ready, k + 1)
                for n in range(NB):
                    f = NB * k + n
                    last = nc.scalar.activation(p[:, n, :], p[:, n, :], ACT.Identity,
                                                bias=params[:, P_LB + f:P_LB + f + 1],
                                                scale=params[:, P_LW + f:P_LW + f + 1])
                last.then_inc(aff_ready, 1)
                act.wait_ge(aff_ready, k + 1)
                nc.scalar.activation(x_hi[:, NB * k:NB * (k + 1), META:T], p, ACT.Copy).then_inc(x1hi_ready, 1)

            def relu_group(g):
                for n in range(NB):
                    act.wait_ge(bank_full, banks_full(g, n))
                    nc.scalar.activation(pair[:, 0, n, :], bank[n][:, 0:N], ACT.Relu).then_inc(bank_free[n], 1)

            def up(b):
                with act.Fori(0, NB) as j:
                    g = w1_group(b, j)
                    group_splits(g)
                    act.wait_ge(sq2_ready, NB * b + j + 1)
                    relu_group(g)
                    split_hi(act, g + 1, SLOTS - 1)

            with act.Fori(0, LAST_B) as b:
                up(b)
                with act.Fori(0, NB) as j:
                    group_splits(w2_group(b, j))
                    split_hi(act, w2_group(b, j) + 1, SLOTS - 1)
            up(LAST_B)

            def rows_out(first, m):
                for t in range(NTT):
                    act.wait_ge(g_full[t], first(t))
                    nc.scalar.activation(yrow[0:TT, t, bass.ds(m * GW, GW)], gbank[t][0:TT, :], ACT.Copy)\
                        .then_inc(yrow_copied, 1)

            used = [NB + 1, NB, NB]
            full0 = [G_END[t] + used[t] for t in range(NTT)]
            group_splits(w2_group(LAST_B, 0))
            split_hi(act, w2_group(LAST_B, 1), SLOTS - 1)
            with act.Fori(1, NB - 1) as j:
                g = w2_group(LAST_B, j)
                for i in range(SLOTS, UNITS):
                    split_hi(act, g, i)
                rows_out(lambda t: full0[t] + j, j - 1)
                for i in range(SLOTS):
                    split_hi(act, g + 1, i)
            for i in range(SLOTS, UNITS):
                split_hi(act, END_G, i)
            rows_out(lambda t: full0[t] + NB - 1, NB - 2)
            rows_out(lambda t: full0[t] + NB, NB - 1)
            act.wait_ge(row_stats, 5)
            nc.scalar.activation(rstd[0:TT, :], rstd[0:TT, :], ACT.Sqrt).then_inc(row_sqrt, 1)
            act.wait_ge(row_scale, 4)
            for t in range(NTT):
                for half in range(2):
                    c = slice(half * D // 2, (half + 1) * D // 2)
                    nc.scalar.activation(yrow[0:TT, t, c], yrow[0:TT, t, c], ACT.Identity,
                                         bias=nbias[0:TT, t:t + 1], scale=rstd[0:TT, t:t + 1]).then_inc(yn_ready, 1)

        @block.vector
        def _(dve):
            dve.sem_inc(lo_ready, SLOTS)
            nc.vector.memset(carry[:, :], 1.0).then_inc(dve_step, 1)
            dve.wait_ge(dve_step, 1)
            for c in (0, CHUNK, 2 * CHUNK):
                nc.vector.memset(carry[:, c:c + 1], 0.0)
            nc.vector.memset(carry[:, PROMPT:T:DSEQ], 0.0)
            nc.vector.memset(q_dec[:, :, :, :], 0.0).then_inc(const_ready, 1)

            for i, rows in enumerate([P, P, T - 2 * P]):
                dve.wait_ge(x_landed[i], 16 if i == 1 else 32)
                for q in range(4):
                    last = nc.vector.bn_stats(stats_in[0:rows, i, q, :], xrow[0:rows, i, q * 512:(q + 1) * 512])
                last.then_inc(dve_step, 1)
                dve.wait_ge(dve_step, 3 * i + 2)
                nc.vector.bn_aggr(mv[0:rows, i, :], stats_in[0:rows, i, :, :].rearrange("p q s -> p (q s)"))\
                    .then_inc(dve_step, 1)
                dve.wait_ge(dve_step, 3 * i + 3)
                nc.vector.tensor_scalar(rstd[0:rows, i:i + 1], mv[0:rows, i, 1:2], EPS, None, ALU.add)\
                    .then_inc(row_stats, 1)
                dve.wait_ge(row_sqrt, i + 1)
                nc.vector.reciprocal(rstd[0:rows, i:i + 1], rstd[0:rows, i:i + 1]).then_inc(dve_step, 1)
                dve.wait_ge(dve_step, 3 * i + 4)
                nc.vector.scalar_tensor_tensor(out=nbias[0:rows, i:i + 1], in0=mv[0:rows, i, 0:1], scalar=-1.0,
                                               in1=rstd[0:rows, i:i + 1], op0=ALU.mult, op1=ALU.mult)\
                    .then_inc(row_scale, 1)
            for i in range(SLOTS):
                split_lo(dve, 0, i)
            dve.wait_ge(wa1_split, 1)
            nc.vector.tensor_tensor(wa1_lo[:, :, :], wa1[:, :, :], wa1_hi[:, :, :].bitcast(F32), ALU.subtract)\
                .then_inc(wa1_split, 1)
            dve.wait_ge(pool_step, 1)
            for q in range(3):
                nc.vector.tensor_copy(segmask[32 * q:32 * q + 32, :], seg0[0:32, :])
            for k in range(KT):
                dve.wait_ge(bank_free[k % NB], k // NB + 1)
                nc.vector.tensor_copy(x_hi[:, k, :], hf[:, k % 2, :]).then_inc(x_hi_ready, 1)
            dve.wait_ge(g_free[2], 1)
            dve.sem_inc(g_free[3], 1)

            def halves(ap, lo, hi, L):
                return ap[:, :, lo:hi].rearrange("p d (b l) -> p d b l", l=2 * L)

            def distance(h, lv, L, hi):
                out, b = halves(lev[:, lv % 4, :, :], 0, hi, L), halves(bT, 0, hi, L)
                nb = hi // (2 * L)
                ref = b[:, :, :, L - 1:L].to_broadcast([P, DT, nb, 2 * L])
                nc.vector.tensor_tensor(out, b, ref, ALU.subtract).then_inc(dve_step, 1)

            def negative(lv, hi):
                x = lev[:, lv, :, 0:hi]
                return nc.vector.scalar_tensor_tensor(out=x, in0=x, scalar=-1.0, in1=x, op0=ALU.mult, op1=ALU.min)

            def levels_evac(h, k, use, w, n, msk, first):
                if not first or k > 0:
                    dve.wait_ge(sc1_ready, 5 * h + k + (0 if first else 3))
                dve.wait_ge(g_full[k], g_filled(h, k, use))
                pr = prod[0:w, :, :].rearrange("p a b -> p (a b)")[:, 0:n * w].rearrange("p (a b) -> p a b", b=w)
                nc.vector.tensor_tensor(pr, gbank[k][0:w, 0:n * w].rearrange("p (a b) -> p a b", b=w), msk, ALU.mult)\
                    .then_inc(g_free[k], 1)
                c = k
                dst = att[0:w, c, 0:w] if first else tmpA[0:w, 0:w]
                dve.wait_ge(g_free[k], g_emptied(h, k, use))
                nc.vector.tensor_reduce(out=dst, in_=pr.rearrange("p a b -> p b a"), axis=AX_X, op=ALU.add)\
                    .then_inc(sc1_ready, 1)
                if not first:
                    dve.wait_ge(sc1_ready, 5 * h + 3 + c + 1)
                    nc.vector.tensor_tensor(att[0:w, c, 0:w], att[0:w, c, 0:w], tmpA[0:w, 0:w], ALU.add)\
                        .then_inc(att_ready, 1)

            def rms(h, c, rows):
                dve.wait_ge(ss_ready, 3 * h + c + 1)
                nc.vector.tensor_scalar(rs[0:rows, c:c + 1], ss[0:rows, c:c + 1], 1.0 / DV, EPS, ALU.mult, ALU.add)\
                    .then_inc(ms_ready, 1)
                dve.wait_ge(sq_ready, 3 * h + c + 1)
                nc.vector.reciprocal(rs[0:rows, c:c + 1], rs[0:rows, c:c + 1]).then_inc(rs_ready, 1)

            def seq_state(h, i):
                s = i % S0_SLOTS
                for d in range(DT):
                    dve.wait_ge(g_full[1 + d], g_filled(h, 1 + d, f"d{i}"))
                    nc.vector.scalar_tensor_tensor(out=S0[:, s, d, :], in0=S0[:, s, d, :],
                                                   scalar=ebl[:, d, 3 + i:4 + i], in1=gbank[1 + d][:, :],
                                                   op0=ALU.mult, op1=ALU.add).then_inc(g_free[1 + d], 1)

            def prompt_state(h, c):
                for d in range(DT):
                    dve.wait_ge(g_full[1 + d], g_filled(h, 1 + d, f"s{c}"))
                    if c == 0:
                        if d == 0:
                            dve.wait_ge(S_stored, 16 * h + 1)
                        nc.vector.tensor_copy(S[:, d, :], gbank[1 + d][:, :]).then_inc(g_free[1 + d], 1)
                    else:
                        nc.vector.scalar_tensor_tensor(out=S[:, d, :], in0=S[:, d, :], scalar=ebl[:, d, c:c + 1],
                                                       in1=gbank[1 + d][:, :], op0=ALU.mult, op1=ALU.add)\
                            .then_inc(g_free[1 + d], 1)

            STEP0 = 10
            HS = 7 + 2 * NB + 3

            with dve.Fori(0, HEADS) as h:
                step = [0]

                def link(ins):
                    ins.then_inc(dve_step, 1)
                    step[0] += 1
                    dve.wait_ge(dve_step, STEP0 + HS * h + step[0])

                for j in range(HG):
                    g = HG * h + j
                    for i in range(SLOTS, UNITS):
                        split_lo(dve, g, i)
                        if j == 1 and i < 6:
                            for m in range(2):
                                lv = 2 * (i - SLOTS) + m
                                distance(h, lv, LEVELS[lv], T)
                                step[0] += 1
                                dve.wait_ge(dve_step, STEP0 + HS * h + step[0])
                                negative(lv, T).then_inc(dist_ready, 1)
                        if j == 1 and i == 6:
                            b0, k0 = bT[:, :, 0:2 * CHUNK], kh[:, :, 0:2 * CHUNK]
                            v = b0.rearrange("p d (c t) -> p d c t", t=CHUNK)
                            nc.vector.tensor_tensor(k0.rearrange("p d (c t) -> p d c t", t=CHUNK),
                                                    v[:, :, :, CHUNK - 1:CHUNK].to_broadcast([P, DT, 2, CHUNK]), v,
                                                    ALU.subtract)
                            v = bT[:, :, 2 * CHUNK:PROMPT]
                            nc.vector.tensor_tensor(kh[:, :, 2 * CHUNK:PROMPT],
                                                    v[:, :, META - 1:META].to_broadcast([P, DT, META]), v, ALU.subtract)
                            v = bT[:, :, PROMPT:T].rearrange("p d (c t) -> p d c t", t=DSEQ)
                            nc.vector.tensor_tensor(kh[:, :, PROMPT:T].rearrange("p d (c t) -> p d c t", t=DSEQ),
                                                    v[:, :, :, DSEQ - 1:DSEQ].to_broadcast([P, DT, NSEQ, DSEQ]), v,
                                                    ALU.subtract).then_inc(kd_ready, 1)
                        if j == 3 and i < 7:
                            lv = 4 + i - SLOTS
                            if i == SLOTS:
                                dve.wait_ge(g_full[3], g_filled(h, 3, "kT"))
                            distance(h, lv, LEVELS[lv], 2 * CHUNK)
                            step[0] += 1
                            dve.wait_ge(dve_step, STEP0 + HS * h + step[0])
                            negative(lv - 4, 2 * CHUNK).then_inc(dist_ready, 1)
                        if j == 4 and i == SLOTS:
                            dve.wait_ge(bank_free[NB - 1], bank_frees(g - 1))
                            nc.vector.tensor_tensor(A[:, :, :], A[:, :, :], B[:, :, :], ALU.mult).then_inc(u_ready, 1)
                        if j == 4 and i > SLOTS:
                            if i == SLOTS + 1:
                                dve.wait_ge(u_ready, h + 1)
                                dve.wait_ge(uD_ready, 2 * h + 2)
                            for n in ([0], [1, 2], [3])[i - SLOTS - 1]:
                                for t in range(CW):
                                    w = params[:, bass.ds(P_CW + KT * t + NB * h + n, 1)]
                                    off = META - (CW - 1) + t
                                    y, yd = B[:, n, 0:SEQ], B[:, n, SEQ:N].rearrange("p (i t) -> p i t", t=DSEQ)
                                    u, ud = A[:, n, off:off + SEQ], uD[:, n, :, t:t + DSEQ]
                                    if t == 0:
                                        nc.vector.tensor_scalar(y, u, w, None, ALU.mult)
                                        last = nc.vector.tensor_scalar(yd, ud, w, None, ALU.mult)
                                    else:
                                        nc.vector.scalar_tensor_tensor(out=y, in0=u, scalar=w, in1=y,
                                                                       op0=ALU.mult, op1=ALU.add)
                                        last = nc.vector.scalar_tensor_tensor(out=yd, in0=ud, scalar=w, in1=yd,
                                                                              op0=ALU.mult, op1=ALU.add)
                                    if t < CW - 1:
                                        link(last)
                                    elif n == NB - 1:
                                        last.then_inc(conv_done, 1)
                        if j == 5 and i == SLOTS:
                            dve.wait_ge(bank_free[NB - 1], bank_frees(g - 1))
                            dve.wait_ge(conv_done, h + 1)
                            nc.vector.tensor_tensor(B[:, :, 0:N], B[:, :, 0:N], V[:, :, 0:N], ALU.mult)\
                                .then_inc(cb_used, 1)
                        if j == 6 and i == SLOTS:
                            dve.wait_ge(bank_free[NB - 1], bank_frees(g - 1))
                            dve.wait_ge(cb_used, h + 1)
                            nc.vector.tensor_tensor(B[:, :, 0:N], B[:, :, 0:N], A[:, :, 0:N], ALU.mult)\
                                .then_inc(ga_used, 1)
                    for i in range(SLOTS):
                        split_lo(dve, g + 1, i)
                    if j == 0:
                        dve.wait_ge(act_step, 3 * h + 3)
                        link(nc.vector.scalar_tensor_tensor(out=lev[:, 2, :, :], in0=lev[:, 2, :, :], scalar=0.0,
                                                            in1=lev[:, 3, :, :], op0=ALU.min, op1=ALU.subtract))
                        for d in range(DT):
                            last = nc.vector.tensor_tensor_scan(bT[:, d, :], carry[:, :], lev[:, 2, d, :],
                                                                0.0, ALU.mult, ALU.add)
                        last.then_inc(b_ready, 1)
                        dve.wait_ge(b_ready, h + 1)
                    if j == 2:
                        for c in range(2):
                            levels_evac(h, c, f"lev_a{c}", CHUNK, 4, mask[:, 0:4, :], True)
                        levels_evac(h, 2, "lev_a2", 48, 4, mask2[0:48, 0:4, :], True)
                    if j == 4:
                        for c in range(2):
                            levels_evac(h, c, f"lev_b{c}", CHUNK, 4, mask[:, 4:8, :], False)
                        dve.wait_ge(g_full[2], g_filled(h, 2, "lev_b2"))
                        dve.wait_ge(att_ready, 3 * h + 2)
                        link(nc.vector.tensor_tensor(tmpA[0:48, 0:48], gbank[2][0:48, 0:48], mask2[0:48, 4, :], ALU.mult))
                        nc.vector.tensor_tensor(att[0:48, 2, 0:48], att[0:48, 2, 0:48], tmpA[0:48, 0:48], ALU.add)\
                            .then_inc(att_ready, 1)
                        nc.vector.tensor_copy(kt2[:, :, :], gbank[2][0:16, P:P + DK]).then_inc(g_free[2], 1)
                    if j in (5, 6):
                        prompt_state(h, j - 5)
                        rms(h, j - 5, CHUNK)
                    if j in (5, 6):
                        for i in PIECE_SEQS[j]:
                            seq_state(h, i)
                    if j == 7:
                        rms(h, 2, 48)
                        prompt_state(h, 2)
                        for i in PIECE_SEQS[j]:
                            seq_state(h, i)
                        dve.wait_ge(g_free[1], g_emptied(h, 1, "o2T"))
                        dve.wait_ge(gated_ready, h + 1)
                        link(nc.vector.tensor_tensor(onT[:, :, :], onT[:, :, :], QK[:, :, 0:N], ALU.mult))
                        nc.vector.tensor_tensor(mix[:, bass.ds(NB * h, NB), :], onT[:, :, :], B[:, :, 0:N], ALU.add)\
                            .then_inc(m_ready, 1)
                assert step[0] == HS

            for k in range(HEADS):
                dve.wait_ge(fhi_ready, k + 1)
                kk = slice(NB * k, NB * (k + 1))
                if k == HEADS - 1:
                    dve.wait_ge(tail_stored, 1 + 32 * HEADS)
                nc.vector.tensor_tensor(f_lo[:, kk, :], mix[:, kk, :], f_hi[:, kk, :].bitcast(F32), ALU.subtract)\
                    .then_inc(f_ready, 1)

            def group_splits(g, has_next=True):
                for i in range(SLOTS, UNITS):
                    split_lo(dve, g, i)
                if has_next:
                    for i in range(SLOTS):
                        split_lo(dve, g + 1, i)

            def row_stats_of(m, first, copied=None):
                for t in range(NTT):
                    dve.wait_ge(g_full[t], first(t))
                    if copied is not None:
                        dve.wait_ge(yrow_copied, copied + t + 1)
                    nc.vector.bn_stats(stats[0:TT, t, bass.ds(m, 1), :], gbank[t][0:TT, :]).then_inc(g_free[t], 1)

            AFTER = STEP0 + HS * HEADS

            def residual(j, n_step):
                for n in range(NB):
                    dve.wait_ge(bank_full, banks_full(WO_G + j, n))
                    nc.vector.scalar_tensor_tensor(out=stage[:, n, :],
                                                   in0=x_hi[:, bass.ds(NB * j + n, 1), META:T].bitcast(F32),
                                                   scalar=ALPHA, in1=bank[n][:, 0:N], op0=ALU.mult, op1=ALU.add)\
                        .then_inc(bank_free[n], 1)
                dve.wait_ge(bank_free[NB - 1], bank_frees(WO_G + j))
                nc.vector.scalar_tensor_tensor(out=stage[:, :, :], in0=x_lo[:, bass.ds(NB * j, NB), META:T].bitcast(F32),
                                               scalar=ALPHA, in1=stage[:, :, :], op0=ALU.mult, op1=ALU.add)\
                    .then_inc(stage_full, 1)

            full1 = [G_END[t] for t in range(NTT)]
            for i in range(SLOTS, UNITS):
                split_lo(dve, WO_G, i)
            for i in range(SLOTS - 1):
                split_lo(dve, WO_G + 1, i)
            residual(0, 0)
            split_lo(dve, WO_G + 1, SLOTS - 1)
            with dve.Fori(1, NB) as j:
                for i in range(SLOTS, UNITS):
                    split_lo(dve, WO_G + j, i)
                row_stats_of(j - 1, lambda t: full1[t] + j)
                for i in range(SLOTS - 1):
                    split_lo(dve, WO_G + j + 1, i)
                dve.wait_ge(stage_copied, j)
                residual(j, 0)
                split_lo(dve, WO_G + j + 1, SLOTS - 1)
            row_stats_of(NB - 1, lambda t: full1[t] + NB)

            n_link = [0]

            def chain(ins):
                ins.then_inc(dve_step, 1)
                n_link[0] += 1
                dve.wait_ge(dve_step, AFTER + n_link[0])

            def aggregate(n_th, free_count):
                for t in range(NTT):
                    dve.wait_ge(g_free[t], free_count(t))
                    last = nc.vector.bn_aggr(mv[0:TT, t, :], stats[0:TT, t, :, :].rearrange("p q s -> p (q s)"))
                chain(last)
                nc.vector.tensor_scalar(rstd[0:TT, :], mv[0:TT, :, 1], EPS, None, ALU.add).then_inc(row_stats, 1)

            aggregate(1, lambda t: G_END[t] + NB)
            for t in range(NTT):
                last = nc.vector.tensor_scalar(diag[0:TT, 0, t, :], ident[0:TT, 0:TT], mv[0:TT, t, 0:1], None, ALU.mult)
            last.then_inc(diag_ready, 1)
            dve.wait_ge(row_sqrt, 4)
            chain(nc.vector.reciprocal(rstd[0:TT, :], rstd[0:TT, :]))
            for t in range(NTT):
                last = nc.vector.tensor_scalar(diag[0:TT, 1, t, :], ident[0:TT, 0:TT], rstd[0:TT, t:t + 1], None, ALU.mult)
            last.then_inc(diag_ready, 1)
            dve.wait_ge(g_full[3], G_END[3] + 1)
            dve.wait_ge(g_full[0], G_END[0] + NB + 1)
            dve.wait_ge(stage_copied, NB)
            for k in range(NB):
                kk = slice(NB * k, NB * (k + 1))
                if k >= 2:
                    dve.wait_ge(acc_ready, k - 1)
                p = pair[:, k % 2, :, :]
                chain(nc.vector.tensor_tensor(p, mix[:, kk, :], gbank[3][:, None, 0:N].to_broadcast([P, NB, N]),
                                              ALU.subtract))
                nc.vector.tensor_tensor(p, p, gbank[0][:, None, 0:N].to_broadcast([P, NB, N]), ALU.mult)\
                    .then_inc(norm_ready, 1)
                dve.wait_ge(x1hi_ready, k + 1)
                nc.vector.tensor_tensor(x_lo[:, kk, META:T], p, x_hi[:, kk, META:T].bitcast(F32), ALU.subtract)\
                    .then_inc(x1_ready, 1)
            dve.wait_ge(acc_ready, NB)
            dve.sem_inc(g_free[0], 1)
            dve.sem_inc(sq2_ready, 1)

            def up(b):
                with dve.Fori(0, NB) as j:
                    g = w1_group(b, j)
                    group_splits(g)
                    dve.wait_ge(bank_free[NB - 1], bank_frees(g))
                    dve.wait_ge(f_ready, HEADS + NB * b + j)
                    nc.vector.tensor_tensor(pair[:, 1, :, :], pair[:, 0, :, :], pair[:, 0, :, :], ALU.mult)\
                        .then_inc(sq2_ready, 1)

            with dve.Fori(0, LAST_B) as b:
                up(b)
                with dve.Fori(0, NB) as j:
                    g = w2_group(b, j)
                    for i in range(SLOTS, UNITS):
                        split_lo(dve, g, i)
                    for i in range(SLOTS - 1):
                        split_lo(dve, g + 1, i)
                    for n in range(NB):
                        dve.wait_ge(bank_full, banks_full(g, n))
                        acc = mix[:, bass.ds(NB * j + n, 1), :]
                        nc.vector.tensor_tensor(acc, acc, bank[n][:, 0:N], ALU.add).then_inc(bank_free[n], 1)
                    split_lo(dve, g + 1, SLOTS - 1)
            up(LAST_B)

            def last_sum(j):
                for n in range(NB):
                    dve.wait_ge(bank_full, banks_full(w2_group(LAST_B, j), n))
                    nc.vector.tensor_tensor(stage[:, n, :], mix[:, bass.ds(NB * j + n, 1), :], bank[n][:, 0:N],
                                            ALU.add).then_inc(bank_free[n], 1)
                dve.wait_ge(bank_free[NB - 1], bank_frees(w2_group(LAST_B, j)))
                dve.sem_inc(stage_full, 1)

            used = [NB + 1, NB, NB]
            full2 = [G_END[t] + used[t] for t in range(NTT)]
            g0 = w2_group(LAST_B, 0)
            for i in range(SLOTS, UNITS):
                split_lo(dve, g0, i)
            for i in range(SLOTS - 1):
                split_lo(dve, g0 + 1, i)
            last_sum(0)
            split_lo(dve, g0 + 1, SLOTS - 1)
            with dve.Fori(1, NB - 1) as j:
                for i in range(SLOTS, UNITS):
                    split_lo(dve, g0 + j, i)
                row_stats_of(j - 1, lambda t: full2[t] + j, NTT * (j - 1))
                for i in range(SLOTS - 1):
                    split_lo(dve, g0 + j + 1, i)
                last_sum(j)
                split_lo(dve, g0 + j + 1, SLOTS - 1)
            for i in range(SLOTS, UNITS):
                split_lo(dve, END_G, i)
            row_stats_of(NB - 2, lambda t: full2[t] + NB - 1, NTT * (NB - 2))
            last_sum(NB - 1)
            row_stats_of(NB - 1, lambda t: full2[t] + NB, NTT * (NB - 1))
            aggregate(2, lambda t: full2[t] + NB)
            dve.wait_ge(row_sqrt, 5)
            chain(nc.vector.reciprocal(rstd[0:TT, :], rstd[0:TT, :]))
            nc.vector.scalar_tensor_tensor(out=nbias[0:TT, :], in0=mv[0:TT, :, 0], scalar=-1.0, in1=rstd[0:TT, :],
                                           op0=ALU.mult, op1=ALU.mult).then_inc(row_scale, 1)
            dve.wait_ge(lnrow_landed, 32)
            for t in range(NTT):
                for half in range(2):
                    c = slice(half * D // 2, (half + 1) * D // 2)
                    m = 2 * t + half
                    dve.wait_ge(yn_ready, m + 1)
                    nc.vector.tensor_tensor(yrow[0:TT, t, c], yrow[0:TT, t, c], ln_w_row[0:TT, c], ALU.mult)\
                        .then_inc(yw_ready, 1)
                    dve.wait_ge(yw_ready, m + 1)
                    nc.vector.tensor_tensor(yrow[0:TT, t, c], yrow[0:TT, t, c], ln_b_row[0:TT, c], ALU.add)\
                        .then_inc(yb_ready, 1)

        @block.gpsimd
        def _(pool):
            for src, at, rows in [(ln_in_w, P_INW, 16), (ln_in_b, P_INB, 16), (ln1_w[0], P_LW, 16), (ln1_b[0], P_LB, 16),
                                  (b_a2[0], P_BA, 8), (gn_w[0], P_GN, 4)]:
                pool.dma_start(prow[at:at + rows, :], src.rearrange("(r c) -> r c", c=P)).then_inc(prow_landed, 16)
            pool.dma_start(prow[P_CW:P_ALL, :], conv_w[0].rearrange("w (r c) -> (w r) c", c=P)).then_inc(prow_landed, 16)
            pstep = [0]

            def seq(ins):
                ins.then_inc(pool_seq, 1)
                pstep[0] += 1
                pool.wait_ge(pool_seq, pstep[0])

            seq(nc.gpsimd.memset(ident[:, :], 0.0))
            nc.gpsimd.affine_select(out=ident[:, :], in_=ident[:, :], compare_op=ALU.not_equal, fill=1.0, base=0,
                                    pattern=[[-1, P]], channel_multiplier=1).then_inc(ident_ready, 1)
            nc.gpsimd.memset(ones[:, :], 1.0)
            seq(nc.gpsimd.memset(mask[:, :, :], 0.0))
            nc.gpsimd.affine_select(out=mask[:, 0, :], in_=mask[:, 0, :], compare_op=ALU.not_equal, fill=1.0, base=0,
                                    pattern=[[-1, P]], channel_multiplier=1)
            rights = []
            for m, L in enumerate(LEVELS):
                right = mask[:, m + 1, :].rearrange("p (b l) -> p b l", l=2 * L)[:, :, L:2 * L]
                rights.append(right)
                last = nc.gpsimd.memset(right, 1.0)
            seq(last)
            for m, L in enumerate(LEVELS):
                last = nc.gpsimd.affine_select(out=rights[m], in_=rights[m], compare_op=ALU.is_ge, fill=0.0, base=0,
                                               pattern=[[-2 * L, P // (2 * L)], [0, L]], channel_multiplier=1)
            seq(last)
            for m, L in enumerate(LEVELS):
                last = nc.gpsimd.affine_select(out=rights[m], in_=rights[m], compare_op=ALU.is_ge, fill=0.0, base=L - 1,
                                               pattern=[[2 * L, P // (2 * L)], [0, L]], channel_multiplier=-1)
            seq(last)
            seq(nc.gpsimd.tensor_copy(mask2[0:48, :, :], mask[0:48, 0:5, 0:48]))
            nc.gpsimd.memset(mask2[0:48, 3:5, META:48], 0.0)
            seq(nc.gpsimd.memset(seg0[0:32, :], 1.0))
            seq(nc.gpsimd.affine_select(out=seg0[0:32, :], in_=seg0[0:32, :], compare_op=ALU.is_ge, fill=0.0, base=0,
                                        pattern=[[-DSEQ, NSEQ]], channel_multiplier=1))
            nc.gpsimd.affine_select(out=seg0[0:32, :], in_=seg0[0:32, :], compare_op=ALU.is_ge, fill=0.0, base=DSEQ - 1,
                                    pattern=[[DSEQ, NSEQ]], channel_multiplier=-1).then_inc(pool_step, 1)
            for started in (*s0_stored, S_stored, tail_stored):
                pool.sem_inc(started, 1)
            for k in range(KT):
                pool.wait_ge(x_hi_ready, k + 1)
                nc.gpsimd.tensor_tensor(x_lo[:, k, :], hf[:, k % 2, :], x_hi[:, k, :].bitcast(F32), ALU.subtract)\
                    .then_inc(x_lo_ready, 1)
            pool.wait_ge(wa_landed, 16)
            pool.wait_ge(const_ready, 1)
            pool.wait_ge(g_free[2], 1)

            def load_state(h, i):
                s = i % S0_SLOTS
                per = len(range(s, NSEQ, S0_SLOTS))
                pool.wait_ge(s0_stored[s], 16 * (per * h + i // S0_SLOTS) + 1)
                pool.dma_start(S0[:, s, :, :], state_gla[0, i, bass.ds(h, 1), :, :]
                               .rearrange("o (d p) v -> p (o d) v", p=P)).then_inc(s0_landed[s], 16)

            def select_keys(h, i):
                if i >= 2:
                    pool.wait_ge(g_full[2], g_filled(h, 2, f"d{i - 2}"))
                    alone(pool)
                nc.gpsimd.tensor_scalar(kms[:, i % 2, :, :], kstk[:, :, :], segmask[0:96, i:i + 1], None, ALU.mult)\
                    .then_inc(kms_ready, 1)

            with pool.Fori(0, HEADS) as h:
                nc.gpsimd.tensor_copy(wa2h[:, :], wa2[:, bass.ds(h * DK, DK)]).then_inc(wa2h_ready, 1)
                for i in range(S0_SLOTS):
                    load_state(h, i)
                pool.wait_ge(eb_ready, h + 1)
                alone(pool)
                nc.gpsimd.tensor_copy(ebl[:, :, 0:2], eb[:, :, CHUNK - 1:2 * CHUNK:CHUNK])
                nc.gpsimd.tensor_copy(ebl[:, :, 2:11], eb[:, :, PROMPT - 1:T:DSEQ]).then_inc(ebl_ready, 1)
                pool.wait_ge(bank_free[NB - 1], bank_frees(HG * h + 1))

                def decay(lv, hi):
                    L = LEVELS[lv]
                    pool.wait_ge(exp_ready, 7 * h + lv + 1)
                    for d in range(DT):
                        x = lev[:, lv % 4, d, 0:hi].rearrange("p (b l) -> p b l", l=2 * L)
                        q = QK[:, d, 0:hi].rearrange("p (b l) -> p b l", l=2 * L)
                        k = QK[:, DT + d, 0:hi].rearrange("p (b l) -> p b l", l=2 * L)
                        nc.gpsimd.tensor_tensor(x[:, :, 0:L], x[:, :, 0:L], k[:, :, 0:L], ALU.mult)
                        last = nc.gpsimd.tensor_tensor(x[:, :, L:2 * L], x[:, :, L:2 * L], q[:, :, L:2 * L], ALU.mult)
                    last.then_inc(lev_ready, 1)

                for lv in range(3):
                    decay(lv, T)
                pool.wait_ge(kdecay_ready, h + 1)
                nc.gpsimd.tensor_tensor(kh[:, :, :], kh[:, :, :], QK[:, DT:2 * DT, :], ALU.mult).then_inc(qk_pool, 1)
                nc.gpsimd.tensor_tensor(qh[:, :, :], QK[:, 0:DT, CHUNK:2 * CHUNK], eb[:, :, CHUNK:2 * CHUNK], ALU.mult)\
                    .then_inc(qk_pool, 1)
                nc.gpsimd.tensor_tensor(q_dec[:, :, 0, 0:META], QK[:, 0:DT, 2 * CHUNK:PROMPT],
                                        eb[:, :, 2 * CHUNK:PROMPT], ALU.mult).then_inc(qk_pool, 1)
                for d in range(DT):
                    rows = q_dec[:, d, :, :].rearrange("p a b -> p (a b)")[:, 48 + META:48 + META + NSEQ * 52]
                    last = nc.gpsimd.tensor_tensor(rows.rearrange("p (i c) -> p i c", c=52)[:, :, 0:DSEQ],
                                                   QK[:, d, PROMPT:T].rearrange("p (i c) -> p i c", c=DSEQ),
                                                   eb[:, d, PROMPT:T].rearrange("p (i c) -> p i c", c=DSEQ), ALU.mult)
                last.then_inc(qk_pool, 1)
                decay(3, T)
                pool.wait_ge(qk_pool, 5 * h + 1)
                alone(pool)
                nc.gpsimd.tensor_copy(kst[:, :, 0:DEC], kh[:, :, PROMPT:T])
                nc.gpsimd.tensor_copy(kst[:, :, 2 * DEC:3 * DEC], kh[:, :, PROMPT:T]).then_inc(pool_head, 1)
                pool.wait_ge(pool_head, h + 1)
                nc.gpsimd.tensor_tensor(kst[:, :, DEC:2 * DEC], kh[:, :, PROMPT:T], kst[:, :, 0:DEC].bitcast(F32),
                                        ALU.subtract).then_inc(qk_pool, 1)
                pool.wait_ge(bank_free[NB - 1], bank_frees(HG * h + 2))
                alone(pool)
                nc.gpsimd.tensor_copy(vst[:, :, 0:DEC], V[:, :, PROMPT:T]).then_inc(vst_ready, 1)
                nc.gpsimd.tensor_copy(vst[:, :, DEC:2 * DEC], V[:, :, PROMPT:T]).then_inc(vst_ready, 1)
                pool.wait_ge(vst_ready, 3 * h + 2)
                nc.gpsimd.tensor_tensor(vst[:, :, 2 * DEC:3 * DEC], V[:, :, PROMPT:T], vst[:, :, 0:DEC].bitcast(F32),
                                        ALU.subtract).then_inc(vst_ready, 1)
                for lv in (4, 5, 6):
                    decay(lv, 2 * CHUNK)
                nc.gpsimd.tensor_copy(uD[:, :, :, 0:2], stT[:, bass.ds(NB * h, NB), :]
                                      .rearrange("p n (i c) -> p n i c", c=2)).then_inc(uD_ready, 1)
                pool.wait_ge(u_ready, h + 1)
                alone(pool)
                nc.gpsimd.tensor_copy(uD[:, :, :, 2:6], A[:, :, PROMPT:T].rearrange("p n (i c) -> p n i c", c=DSEQ))\
                    .then_inc(uD_ready, 1)
                nc.gpsimd.tensor_copy(tails[:, :, 0:2], A[:, :, PROMPT - 2:PROMPT])
                nc.gpsimd.tensor_copy(tails[:, :, 2:18].rearrange("p n (i c) -> p n i c", c=2),
                                      A[:, :, PROMPT:T].rearrange("p n (i c) -> p n i c", c=DSEQ)[:, :, :, 2:4])\
                    .then_inc(tails_ready, 1)
                pool.wait_ge(g_free[3], g_emptied(h, 3, "kst"))
                alone(pool)
                select_keys(h, 0)
                select_keys(h, 1)
                for j in (5, 6, 7):
                    if j == 7:
                        pool.wait_ge(bank_free[NB - 1], bank_frees(HG * h + 6))
                        nc.gpsimd.tensor_tensor(QK[:, :, 0:N], QK[:, :, 0:N], Fs[:, :, :], ALU.mult)\
                            .then_inc(silu_ready, 1)
                        pool.wait_ge(bank_free[NB - 1], bank_frees(HG * h + 7))
                        pool.wait_ge(silu_ready, h + 1)
                        nc.gpsimd.tensor_tensor(QK[:, :, 0:N], QK[:, :, 0:N], A[:, :, 0:N], ALU.mult)\
                            .then_inc(gated_ready, 1)
                    for i in PIECE_SEQS[j]:
                        if i + 2 < NSEQ:
                            select_keys(h, i + 2)
                        if i + S0_SLOTS < NSEQ:
                            load_state(h, i + S0_SLOTS)

            with pool.Fori(0, NB) as j:
                pool.wait_ge(stage_full, j + 1)
                alone(pool)
                nc.gpsimd.tensor_copy(mix[:, bass.ds(NB * j, NB), :], stage[:, :, :]).then_inc(stage_copied, 1)
            for s in range(S0_SLOTS):
                pool.wait_ge(s0_stored[s], 1 + 16 * HEADS * len(range(s, NSEQ, S0_SLOTS)))
            pool.wait_ge(tail_stored, 1 + 32 * HEADS)
            for row, src in ((ln_w_row, ln2_w), (ln_b_row, ln2_b)):
                pool.dma_start(row[0:TT, :], src[0:1, :].to_broadcast([TT, D])).then_inc(lnrow_landed, 16)
            for k in range(NB):
                pool.wait_ge(x1_ready, k + 1)
                nc.gpsimd.tensor_scalar(mix[:, NB * k:NB * (k + 1), :], pair[:, k % 2, :, :], ALPHA, None, ALU.mult)\
                    .then_inc(acc_ready, 1)
            with pool.Fori(0, FB) as b:
                with pool.Fori(0, NB) as j:
                    pool.wait_ge(sq2_ready, NB * b + j + 2)
                    alone(pool)
                    f = bass.ds(NB * j, NB)
                    nc.gpsimd.tensor_copy(f_hi[:, f, :], pair[:, 1, :, :]).then_inc(fhi_ready, 1)
                    pool.wait_ge(fhi_ready, HEADS + NB * b + j + 1)
                    nc.gpsimd.tensor_tensor(f_lo[:, f, :], pair[:, 1, :, :], f_hi[:, f, :].bitcast(F32), ALU.subtract)\
                        .then_inc(f_ready, 1)


_INS = ["x_prompt", "x_sample", "state_conv", "state_gla", "meta", "ln_in_w", "ln_in_b", "w_in", "conv_w", "w_a2",
        "b_a2", "gn_w", "w_o", "ln1_w", "ln1_b", "w1", "w2", "ln2_w", "ln2_b"]
_OUTS = [(1, SEQ, D), (NSEQ, DSEQ, D), (1, 1, CW - 1, D), (1, 1, HEADS, DK, DV), (1, NSEQ, CW - 1, D),
         (1, NSEQ, HEADS, DK, DV)]


def kernel(**inputs):
    import numpy as _np
    import concourse.bacc as _bacc
    from concourse.bass_utils import run_bass_kernel_spmd as _run

    nc = _bacc.Bacc("TRN2", target_bir_lowering=False, num_devices=1)
    arrays, args = {}, []
    for name in _INS:
        a = _np.ascontiguousarray(inputs[name])
        arrays[f"in_{name}"] = a
        args.append(nc.dram_tensor(f"in_{name}", a.shape, F32, kind="ExternalInput").ap())
    for i, shape in enumerate(_OUTS):
        args.append(nc.dram_tensor(f"out_{i}", shape, F32, kind="ExternalOutput").ap())
    build(nc, *args)
    r = _run(nc, [arrays], core_ids=[0])
    return tuple(r.results[0][f"out_{i}"] for i in range(len(_OUTS)))
```

```python
from contextlib import ExitStack

import concourse.bass as bass
from concourse import mybir

F32 = mybir.dt.float32
F32R = mybir.dt.float32r
BF16 = mybir.dt.bfloat16
ALU = mybir.AluOpType
ACT = mybir.ActivationFunctionType
AX_X = mybir.AxisListType.X

P = 128
D = 2048
KT = D // P
META, SEQ = 16, 256
NSEQ, DSEQ = 8, 4
DEC = NSEQ * DSEQ
PROMPT = META + SEQ
T = PROMPT + DEC
N = T - META
HEADS, DK, DV = 4, 256, 512
DT = DK // P
RANK = 16
FF = 4 * D
CW = 3
EPS = 1e-5
ALPHA = 2.0 ** 0.25
GW = 512
NB = GW // P
UK = 2
UNITS = KT // UK
SLOTS = 4
HG = 8
CHUNK = 128
CONV0 = META - (CW - 1)
EARLY = 2 * CHUNK - META
TT = 96
NTT = N // TT
FB = FF // D
CB, CC, CX, WQ, WK = 0, D, 2 * D, 3 * D, 3 * D + D // 2
WV = 4 * D
WG, WA, WGA, WGB = 5 * D, 6 * D, 6 * D + RANK, 7 * D + RANK
P_INW, P_INB, P_LW, P_LB, P_BA, P_GN, P_CW = 0, 16, 32, 48, 64, 72, 76
P_ALL = P_CW + CW * KT
LEVELS = [1, 2, 4, 8, 16, 32, 64]
USES = [
    ["z0", "lev_a0", "v0", "lev_b0", "o0", "o1", "o0T", "o1T", "tail"],
    ["z1", "lev_a1", "v1", "lev_b1", "d0", "d1", "d2", "s0", "d3", "d4", "d5", "s1", "d6", "d7", "s2"],
    ["lev_a2", "v2", "lev_b2", "d0", "d1", "d2", "s0", "d3", "d4", "d5", "s1", "d6", "d7", "s2"],
    ["kT", "vst", "kst", "o2", "o2T"],
]
BEFORE = [7, 6, 5, 1]
X_BANKS = 3
X_FIRST = [1, 1, 0]
HF_SLOTS = 4
S0_SLOTS = 3
PIECE_SEQS = {5: [0, 1, 2], 6: [3, 4, 5], 7: [6, 7]}
SPLIT_AFTER = [SLOTS, SLOTS + 1, SLOTS + 3]
READ_AFTER = [SLOTS - 1, SLOTS, SLOTS + 2]
UPDATE_AFTER = [SLOTS + 3, UNITS, UNITS + 2]
Q_LO = 64
QW = Q_LO + 48


def build(nc, x_prompt, x_sample, state_conv, state_gla, meta, ln_in_w, ln_in_b, w_in, conv_w,
          w_a2, b_a2, gn_w, w_o, ln1_w, ln1_b, w1, w2, ln2_w, ln2_b,
          y_prompt, y_sample, conv_prompt, gla_prompt, conv_sample, gla_sample):
    w_in, w_o, w1, w2 = w_in[0], w_o[0], w1[0], w2[0]
    with ExitStack() as ctx:
        scope = [ctx]

        def sb(name, shape, dt=F32):
            return scope[-1].enter_context(nc.sbuf_tensor(name, shape, dt))

        def sem(name):
            return ctx.enter_context(nc.semaphore(name))

        raw = sb("raw", [P, SLOTS, UK, GW])
        w_hi = sb("w_hi", [P, SLOTS, UK, GW], F32R)
        w_lo = sb("w_lo", [P, SLOTS, UK, GW], F32R)
        x_hi = sb("x_hi", [P, KT, T], F32R)
        x_lo = sb("x_lo", [P, KT, T], F32R)
        mix = sb("mix", [P, KT, N])
        ident = sb("ident", [P, P])
        ones = sb("ones", [P, P])
        params = sb("params", [P, P_ALL])
        stats = sb("stats", [P, NTT, KT // NB, 6])
        mv = sb("mv", [P, NTT, 2])
        var = sb("var", [P, NTT])
        neg_mean = sb("neg_mean", [P, NTT])
        rstd = sb("rstd", [P, NTT])
        nbias = sb("nbias", [P, NTT])
        minus_half = sb("minus_half", [P, NTT])
        stage = sb("stage", [P, NB, N])
        consts = ExitStack()
        scope.append(consts)
        mask = sb("mask", [P, 8, P], BF16)
        mask2 = sb("mask2", [P, 5, 48], BF16)
        segmask = sb("segmask", [P, NSEQ])
        carry = sb("carry", [P, T], BF16)
        a1T = sb("a1T", [RANK, T])
        stT = sb("stT", [P, KT, NSEQ * 2])
        q_dec = sb("q_dec", [P, (DT - 1) * 48 + QW])
        q_parts = sb("q_parts", [P, DT, NSEQ, QW], F32R)

        def phase(alloc):
            with ExitStack() as inner:
                scope.append(inner)
                got = alloc()
                scope.pop()
            return got

        def start_buffers():
            return (sb("xrow", [P, 3, D]), sb("wa1", [P, KT, P]), sb("wa1_hi", [P, KT, RANK], F32R),
                    sb("wa1_lo", [P, KT, RANK], F32R), sb("hf", [P, HF_SLOTS, T]), sb("prow", [P, P]), sb("strow", [16, D]),
                    sb("stats_in", [P, 3, 4, 6]))

        xrow, wa1, wa1_hi, wa1_lo, hf, prow, strow, stats_in = phase(start_buffers)

        def head_buffers():
            return dict(
                lev=sb("lev", [P, 4, DT, T]), eb=sb("eb", [P, DT, T]), kh=sb("kh", [P, DT, T]),
                bT=sb("bT", [P, DT, T]), qh=sb("qh", [P, DT, CHUNK]), prod=sb("prod", [P, 4, CHUNK]),
                ktok=sb("ktok", [P, 2, DT, P]), kst=sb("kst", [P, DT, 96], F32R), vst=sb("vst", [P, NB, 96], F32R),
                V=sb("V", [P, NB, T]), F=sb("F", [P, NB, N]), kt2=sb("kt2", [16, DT, P]),
                kstk=sb("kstk", [96, DT, P]), kms=sb("kms", [96, 2, DT, P], F32R), tmpA=sb("tmpA", [P, CHUNK]),
                wa2h=sb("wa2h", [RANK, DK]),
                onT=sb("onT", [P, NB, N]), QK=sb("QK", [P, NB, T]), A=sb("A", [P, NB, T]), B=sb("B", [P, NB, T]),
                vtok=sb("vtok", [P, 3, DV]), vstk=sb("vstk", [96, DV], F32R), att=sb("att", [P, 3, CHUNK]),
                S=sb("S", [P, DT, DV]), S0=sb("S0", [P, S0_SLOTS, DT, DV]), uD=sb("uD", [P, NB, NSEQ, 6]),
                tails=sb("tails", [P, NB, 18]), ebl=sb("ebl", [P, DT, 11]),
                ss=sb("ss", [P, 3]), rs=sb("rs", [P, 3]), ms=sb("ms", [P, 3]))

        hb = phase(head_buffers)
        lev, eb, kh, bT, qh, prod, ktok, kst, vst = (hb[k] for k in "lev eb kh bT qh prod ktok kst vst".split())
        V, Fs, kt2, kstk, kms, tmpA, wa2h, onT, QK = (hb[k] for k in "V F kt2 kstk kms tmpA wa2h onT QK".split())
        A, B, vtok, vstk, att, S, S0, uD = (hb[k] for k in "A B vtok vstk att S S0 uD".split())
        tails, ebl, ss, rs, ms = (hb[k] for k in "tails ebl ss rs ms".split())
        junk = prod[:, :, :].rearrange("p a b -> p (a b)")
        tailrow = ktok[0:18, :, :, :].rearrange("p a b c -> p (a b c)")

        def state_parts():
            return sb("s_hi", [P, 2, DT, DV], F32R), sb("s_lo", [P, 2, DT, DV], F32R)

        def o2_parts():
            return sb("o2_low", [48, DV]), sb("o2_sum", [48, DV])

        def tail_buffers():
            return (sb("f_hi", [P, KT, N], F32R), sb("f_lo", [P, KT, N], F32R),
                    sb("pair", [P, 2, NB, N]), sb("diag", [P, 2, NTT, TT]), sb("yrow", [P, NTT, D]),
                    sb("ln_w_row", [P, D]), sb("ln_b_row", [P, D]))

        s_hi, s_lo = phase(state_parts)
        o2_low, o2_sum = phase(o2_parts)
        scope.pop()
        consts.close()
        f_hi, f_lo, pair, diag, yrow, ln_w_row, ln_b_row = phase(tail_buffers)

        bank = [ctx.enter_context(nc.psum_tensor(f"bank{n}", [P, 512], F32)) for n in range(NB)]
        gbank = [ctx.enter_context(nc.psum_tensor(f"gbank{n}", [P, 512], F32)) for n in range(4)]

        raw_landed = [sem(f"raw_landed{s}") for s in range(SLOTS)]
        k_landed = [sem(f"k_landed{s}") for s in range(SLOTS)]
        hi_ready = sem("hi_ready")
        lo_ready = sem("lo_ready")
        units_used = sem("units_used")
        bank_full = sem("bank_full")
        bank_free = [sem(f"bank_free{n}") for n in range(NB)]
        g_full = [sem(f"g_full{n}") for n in range(4)]
        g_free = [sem(f"g_free{n}") for n in range(4)]
        x_landed = [sem(f"x_landed{i}") for i in range(3)]
        prow_landed = sem("prow_landed")
        st_landed = sem("st_landed")
        wa1_landed = sem("wa1_landed")
        row_stats = sem("row_stats")
        row_pow = sem("row_pow")
        row_scale = sem("row_scale")
        row_done = sem("row_done")
        last_rows_done = sem("last_rows_done")
        const_ready = sem("const_ready")
        ident_ready = sem("ident_ready")
        x_hi_ready = sem("x_hi_ready")
        x_lo_ready = [sem("x_lo_ready_even"), sem("x_lo_ready_odd")]
        wa1_split = sem("wa1_split")
        pool_seq = sem("pool_seq")
        pool_head = sem("pool_head")
        masks_ready = sem("masks_ready")
        dve_step = sem("dve_step")
        act_step = sem("act_step")
        z_ready = sem("z_ready")
        ln_ready = sem("ln_ready")
        b_ready = sem("b_ready")
        dist_ready = sem("dist_ready")
        exp_ready = sem("exp_ready")
        eb_ready = sem("eb_ready")
        kd_ready = sem("kd_ready")
        kdecay_ready = sem("kdecay_ready")
        lev_ready = sem("lev_ready")
        wa2h_landed = sem("wa2h_landed")
        q_step = sem("q_step")
        s_hi_ready = sem("s_hi_ready")
        s_lo_ready = sem("s_lo_ready")
        s_read = sem("s_read")
        o2_low_ready = sem("o2_low_ready")
        o2_sum_ready = sem("o2_sum_ready")
        qk_pool = sem("qk_pool")
        ebl_ready = sem("ebl_ready")
        vst_ready = sem("vst_ready")
        kms_ready = sem("kms_ready")
        tails_ready = sem("tails_ready")
        u_ready = sem("u_ready")
        uD_ready = sem("uD_ready")
        conv_done = sem("conv_done")
        cb_used = sem("cb_used")
        ga_used = sem("ga_used")
        silu_ready = sem("silu_ready")
        gated_ready = sem("gated_ready")
        ss_ready = sem("ss_ready")
        ms_ready = sem("ms_ready")
        rs_ready = sem("rs_ready")
        att_ready = sem("att_ready")
        sc1_ready = sem("sc1_ready")
        s0_landed = [sem(f"s0_landed{s}") for s in range(S0_SLOTS)]
        s0_stored = [sem(f"s0_stored{s}") for s in range(S0_SLOTS)]
        s0_updated = sem("s0_updated")
        S_final = sem("S_final")
        S_stored = sem("S_stored")
        m_ready = sem("m_ready")
        tail_stored = sem("tail_stored")
        fhi_ready = sem("fhi_ready")
        f_ready = sem("f_ready")
        x_staged = sem("x_staged")
        stage_copied = sem("stage_copied")
        diag_ready = sem("diag_ready")
        norm_ready = sem("norm_ready")
        aff_ready = sem("aff_ready")
        x1hi_ready = sem("x1hi_ready")
        x1_ready = [sem("x1_ready_even"), sem("x1_ready_odd")]
        acc_ready = sem("acc_ready")
        relu_ready = sem("relu_ready")
        sq2_ready = sem("sq2_ready")
        yrow_copied = sem("yrow_copied")
        lnrow_landed = sem("lnrow_landed")
        yn_ready = sem("yn_ready")
        yw_ready = sem("yw_ready")
        yb_ready = sem("yb_ready")
        out_stored = sem("out_stored")

        nbias_step = sem("nbias_step")
        nbias_ready = sem("nbias_ready")
        pool_w = sem("pool_w")
        pool_piece_ready = sem("pool_piece_ready")
        waits_alone = sem("waits_alone")

        def banks_full(g, n):
            return NB * g + n + 1

        def bank_frees(g):
            return g + 2

        def landed(g, i):
            return 16 * (2 * g + 1 + i // SLOTS)

        def g_index(h, k, use):
            return BEFORE[k] + len(USES[k]) * h + USES[k].index(use)

        def g_filled(h, k, use):
            return g_index(h, k, use) + 1

        def g_emptied(h, k, use):
            return g_index(h, k, use) + 1

        def g_available(h, k, use):
            return g_index(h, k, use)

        G_END = [BEFORE[k] + len(USES[k]) * HEADS for k in range(4)]
        WO_G, FF_G = HG * HEADS, HG * HEADS + NB
        LAST_B = FB - 1

        def w1_group(b, j):
            return FF_G + 2 * NB * b + j

        def w2_group(b, j):
            return FF_G + 2 * NB * b + NB + j

        END_G = w2_group(LAST_B, NB - 1)

        def alone(engine):
            engine.sem_inc(waits_alone, 1)

        PIECES = [(t, slice(half * D // 2, (half + 1) * D // 2)) for t in range(NTT) for half in range(2)]
        POOL_PIECE = PIECES[-1]
        DVE_PIECES = PIECES[:-1]

        def split_hi(act, g, i, with_k=None):
            s = i % SLOTS
            act.wait_ge(raw_landed[s], landed(g, i))
            if with_k is not None:
                act.wait_ge(k_landed[s], 16 * (2 * with_k + 1 + i // SLOTS))
            if i >= SLOTS:
                act.wait_ge(units_used, (UNITS - 1) * g + i - SLOTS + 1)
            elif not (isinstance(g, int) and g == 0):
                if i < SLOTS - 1:
                    act.wait_ge(units_used, (UNITS - 1) * (g - 1) + i + SLOTS + 1)
                else:
                    act.wait_ge(bank_full, banks_full(g - 1, NB - 1))
            nc.scalar.activation(w_hi[:, s, :, :], raw[:, s, :, :], ACT.Copy).then_inc(hi_ready, 1)

        def split_lo(dve, g, i):
            s = i % SLOTS
            dve.wait_ge(hi_ready, UNITS * g + i + 1)
            nc.vector.tensor_tensor(w_lo[:, s, :, :], raw[:, s, :, :], w_hi[:, s, :, :].bitcast(F32),
                                    ALU.subtract).then_inc(lo_ready, 1)

        def dense_group(pe, g, a_hi, a_lo, cols, operand=None, between=None, after=None):
            for i in range(UNITS):
                s = i % SLOTS
                pe.wait_ge(lo_ready, SLOTS + UNITS * g + i + 1)
                if operand is not None:
                    pe.wait_ge(*operand(i))
                for n in range(NB):
                    if i == 0:
                        pe.wait_ge(bank_free[n], bank_frees(g - 1))
                    c0, c1 = cols[n]
                    out = bank[n][:, 0:c1 - c0]
                    for kk in range(UK):
                        kt = UK * i + kk
                        wh, wl = w_hi[:, s, kk, n * P:(n + 1) * P], w_lo[:, s, kk, n * P:(n + 1) * P]
                        nc.tensor.matmul(out, wh, a_hi[:, kt, c0:c1], start=(kt == 0), stop=False)
                        nc.tensor.matmul(out, wh, a_lo[:, kt, c0:c1], start=False, stop=False)
                        last = nc.tensor.matmul(out, wl, a_hi[:, kt, c0:c1], start=False, stop=(kt == KT - 1))
                    if i == UNITS - 1:
                        last.then_inc(bank_full, 1)
                if i < UNITS - 1:
                    last.then_inc(units_used, 1)
                if i == SLOTS - 1 and between is not None:
                    between()
                if after is not None:
                    after(i)

        def split_x1(engine, ops, i):
            kk = slice(UK * i, UK * (i + 1))
            engine.wait_ge(x1hi_ready, i + 1)
            ops.tensor_tensor(x_lo[:, kk, META:T], mix[:, kk, :], x_hi[:, kk, META:T].bitcast(F32), ALU.subtract)\
                .then_inc(x1_ready[i % 2], 1)

        ALL, OUT, MIX = [(0, T)] * NB, [(META, T)] * NB, [(0, N)] * NB
        CONV = [(CONV0, T)] * NB
        GROUP_COLS = [CONV, OUT[:DT] + ALL[DT:], ALL, CONV, OUT, OUT, OUT, OUT]

        def transpose(out, in_, rows):
            return nc.tensor.transpose(out, in_, ident[0:rows, 0:rows])

        def row_transposes(pe, first, g):
            for n in range(NB):
                pe.wait_ge(bank_free[n], bank_frees(g))
                for t in range(NTT):
                    if n == 0:
                        pe.wait_ge(g_free[t], first(t))
                    last = transpose(gbank[t][0:TT, n * P:(n + 1) * P], stage[:, n, t * TT:(t + 1) * TT], P)
                    if n == NB - 1:
                        last.then_inc(g_full[t], 1)

        block = ctx.enter_context(nc.Block())

        @block.sync
        def _(sp):
            sp.dma_start(xrow[0:META, 0, :], meta).then_inc(x_landed[0], 16)
            sp.dma_start(xrow[META:P, 0, :], x_prompt[0, 0:P - META, :]).then_inc(x_landed[0], 16)
            sp.dma_start(xrow[:, 1, :], x_prompt[0, P - META:2 * P - META, :]).then_inc(x_landed[1], 16)
            sp.dma_start(xrow[0:META, 2, :], x_prompt[0, 2 * P - META:SEQ, :]).then_inc(x_landed[2], 16)
            sp.dma_start(xrow[META:META + DEC, 2, :], x_sample.rearrange("a b d -> (a b) d")).then_inc(x_landed[2], 16)
            for src, at, rows in [(ln_in_w, P_INW, 16), (ln_in_b, P_INB, 16), (ln1_w[0], P_LW, 16), (ln1_b[0], P_LB, 16),
                                  (b_a2[0], P_BA, 8), (gn_w[0], P_GN, 4)]:
                sp.dma_start(prow[at:at + rows, :], src.rearrange("(r c) -> r c", c=P)).then_inc(prow_landed, 16)
            sp.dma_start(prow[P_CW:P_ALL, :], conv_w[0].rearrange("w (r c) -> (w r) c", c=P)).then_inc(prow_landed, 16)
            sp.dma_start(wa1[:, :, :], w_in[:, WA:WA + P].rearrange("(k p) c -> p k c", p=P)).then_inc(wa1_landed, 16)

            def load_unit(u, slot, src):
                sp.wait_ge(lo_ready, u + 1)
                alone(sp)
                sp.dma_start(raw[:, slot, :, :], src.rearrange("(k p) c -> p k c", p=P))\
                    .then_inc(raw_landed[slot], 16)

            def load_group(g, w, row0, col):
                for i in range(UNITS):
                    load_unit(UNITS * g + i, i % SLOTS, w[bass.ds(row0 + i * UK * P, UK * P), bass.ds(col, GW)])

            with sp.Fori(0, HEADS) as h:
                for j, first in enumerate([CC, None, WV, CX, CB, WGA, WG, WGB]):
                    if first is not None:
                        load_group(HG * h + j, w_in, 0, first + h * GW)
                        continue
                    for i in range(UNITS):
                        s, rows = i % SLOTS, slice(i * UK * P, (i + 1) * UK * P)
                        sp.wait_ge(lo_ready, UNITS * (HG * h + j) + i + 1)
                        sp.dma_start(raw[:, s, :, 0:DK], w_in[rows, bass.ds(WQ + h * DK, DK)]
                                     .rearrange("(k p) c -> p k c", p=P)).then_inc(raw_landed[s], 16)
                        sp.dma_start(raw[:, s, :, DK:GW], w_in[rows, bass.ds(WK + h * DK, DK)]
                                     .rearrange("(k p) c -> p k c", p=P)).then_inc(k_landed[s], 16)
            with sp.Fori(0, NB) as j:
                load_group(WO_G + j, w_o, 0, j * GW)
            with sp.Fori(0, FB) as b:
                with sp.Fori(0, NB) as j:
                    load_group(w1_group(b, j), w1, 0, b * D + j * GW)
                with sp.Fori(0, NB) as j:
                    load_group(w2_group(b, j), w2, b * D, j * GW)
            for m, (t, c) in enumerate(PIECES):
                if (t, c) == POOL_PIECE:
                    sp.wait_ge(pool_piece_ready, 1)
                else:
                    sp.wait_ge(yb_ready, m + 1)
                a, e = t * TT, (t + 1) * TT
                n_prompt = min(e, SEQ) - a
                sp.dma_start(y_prompt[0, a:a + n_prompt, c], yrow[0:n_prompt, t, c]).then_inc(out_stored, 16)
                if n_prompt < TT:
                    sp.dma_start(y_sample.rearrange("a b d -> (a b) d")[:, c],
                                 yrow[n_prompt:TT, t, c]).then_inc(out_stored, 16)
            sp.wait_ge(out_stored, 16 * 2 * (NTT + 1))
            for s in range(S0_SLOTS):
                sp.wait_ge(s0_stored[s], 1 + 16 * HEADS * len(range(s, NSEQ, S0_SLOTS)))
            sp.wait_ge(S_stored, 1 + 16 * HEADS)
            sp.wait_ge(tail_stored, 1 + 32 * HEADS)

        @block.tensor
        def _(pe):
            pe.wait_ge(ident_ready, 1)
            pe.wait_ge(prow_landed, 16 * 7)
            transpose(gbank[0][:, 0:P_ALL], prow[0:P_ALL, :], P_ALL).then_inc(g_full[0], 1)
            pe.wait_ge(st_landed, 16)
            for k in range(KT):
                last = transpose(gbank[1][:, 16 * k:16 * k + 16], strow[:, k * P:(k + 1) * P], 16)
            last.then_inc(g_full[1], 1)
            for k in range(KT + HF_SLOTS):
                if k < KT:
                    n = k % X_BANKS
                    if X_FIRST[n] + k // X_BANKS > 0:
                        pe.wait_ge(g_free[n], X_FIRST[n] + k // X_BANKS)
                    for i, rows in enumerate([P, P, T - 2 * P]):
                        if k == 0:
                            pe.wait_ge(*((row_done, i + 1) if i < 2 else (last_rows_done, 1)))
                        last = transpose(gbank[n][:, i * P:i * P + rows], xrow[0:rows, i, k * P:(k + 1) * P], rows)
                    last.then_inc(g_full[n], 1)
                if k >= HF_SLOTS:
                    kt = k - HF_SLOTS
                    if kt == 0:
                        pe.wait_ge(wa1_split, 2)
                    pe.wait_ge(x_lo_ready[kt % 2], kt // 2 + 1)
                    out = gbank[3][0:RANK, 0:T]
                    nc.tensor.matmul(out, wa1_hi[:, kt, :], x_hi[:, kt, :], start=(kt == 0), stop=False)
                    nc.tensor.matmul(out, wa1_hi[:, kt, :], x_lo[:, kt, :], start=False, stop=False)
                    last = nc.tensor.matmul(out, wa1_lo[:, kt, :], x_hi[:, kt, :], start=False, stop=(kt == KT - 1))
            last.then_inc(g_full[3], 1)

            def level(h, k, c, c0, w, entries, use):
                pe.wait_ge(g_free[k], g_available(h, k, use))
                for m, buf in enumerate(entries):
                    out = gbank[k][0:w, m * w:(m + 1) * w]
                    for d in range(DT):
                        ks = QK[:, DT + d, c0:c0 + w] if buf is None else lev[:, buf, d, c0:c0 + w]
                        qs = QK[:, d, c0:c0 + w] if buf is None else ks
                        last = nc.tensor.matmul(out, ks, qs, start=(d == 0), stop=(d == DT - 1))
                return last

            def state_update(h, use, keys, vals):
                for d in range(DT):
                    pe.wait_ge(g_free[1 + d], g_available(h, 1 + d, use))
                    nc.tensor.matmul(gbank[1 + d][:, :], keys[:, d, :], vals, start=True, stop=True)\
                        .then_inc(g_full[1 + d], 1)

            def seq_read(h, i):
                if i == 0:
                    pe.wait_ge(g_free[3], g_available(h, 3, "o2"))
                    alone(pe)
                pe.wait_ge(s_lo_ready, NSEQ * h + i + 1)
                for d in range(DT):
                    nc.tensor.matmul(gbank[3][0:QW, :], q_parts[:, d, i, :], s_hi[:, i % 2, d, :],
                                     start=(i == 0 and d == 0), stop=False)
                for d in range(DT):
                    last = nc.tensor.matmul(gbank[3][0:48, :], q_parts[:, d, i, 0:48], s_lo[:, i % 2, d, :],
                                            start=False, stop=False)
                last.then_inc(s_read, 1)

            def rows_to_features(h, k, use, src, rows):
                pe.wait_ge(g_free[k], g_available(h, k, use))
                alone(pe)
                for n in range(NB):
                    last = transpose(src[0](n), src[1](n), rows)
                last.then_inc(g_full[k], 1)

            def o_transposed(h, c):
                rows_to_features(h, 0, f"o{c}T", (lambda n: gbank[0][:, n * P:(n + 1) * P],
                                                  lambda n: vtok[:, c, n * P:(n + 1) * P]), P)

            def last_chunk(h):
                nc.tensor.matmul(gbank[3][0:48, :], att[0:48, 2, 0:48], vtok[0:48, 2, :], start=False, stop=False)
                for d in range(DT):
                    w = QW if d == DT - 1 else 48
                    last = nc.tensor.matmul(gbank[3][0:w, :], q_dec[:, d * 48:d * 48 + w], S[:, d, :],
                                            start=False, stop=(d == DT - 1))
                last.then_inc(g_full[3], 1)

            def reads(h, j):
                if j not in PIECE_SEQS:
                    return None

                def after(unit):
                    if unit in READ_AFTER:
                        m = READ_AFTER.index(unit)
                        if m < len(PIECE_SEQS[j]):
                            seq_read(h, PIECE_SEQS[j][m])
                            seq_write(h, PIECE_SEQS[j][m])
                    if j == 7:
                        if unit == 0:
                            o_transposed(h, 0)
                        if unit == 2:
                            o_transposed(h, 1)
                        if unit == 4:
                            pe.wait_ge(tails_ready, h + 1)
                            rows_to_features(h, 0, "tail", (lambda n: gbank[0][0:18, n * P:(n + 1) * P],
                                                            lambda n: tails[:, n, :]), P)
                        if unit == 5:
                            last_chunk(h)
                        if unit == 6:
                            state_update(h, "s2", kt2, vtok[0:16, 2, :])
                return after

            def seq_write(h, i):
                pe.wait_ge(kms_ready, NSEQ * h + i + 1)
                state_update(h, f"d{i}", kms[:, i % 2, :, :], vstk[:, :])

            with pe.Fori(0, HEADS) as h:
                for j in range(HG):
                    dense_group(pe, HG * h + j, x_hi, x_lo, GROUP_COLS[j], after=reads(h, j))
                    if j == 0:
                        pe.wait_ge(wa2h_landed, 16 * (h + 1))
                        for d in range(DT):
                            pe.wait_ge(g_free[d], g_available(h, d, f"z{d}"))
                            nc.tensor.matmul(gbank[d][:, 0:T], wa2h[:, d * P:(d + 1) * P], a1T[:, :],
                                             start=True, stop=True).then_inc(g_full[d], 1)
                    if j == 2:
                        pe.wait_ge(lev_ready, 7 * h + 3)
                        for c in range(2):
                            level(h, c, c, c * CHUNK, CHUNK, [None, 0, 1, 2], f"lev_a{c}").then_inc(g_full[c], 1)
                        level(h, 2, 2, 2 * CHUNK, 48, [None, 0, 1, 2], "lev_a2").then_inc(g_full[2], 1)
                        pe.wait_ge(qk_pool, 5 * h + 4)
                        pe.wait_ge(g_free[3], g_available(h, 3, "kT"))
                        for c in range(2):
                            for d in range(DT):
                                m = c * DT + d
                                last = transpose(gbank[3][:, m * P:(m + 1) * P],
                                                 kh[:, d, c * CHUNK:(c + 1) * CHUNK], P)
                        last.then_inc(g_full[3], 1)
                    if j == 3:
                        for c, w in enumerate([CHUNK, CHUNK, 48]):
                            pe.wait_ge(g_free[c], g_available(h, c, f"v{c}"))
                            alone(pe)
                            for n in range(NB):
                                last = transpose(gbank[c][0:w, n * P:(n + 1) * P], V[:, n, c * CHUNK:c * CHUNK + w], P)
                            last.then_inc(g_full[c], 1)
                        pe.wait_ge(vst_ready, 3 * h + 3)
                        pe.wait_ge(g_free[3], g_available(h, 3, "vst"))
                        for n in range(NB):
                            last = transpose(gbank[3][0:96, n * P:(n + 1) * P], vst[:, n, :].bitcast(F32), P)
                        last.then_inc(g_full[3], 1)
                    if j == 4:
                        pe.wait_ge(lev_ready, 7 * h + 7)
                        for c in range(2):
                            level(h, c, c, c * CHUNK, CHUNK, [3, 0, 1, 2], f"lev_b{c}").then_inc(g_full[c], 1)
                        level(h, 2, 2, 2 * CHUNK, 48, [3], "lev_b2")
                        for d in range(DT):
                            last = transpose(gbank[2][0:16, P + d * P:P + (d + 1) * P],
                                             kh[:, d, 2 * CHUNK:PROMPT], P)
                        last.then_inc(g_full[2], 1)
                        pe.wait_ge(qk_pool, 5 * h + 5)
                        pe.wait_ge(g_free[3], g_available(h, 3, "kst"))
                        for d in range(DT):
                            last = transpose(gbank[3][0:96, d * P:(d + 1) * P], kst[:, d, :].bitcast(F32), P)
                        last.then_inc(g_full[3], 1)
                    if j == 5:
                        pe.wait_ge(att_ready, 3 * h + 3)
                        pe.wait_ge(g_free[0], g_available(h, 0, "o0"))
                        nc.tensor.matmul(gbank[0][:, :], att[:, 0, :], vtok[:, 0, :], start=True, stop=True)\
                            .then_inc(g_full[0], 1)
                        state_update(h, "s0", ktok[:, 0, :, :], vtok[:, 0, :])
                    if j == 6:
                        pe.wait_ge(g_free[0], g_available(h, 0, "o1"))
                        nc.tensor.matmul(gbank[0][:, :], att[:, 1, :], vtok[:, 1, :], start=True, stop=False)
                        for d in range(DT):
                            last = nc.tensor.matmul(gbank[0][:, :], qh[:, d, :], S[:, d, :], start=False,
                                                    stop=(d == DT - 1))
                        last.then_inc(g_full[0], 1)
                        state_update(h, "s1", ktok[:, 1, :, :], vtok[:, 1, :])
                    if j == 7:
                        rows_to_features(h, 3, "o2T", (lambda n: gbank[3][:, n * 48:(n + 1) * 48],
                                                       lambda n: vtok[0:48, 2, n * P:(n + 1) * P]), 48)

            mix_part = lambda i: (f_ready, i // 2 + 1)
            dense_group(pe, WO_G, f_hi, f_lo, MIX, mix_part)
            with pe.Fori(1, NB) as j:
                dense_group(pe, WO_G + j, f_hi, f_lo, MIX, mix_part,
                            between=lambda: row_transposes(pe, lambda t: G_END[t] + j - 1, WO_G + j - 1))
            row_transposes(pe, lambda t: G_END[t] + NB - 1, WO_G + NB - 1)
            for m, k in enumerate([3, 0]):
                pe.wait_ge(diag_ready, m + 1)
                pe.wait_ge(g_free[k], G_END[3] if k == 3 else G_END[0] + NB)
                for t in range(NTT):
                    last = nc.tensor.matmul(gbank[k][:, t * TT:(t + 1) * TT], ones[0:TT, :], diag[0:TT, m, t, :],
                                            start=True, stop=True)
                last.then_inc(g_full[k], 1)

            def up(b):
                with pe.Fori(0, NB) as j:
                    dense_group(pe, w1_group(b, j), x_hi, x_lo, OUT, lambda i: (x1_ready[i % 2], i // 2 + 1))

            def down_part(b):
                return lambda i: (f_ready, HEADS + NB * b + i // 2 + 1)

            with pe.Fori(0, LAST_B) as b:
                up(b)
                with pe.Fori(0, NB) as j:
                    dense_group(pe, w2_group(b, j), f_hi, f_lo, MIX, down_part(b))
            up(LAST_B)
            dense_group(pe, w2_group(LAST_B, 0), f_hi, f_lo, MIX, down_part(LAST_B))
            used = [NB + 1, NB, NB]
            with pe.Fori(1, NB) as j:
                dense_group(pe, w2_group(LAST_B, j), f_hi, f_lo, MIX, down_part(LAST_B),
                            between=lambda: row_transposes(pe, lambda t: G_END[t] + used[t] + j - 1,
                                                           w2_group(LAST_B, j - 1)))
            row_transposes(pe, lambda t: G_END[t] + used[t] + NB - 1, END_G)

        @block.scalar
        def _(act):
            act.dma_start(strow[:, :], state_conv[0].rearrange("a b d -> (a b) d")).then_inc(st_landed, 16)

            def normalise_rows(i):
                act.wait_ge(row_scale, i + 1)
                nc.scalar.activation(xrow[:, i, :], xrow[:, i, :], ACT.Identity, bias=nbias[:, i:i + 1],
                                     scale=rstd[:, i:i + 1]).then_inc(row_done, 1)

            normalise_rows(0)
            act.wait_ge(g_full[0], 1)
            nc.scalar.activation(params[:, :], gbank[0][:, 0:P_ALL], ACT.Copy).then_inc(g_free[0], 1)
            normalise_rows(1)
            act.wait_ge(g_full[1], 1)
            nc.scalar.activation(stT[:, :, :], gbank[1][:, 0:16 * KT], ACT.Copy).then_inc(g_free[1], 1)
            act.wait_ge(wa1_landed, 16)
            nc.scalar.activation(wa1_hi[:, :, :], wa1[:, :, 0:RANK], ACT.Copy).then_inc(wa1_split, 1)
            act.wait_ge(g_free[0], 1)
            for k in range(KT):
                n = k % X_BANKS
                act.wait_ge(g_full[n], X_FIRST[n] + k // X_BANKS + 1)
                if k >= HF_SLOTS:
                    act.wait_ge(x_lo_ready[k % 2], (k - HF_SLOTS) // 2 + 1)
                nc.scalar.activation(hf[:, k % HF_SLOTS, :], gbank[n][:, 0:T], ACT.Identity,
                                     bias=params[:, P_INB + k:P_INB + k + 1],
                                     scale=params[:, P_INW + k:P_INW + k + 1]).then_inc(g_free[n], 1)
                if k % NB == NB - 1:
                    split_hi(act, 0, k // NB)
            act.wait_ge(g_full[3], 1)
            nc.scalar.activation(a1T[:, :], gbank[3][0:RANK, 0:T], ACT.Copy).then_inc(g_free[3], 1)

            def evacuate(g, dst, func, scale=1.0):
                for n in range(NB):
                    act.wait_ge(bank_full, banks_full(g, n))
                    nc.scalar.activation(dst(n), bank[n][:, 0:dst(n).shape[-1]], func,
                                         scale=(scale if n < DT else 1.0)).then_inc(bank_free[n], 1)

            def normalise(h, c, k, use, rows, summed=None):
                o = gbank[k] if summed is None else summed
                act.wait_ge(g_full[k], g_filled(h, k, use))
                nc.scalar.activation(junk[0:rows, :], o[0:rows, :], ACT.Square,
                                     accum_out=ss[0:rows, c:c + 1]).then_inc(ss_ready, 1)
                act.wait_ge(rs_ready, 3 * h + c + 1)
                act.wait_ge(g_full[2], g_filled(h, 2, f"s{c}"))
                nc.scalar.activation(vtok[0:rows, c, :], o[0:rows, :], ACT.Copy,
                                     scale=rs[0:rows, c:c + 1]).then_inc(g_free[k], 1)

            def rows_back(h, k, use, w, skip, at):
                act.wait_ge(g_full[k], g_filled(h, k, use))
                for n in range(NB):
                    last = nc.scalar.activation(onT[:, n, at:at + w - skip], gbank[k][:, n * w + skip:(n + 1) * w],
                                                ACT.Copy, scale=params[:, P_GN + n:P_GN + n + 1])
                last.then_inc(g_free[k], 1)

            def exp_level(h, lv):
                act.wait_ge(dist_ready, 7 * h + lv + 1)
                nc.scalar.activation(lev[:, lv, :, :], lev[:, lv, :, :], ACT.Exp, scale=1.0 / 16).then_inc(exp_ready, 1)

            def state_hi(h, i):
                s = i % S0_SLOTS
                act.wait_ge(s0_landed[s], 16 * (len(range(s, NSEQ, S0_SLOTS)) * h + i // S0_SLOTS + 1))
                if i >= 2:
                    act.wait_ge(s_read, NSEQ * h + i - 1)
                nc.scalar.activation(s_hi[:, i % 2, :, :], S0[:, s, :, :], ACT.Copy).then_inc(s_hi_ready, 1)

            def store_state(h, i):
                s = i % S0_SLOTS
                act.wait_ge(g_free[2], g_emptied(h, 2, f"d{i}"))
                act.dma_start(gla_sample[0, i, bass.ds(h, 1), :, :].rearrange("o (d p) v -> p (o d) v", p=P),
                              S0[:, s, :, :]).then_inc(s0_stored[s], 16)

            with act.Fori(0, HEADS) as h:
                for j in range(HG):
                    g = HG * h + j
                    for i in range(SLOTS, UNITS):
                        split_hi(act, g, i, with_k=(h if j == 1 else None))
                        if j in PIECE_SEQS and i in SPLIT_AFTER[:len(PIECE_SEQS[j])]:
                            state_hi(h, PIECE_SEQS[j][SPLIT_AFTER.index(i)])
                        if j == 7 and i == SLOTS + 1:
                            rows_back(h, 0, "o0T", CHUNK, META, 0)
                        if j == 7 and i == SLOTS + 3:
                            rows_back(h, 0, "o1T", CHUNK, 0, CHUNK - META)
                        if j == 1 and i > SLOTS:
                            exp_level(h, i - SLOTS - 1)
                        if j == 3 and i < 7:
                            lv = i - SLOTS
                            act.wait_ge(dist_ready, 7 * h + 4 + lv + 1)
                            nc.scalar.activation(lev[:, lv, :, 0:2 * CHUNK], lev[:, lv, :, 0:2 * CHUNK], ACT.Exp,
                                                 scale=1.0 / 16).then_inc(exp_ready, 1)
                    for i in range(SLOTS - 1):
                        split_hi(act, g + 1, i, with_k=(h if j == 0 else None))
                        if j == 7 and i == 1:
                            act.wait_ge(g_full[0], g_filled(h, 0, "tail"))
                            nc.scalar.activation(tailrow, gbank[0][0:18, :], ACT.Copy).then_inc(g_free[0], 1)
                        if j == 7 and i == 2:
                            act.wait_ge(g_full[3], g_filled(h, 3, "o2"))
                            nc.scalar.activation(o2_low[:, :], gbank[3][Q_LO:QW, :], ACT.Copy).then_inc(o2_low_ready, 1)
                            for seq in PIECE_SEQS[j]:
                                store_state(h, seq)
                            act.wait_ge(o2_sum_ready, h + 1)
                            normalise(h, 2, 3, "o2", 48, o2_sum)
                        if j == 1 and i == 0:
                            exp_level(h, 3)
                        if j == 1 and i == 1:
                            nc.scalar.activation(eb[:, :, :], bT[:, :, :], ACT.Exp, scale=1.0 / 16).then_inc(eb_ready, 1)
                        if j == 1 and i == 2:
                            act.wait_ge(kd_ready, h + 1)
                            nc.scalar.activation(kh[:, :, :], kh[:, :, :], ACT.Exp, scale=1.0 / 16)\
                                .then_inc(kdecay_ready, 1)
                    if j == 0:
                        evacuate(g, lambda n: A[:, n, CONV0:T], ACT.Copy)
                    if j == 1:
                        nc.scalar.activation(QK[:, 0:DT, 0:META], ones[:, 0:DT * META], ACT.Copy, scale=0.0)
                        evacuate(g, lambda n: QK[:, n, META if n < DT else 0:T], ACT.Copy, scale=float(DK) ** -0.5)
                    if j == 2:
                        evacuate(g, lambda n: V[:, n, :], ACT.Copy)
                    if j == 3:
                        evacuate(g, lambda n: B[:, n, CONV0:T], ACT.Copy)
                    if j == 4:
                        act.wait_ge(vst_ready, 3 * h + 3)
                        evacuate(g, lambda n: V[:, n, 0:N], ACT.Copy)
                    if j == 5:
                        act.wait_ge(conv_done, h + 1)
                        act.wait_ge(tails_ready, h + 1)
                        evacuate(g, lambda n: A[:, n, 0:N], ACT.Sigmoid)
                    if j == 6:
                        for n in range(NB):
                            act.wait_ge(bank_full, banks_full(g, n))
                            nc.scalar.activation(Fs[:, n, :], bank[n][:, 0:N], ACT.Sigmoid)
                            nc.scalar.activation(QK[:, n, 0:N], bank[n][:, 0:N], ACT.Copy).then_inc(bank_free[n], 1)
                    if j == 7:
                        act.wait_ge(ga_used, h + 1)
                        evacuate(g, lambda n: A[:, n, 0:N], ACT.Sigmoid)
                    split_hi(act, g + 1, SLOTS - 1, with_k=(h if j == 0 else None))
                    if j == 0:
                        for d in range(DT):
                            act.wait_ge(g_full[d], g_filled(h, d, f"z{d}"))
                            nc.scalar.activation(lev[:, 2, d, :], gbank[d][:, 0:T], ACT.Identity,
                                                 bias=params[:, bass.ds(P_BA + DT * h + d, 1)]).then_inc(g_free[d], 1)
                        act.wait_ge(g_free[1], g_emptied(h, 1, "z1"))
                        nc.scalar.activation(lev[:, 3, :, :], lev[:, 2, :, :], ACT.Abs).then_inc(act_step, 1)
                        act.wait_ge(act_step, 3 * h + 1)
                        nc.scalar.activation(lev[:, 3, :, :], lev[:, 3, :, :], ACT.Exp, scale=-1.0).then_inc(act_step, 1)
                        act.wait_ge(act_step, 3 * h + 2)
                        nc.scalar.activation(lev[:, 3, :, :], lev[:, 3, :, :], ACT.Ln, bias=ones[:, 0:1])\
                            .then_inc(act_step, 1)
                    if j == 2:
                        act.wait_ge(tail_stored, 32 * h + 1)
                        act.wait_ge(g_full[3], g_filled(h, 3, "kT"))
                        nc.scalar.activation(ktok[:, :, :, :], gbank[3][:, :], ACT.Copy).then_inc(g_free[3], 1)
                    if j == 3:
                        for c, w in enumerate([CHUNK, CHUNK, 48]):
                            act.wait_ge(g_full[c], g_filled(h, c, f"v{c}"))
                            nc.scalar.activation(vtok[0:w, c, :], gbank[c][0:w, :], ACT.Copy).then_inc(g_free[c], 1)
                        act.wait_ge(g_full[3], g_filled(h, 3, "vst"))
                        nc.scalar.activation(vstk[:, :], gbank[3][0:96, :], ACT.Copy).then_inc(g_free[3], 1)
                    if j == 4:
                        act.wait_ge(g_full[3], g_filled(h, 3, "kst"))
                        nc.scalar.activation(kstk[:, :, :], gbank[3][0:96, 0:DK], ACT.Copy).then_inc(g_free[3], 1)
                    if j in (5, 6):
                        for i in PIECE_SEQS[j]:
                            store_state(h, i)
                        normalise(h, j - 5, 0, f"o{j - 5}", CHUNK)
                    if j == 7:
                        act.wait_ge(g_free[2], g_emptied(h, 2, "s2"))
                        act.dma_start(gla_prompt[0, 0, bass.ds(h, 1), :, :].rearrange("o (d p) v -> p (o d) v", p=P),
                                      S[:, :, :]).then_inc(S_stored, 16)
                        act.wait_ge(g_free[0], g_emptied(h, 0, "tail"))
                        act.dma_start(conv_prompt[0, 0, :, bass.ds(h * GW, GW)], tailrow[0:2]).then_inc(tail_stored, 16)
                        act.dma_start(conv_sample[0].rearrange("i c d -> (i c) d")[:, bass.ds(h * GW, GW)],
                                      tailrow[2:18]).then_inc(tail_stored, 16)
                        rows_back(h, 3, "o2T", 48, 0, 2 * CHUNK - META)

            def group_splits(g, has_next=True):
                for i in range(SLOTS, UNITS):
                    split_hi(act, g, i)
                if has_next:
                    for i in range(SLOTS - 1):
                        split_hi(act, g + 1, i)

            for k in range(HEADS):
                act.wait_ge(m_ready, HEADS if k == HEADS - 1 else HEADS - 1)
                nc.scalar.activation(f_hi[:, NB * k:NB * (k + 1), :], mix[:, NB * k:NB * (k + 1), :], ACT.Copy)\
                    .then_inc(fhi_ready, 1)
            with act.Fori(0, NB) as j:
                group_splits(WO_G + j)
                split_hi(act, WO_G + j + 1, SLOTS - 1)
            for i in range(UNITS):
                act.wait_ge(norm_ready, i + 1)
                for f in range(UK * i, UK * (i + 1)):
                    last = nc.scalar.activation(mix[:, f, :], mix[:, f, :], ACT.Identity,
                                                bias=params[:, P_LB + f:P_LB + f + 1],
                                                scale=params[:, P_LW + f:P_LW + f + 1])
                last.then_inc(aff_ready, 1)
                act.wait_ge(aff_ready, i + 1)
                kk = slice(UK * i, UK * (i + 1))
                nc.scalar.activation(x_hi[:, kk, META:T], mix[:, kk, :], ACT.Copy).then_inc(x1hi_ready, 1)

            def relu_group(g):
                for n in range(NB):
                    act.wait_ge(bank_full, banks_full(g, n))
                    nc.scalar.activation(pair[:, 0, n, :], bank[n][:, 0:N], ACT.Relu).then_inc(bank_free[n], 1)

            def up(b):
                with act.Fori(0, NB) as j:
                    g = w1_group(b, j)
                    group_splits(g)
                    act.wait_ge(sq2_ready, NB * b + j + 1)
                    relu_group(g)
                    split_hi(act, g + 1, SLOTS - 1)

            with act.Fori(0, LAST_B) as b:
                up(b)
                with act.Fori(0, NB) as j:
                    group_splits(w2_group(b, j))
                    split_hi(act, w2_group(b, j) + 1, SLOTS - 1)
            up(LAST_B)

            def rows_out(first, m):
                for t in range(NTT):
                    act.wait_ge(g_full[t], first(t))
                    nc.scalar.activation(yrow[0:TT, t, bass.ds(m * GW, GW)], gbank[t][0:TT, :], ACT.Copy)\
                        .then_inc(yrow_copied, 1)

            used = [NB + 1, NB, NB]
            full0 = [G_END[t] + used[t] for t in range(NTT)]
            group_splits(w2_group(LAST_B, 0))
            split_hi(act, w2_group(LAST_B, 1), SLOTS - 1)
            with act.Fori(1, NB - 1) as j:
                g = w2_group(LAST_B, j)
                for i in range(SLOTS, UNITS):
                    split_hi(act, g, i)
                rows_out(lambda t: full0[t] + j, j - 1)
                for i in range(SLOTS):
                    split_hi(act, g + 1, i)
            for i in range(SLOTS, UNITS):
                split_hi(act, END_G, i)
            rows_out(lambda t: full0[t] + NB - 1, NB - 2)
            rows_out(lambda t: full0[t] + NB, NB - 1)
            act.wait_ge(nbias_ready, 1)
            t, c = POOL_PIECE
            nc.scalar.activation(yrow[0:TT, t, c], yrow[0:TT, t, c], ACT.Identity,
                                 bias=nbias[0:TT, t:t + 1], scale=rstd[0:TT, t:t + 1]).then_inc(yn_ready, 1)

        @block.vector
        def _(dve):
            dve.sem_inc(lo_ready, SLOTS)
            for n in range(NB):
                dve.sem_inc(bank_free[n], 1)
            nc.vector.memset(carry[:, :], 1.0).then_inc(dve_step, 1)
            dve.wait_ge(dve_step, 1)
            for c in (0, CHUNK, 2 * CHUNK):
                nc.vector.memset(carry[:, c:c + 1], 0.0)
            nc.vector.memset(carry[:, PROMPT:T:DSEQ], 0.0)
            nc.vector.memset(q_parts[:, :, :, :].bitcast(F32), 0.0)
            nc.vector.memset(q_dec[:, :], 0.0).then_inc(const_ready, 1)

            for i, rows in enumerate([P, P, T - 2 * P]):
                dve.wait_ge(x_landed[i], 16 if i == 1 else 32)
                for q in range(4):
                    last = nc.vector.bn_stats(stats_in[0:rows, i, q, :], xrow[0:rows, i, q * 512:(q + 1) * 512])
                last.then_inc(dve_step, 1)
                dve.wait_ge(dve_step, 2 * i + 2)
                nc.vector.bn_aggr(mv[0:rows, i, :], stats_in[0:rows, i, :, :].rearrange("p q s -> p (q s)"))\
                    .then_inc(dve_step, 1)
                dve.wait_ge(dve_step, 2 * i + 3)
                nc.vector.tensor_scalar(var[0:rows, i:i + 1], mv[0:rows, i, 1:2], EPS, None, ALU.add)
                nc.vector.tensor_scalar(neg_mean[0:rows, i:i + 1], mv[0:rows, i, 0:1], -1.0, None, ALU.mult)\
                    .then_inc(row_stats, 1)
            dve.wait_ge(row_pow, 3)
            x, i = xrow[0:T - 2 * P, 2, :], 2
            nc.vector.tensor_scalar(x, x, mv[0:T - 2 * P, i, 0:1], rstd[0:T - 2 * P, i:i + 1], ALU.subtract, ALU.mult)\
                .then_inc(last_rows_done, 1)
            for k in range(KT):
                n = k % X_BANKS
                dve.wait_ge(g_free[n], X_FIRST[n] + k // X_BANKS + 1)
                nc.vector.tensor_copy(x_hi[:, k, :], hf[:, k % HF_SLOTS, :]).then_inc(x_hi_ready, 1)
                if k % 2 == 0:
                    dve.wait_ge(x_hi_ready, k + 1)
                    nc.vector.tensor_tensor(x_lo[:, k, :], hf[:, k % HF_SLOTS, :], x_hi[:, k, :].bitcast(F32),
                                            ALU.subtract).then_inc(x_lo_ready[0], 1)
                if k == 0:
                    dve.wait_ge(wa1_split, 1)
                    nc.vector.tensor_tensor(wa1_lo[:, :, :], wa1[:, :, 0:RANK], wa1_hi[:, :, :].bitcast(F32),
                                            ALU.subtract).then_inc(wa1_split, 1)
            for i in range(SLOTS):
                split_lo(dve, 0, i)
            dve.wait_ge(g_free[3], 1)

            def halves(ap, lo, hi, L):
                return ap[:, :, lo:hi].rearrange("p d (b l) -> p d b l", l=2 * L)

            def distance(h, lv, L, hi):
                out, b = halves(lev[:, lv % 4, :, :], 0, hi, L), halves(bT, 0, hi, L)
                nb = hi // (2 * L)
                ref = b[:, :, :, L - 1:L].to_broadcast([P, DT, nb, 2 * L])
                nc.vector.tensor_tensor(out, b, ref, ALU.subtract).then_inc(dve_step, 1)

            def negative(lv, hi):
                x = lev[:, lv, :, 0:hi]
                return nc.vector.scalar_tensor_tensor(out=x, in0=x, scalar=-1.0, in1=x, op0=ALU.mult, op1=ALU.min)

            def levels_evac(h, k, use, w, n, msk, first):
                if not first or k > 0:
                    dve.wait_ge(sc1_ready, 5 * h + k + (0 if first else 3))
                dve.wait_ge(g_full[k], g_filled(h, k, use))
                pr = prod[0:w, :, :].rearrange("p a b -> p (a b)")[:, 0:n * w].rearrange("p (a b) -> p a b", b=w)
                nc.vector.tensor_tensor(pr, gbank[k][0:w, 0:n * w].rearrange("p (a b) -> p a b", b=w), msk, ALU.mult)\
                    .then_inc(g_free[k], 1)
                c = k
                dst = att[0:w, c, 0:w] if first else tmpA[0:w, 0:w]
                dve.wait_ge(g_free[k], g_emptied(h, k, use))
                nc.vector.tensor_reduce(out=dst, in_=pr.rearrange("p a b -> p b a"), axis=AX_X, op=ALU.add)\
                    .then_inc(sc1_ready, 1)
                if not first:
                    dve.wait_ge(sc1_ready, 5 * h + 3 + c + 1)
                    nc.vector.tensor_tensor(att[0:w, c, 0:w], att[0:w, c, 0:w], tmpA[0:w, 0:w], ALU.add)\
                        .then_inc(att_ready, 1)

            def state_lo(h, i):
                dve.wait_ge(s_hi_ready, NSEQ * h + i + 1)
                nc.vector.tensor_tensor(s_lo[:, i % 2, :, :], S0[:, i % S0_SLOTS, :, :],
                                        s_hi[:, i % 2, :, :].bitcast(F32), ALU.subtract).then_inc(s_lo_ready, 1)

            def seq_state(h, i):
                s = i % S0_SLOTS
                for d in range(DT):
                    dve.wait_ge(g_full[1 + d], g_filled(h, 1 + d, f"d{i}"))
                    nc.vector.scalar_tensor_tensor(out=S0[:, s, d, :], in0=S0[:, s, d, :],
                                                   scalar=ebl[:, d, 3 + i:4 + i], in1=gbank[1 + d][:, :],
                                                   op0=ALU.mult, op1=ALU.add).then_inc(g_free[1 + d], 1)

            def prompt_state(h, c):
                for d in range(DT):
                    dve.wait_ge(g_full[1 + d], g_filled(h, 1 + d, f"s{c}"))
                    if c == 0:
                        if d == 0:
                            dve.wait_ge(S_stored, 16 * h + 1)
                        nc.vector.tensor_copy(S[:, d, :], gbank[1 + d][:, :]).then_inc(g_free[1 + d], 1)
                    else:
                        nc.vector.scalar_tensor_tensor(out=S[:, d, :], in0=S[:, d, :], scalar=ebl[:, d, c:c + 1],
                                                       in1=gbank[1 + d][:, :], op0=ALU.mult, op1=ALU.add)\
                            .then_inc(g_free[1 + d], 1)

            STEP0 = 7
            HS = 7 + 2 * NB + 4

            with dve.Fori(0, HEADS) as h:
                step = [0]

                def link(ins):
                    ins.then_inc(dve_step, 1)
                    step[0] += 1
                    dve.wait_ge(dve_step, STEP0 + HS * h + step[0])

                for j in range(HG):
                    g = HG * h + j
                    for i in range(SLOTS, UNITS):
                        split_lo(dve, g, i)
                        if j in PIECE_SEQS and i in SPLIT_AFTER[:len(PIECE_SEQS[j])]:
                            state_lo(h, PIECE_SEQS[j][SPLIT_AFTER.index(i)])
                        if j in PIECE_SEQS and i == UPDATE_AFTER[0]:
                            seq_state(h, PIECE_SEQS[j][0])
                        if j == 1:
                            lv = i - SLOTS
                            distance(h, lv, LEVELS[lv], T)
                            step[0] += 1
                            dve.wait_ge(dve_step, STEP0 + HS * h + step[0])
                            negative(lv, T).then_inc(dist_ready, 1)
                        if j == 3 and i < 7:
                            lv = 4 + i - SLOTS
                            if i == SLOTS:
                                dve.wait_ge(g_full[3], g_filled(h, 3, "kT"))
                            distance(h, lv, LEVELS[lv], 2 * CHUNK)
                            step[0] += 1
                            dve.wait_ge(dve_step, STEP0 + HS * h + step[0])
                            negative(lv - 4, 2 * CHUNK).then_inc(dist_ready, 1)
                        if j == 4 and i == SLOTS:
                            dve.wait_ge(bank_free[NB - 1], bank_frees(g - 1))
                            nc.vector.tensor_tensor(A[:, :, CONV0:T], A[:, :, CONV0:T], B[:, :, CONV0:T], ALU.mult)\
                                .then_inc(u_ready, 1)
                        if j == 4 and i > SLOTS:
                            if i == SLOTS + 1:
                                dve.wait_ge(u_ready, h + 1)
                                dve.wait_ge(uD_ready, 2 * h + 2)
                            for n in ([0], [1, 2], [3])[i - SLOTS - 1]:
                                for t in range(CW):
                                    w = params[:, bass.ds(P_CW + KT * t + NB * h + n, 1)]
                                    off = CONV0 + t
                                    y, yd = B[:, n, 0:SEQ], B[:, n, SEQ:N].rearrange("p (i t) -> p i t", t=DSEQ)
                                    u, ud = A[:, n, off:off + SEQ], uD[:, n, :, t:t + DSEQ]
                                    if t == 0:
                                        nc.vector.tensor_scalar(y, u, w, None, ALU.mult)
                                        last = nc.vector.tensor_scalar(yd, ud, w, None, ALU.mult)
                                    else:
                                        nc.vector.scalar_tensor_tensor(out=y, in0=u, scalar=w, in1=y,
                                                                       op0=ALU.mult, op1=ALU.add)
                                        last = nc.vector.scalar_tensor_tensor(out=yd, in0=ud, scalar=w, in1=yd,
                                                                              op0=ALU.mult, op1=ALU.add)
                                    if t < CW - 1:
                                        link(last)
                                    elif n == NB - 1:
                                        last.then_inc(conv_done, 1)
                        if j == 5 and i == SLOTS:
                            dve.wait_ge(bank_free[NB - 1], bank_frees(g - 1))
                            dve.wait_ge(conv_done, h + 1)
                            nc.vector.tensor_tensor(B[:, :, 0:N], B[:, :, 0:N], V[:, :, 0:N], ALU.mult)\
                                .then_inc(cb_used, 1)
                        if j == 6 and i == SLOTS:
                            dve.wait_ge(bank_free[NB - 1], bank_frees(g - 1))
                            dve.wait_ge(cb_used, h + 1)
                            nc.vector.tensor_tensor(B[:, :, 0:N], B[:, :, 0:N], A[:, :, 0:N], ALU.mult)\
                                .then_inc(ga_used, 1)
                    for i in range(SLOTS):
                        split_lo(dve, g + 1, i)
                        if j == 7 and i == 2:
                            dve.wait_ge(o2_low_ready, h + 1)
                            nc.vector.tensor_tensor(o2_sum[:, :], gbank[3][0:48, :], o2_low[:, :], ALU.add)\
                                .then_inc(o2_sum_ready, 1)
                            prompt_state(h, 2)
                        if j in PIECE_SEQS and UNITS + i in UPDATE_AFTER[:len(PIECE_SEQS[j])]:
                            seq_state(h, PIECE_SEQS[j][UPDATE_AFTER.index(UNITS + i)])
                        if j == 1 and i == 0:
                            b0, k0 = bT[:, :, 0:2 * CHUNK], kh[:, :, 0:2 * CHUNK]
                            v = b0.rearrange("p d (c t) -> p d c t", t=CHUNK)
                            nc.vector.tensor_tensor(k0.rearrange("p d (c t) -> p d c t", t=CHUNK),
                                                    v[:, :, :, CHUNK - 1:CHUNK].to_broadcast([P, DT, 2, CHUNK]), v,
                                                    ALU.subtract)
                            v = bT[:, :, 2 * CHUNK:PROMPT]
                            nc.vector.tensor_tensor(kh[:, :, 2 * CHUNK:PROMPT],
                                                    v[:, :, META - 1:META].to_broadcast([P, DT, META]), v, ALU.subtract)
                            v = bT[:, :, PROMPT:T].rearrange("p d (c t) -> p d c t", t=DSEQ)
                            nc.vector.tensor_tensor(kh[:, :, PROMPT:T].rearrange("p d (c t) -> p d c t", t=DSEQ),
                                                    v[:, :, :, DSEQ - 1:DSEQ].to_broadcast([P, DT, NSEQ, DSEQ]), v,
                                                    ALU.subtract).then_inc(kd_ready, 1)
                    if j == 0:
                        dve.wait_ge(act_step, 3 * h + 3)
                        link(nc.vector.scalar_tensor_tensor(out=lev[:, 2, :, :], in0=lev[:, 2, :, :], scalar=0.0,
                                                            in1=lev[:, 3, :, :], op0=ALU.min, op1=ALU.subtract))
                        for d in range(DT):
                            last = nc.vector.tensor_tensor_scan(bT[:, d, :], carry[:, :], lev[:, 2, d, :],
                                                                0.0, ALU.mult, ALU.add)
                        last.then_inc(b_ready, 1)
                        dve.wait_ge(b_ready, h + 1)
                    if j == 2:
                        dve.wait_ge(masks_ready, 1)
                        for c in range(2):
                            levels_evac(h, c, f"lev_a{c}", CHUNK, 4, mask[:, 0:4, :], True)
                        levels_evac(h, 2, "lev_a2", 48, 4, mask2[0:48, 0:4, :], True)
                    if j == 4:
                        for c in range(2):
                            levels_evac(h, c, f"lev_b{c}", CHUNK, 4, mask[:, 4:8, :], False)
                        dve.wait_ge(g_full[2], g_filled(h, 2, "lev_b2"))
                        dve.wait_ge(att_ready, 3 * h + 2)
                        link(nc.vector.tensor_tensor(tmpA[0:48, 0:48], gbank[2][0:48, 0:48], mask2[0:48, 4, :], ALU.mult))
                        nc.vector.tensor_tensor(att[0:48, 2, 0:48], att[0:48, 2, 0:48], tmpA[0:48, 0:48], ALU.add)\
                            .then_inc(att_ready, 1)
                        nc.vector.tensor_copy(kt2[:, :, :], gbank[2][0:16, P:P + DK]).then_inc(g_free[2], 1)
                    if j in (5, 6):
                        prompt_state(h, j - 5)
                    if j == 7:
                        dve.wait_ge(silu_ready, h + 1)
                        dve.wait_ge(bank_free[NB - 1], bank_frees(g))
                        nc.vector.tensor_tensor(QK[:, :, 0:N], QK[:, :, 0:N], A[:, :, 0:N], ALU.mult)\
                            .then_inc(gated_ready, 1)
                        for a, e, of, k in ((0, EARLY, "o1T", 0), (EARLY, N, "o2T", 3)):
                            dve.wait_ge(g_free[k], g_emptied(h, k, of))
                            if a == 0:
                                dve.wait_ge(gated_ready, h + 1)
                            link(nc.vector.tensor_tensor(onT[:, :, a:e], onT[:, :, a:e], QK[:, :, a:e], ALU.mult))
                            last = nc.vector.tensor_tensor(mix[:, bass.ds(NB * h, NB), a:e], onT[:, :, a:e],
                                                           B[:, :, a:e], ALU.add)
                        last.then_inc(m_ready, 1)
                assert step[0] == HS

            for k in range(HEADS):
                dve.wait_ge(fhi_ready, k + 1)
                kk = slice(NB * k, NB * (k + 1))
                if k == HEADS - 1:
                    dve.wait_ge(tail_stored, 1 + 32 * HEADS)
                nc.vector.tensor_tensor(f_lo[:, kk, :], mix[:, kk, :], f_hi[:, kk, :].bitcast(F32), ALU.subtract)\
                    .then_inc(f_ready, 1)

            def group_splits(g, has_next=True):
                for i in range(SLOTS, UNITS):
                    split_lo(dve, g, i)
                if has_next:
                    for i in range(SLOTS):
                        split_lo(dve, g + 1, i)

            def row_stats_of(m, first, copied=None):
                for t in range(NTT):
                    dve.wait_ge(g_full[t], first(t))
                    if copied is not None:
                        dve.wait_ge(yrow_copied, copied + t + 1)
                    nc.vector.bn_stats(stats[0:TT, t, bass.ds(m, 1), :], gbank[t][0:TT, :]).then_inc(g_free[t], 1)

            AFTER = STEP0 + HS * HEADS

            def residual(j):
                for n in range(NB):
                    dve.wait_ge(bank_full, banks_full(WO_G + j, n))
                    nc.vector.scalar_tensor_tensor(out=stage[:, n, :], in0=stage[:, n, :], scalar=ALPHA,
                                                   in1=bank[n][:, 0:N], op0=ALU.mult, op1=ALU.add)\
                        .then_inc(bank_free[n], 1)

            def stage_x(j):
                f = bass.ds(NB * j, NB)
                nc.vector.tensor_tensor(stage[:, :, :], x_hi[:, f, META:T].bitcast(F32), x_lo[:, f, META:T].bitcast(F32),
                                        ALU.add).then_inc(x_staged, 1)

            full1 = [G_END[t] for t in range(NTT)]
            for i in range(SLOTS, UNITS):
                split_lo(dve, WO_G, i)
            for i in range(SLOTS - 1):
                split_lo(dve, WO_G + 1, i)
            stage_x(0)
            dve.wait_ge(x_staged, 1)
            residual(0)
            with dve.Fori(1, NB) as j:
                for i in range(SLOTS - 1, UNITS):
                    split_lo(dve, WO_G + j, i)
                row_stats_of(j - 1, lambda t: full1[t] + j)
                dve.wait_ge(stage_copied, j)
                stage_x(j)
                for i in range(SLOTS - 1):
                    split_lo(dve, WO_G + j + 1, i)
                dve.wait_ge(x_staged, j + 1)
                residual(j)
            row_stats_of(NB - 1, lambda t: full1[t] + NB)

            n_link = [0]

            def chain(ins):
                ins.then_inc(dve_step, 1)
                n_link[0] += 1
                dve.wait_ge(dve_step, AFTER + n_link[0])

            def aggregate(n_th, free_count):
                for t in range(NTT):
                    dve.wait_ge(g_free[t], free_count(t))
                    last = nc.vector.bn_aggr(mv[0:TT, t, :], stats[0:TT, t, :, :].rearrange("p q s -> p (q s)"))
                chain(last)
                nc.vector.tensor_scalar(var[0:TT, :], mv[0:TT, :, 1], EPS, None, ALU.add).then_inc(row_stats, 1)

            aggregate(1, lambda t: G_END[t] + NB)
            for t in range(NTT):
                last = nc.vector.tensor_scalar(diag[0:TT, 0, t, :], ident[0:TT, 0:TT], mv[0:TT, t, 0:1], None, ALU.mult)
            last.then_inc(diag_ready, 1)
            split_lo(dve, FF_G, SLOTS - 1)
            dve.wait_ge(row_scale, 3)
            for t in range(NTT):
                last = nc.vector.tensor_scalar(diag[0:TT, 1, t, :], ident[0:TT, 0:TT], rstd[0:TT, t:t + 1], None, ALU.mult)
            last.then_inc(diag_ready, 1)
            dve.wait_ge(g_full[3], G_END[3] + 1)
            dve.wait_ge(g_full[0], G_END[0] + NB + 1)

            def normalise(i):
                dve.wait_ge(stage_copied, max(UK * i // NB + 1, NB - 1))
                x = mix[:, UK * i:UK * (i + 1), :]
                chain(nc.vector.tensor_tensor(x, x, gbank[3][:, None, 0:N].to_broadcast([P, UK, N]), ALU.subtract))
                nc.vector.tensor_tensor(x, x, gbank[0][:, None, 0:N].to_broadcast([P, UK, N]), ALU.mult)\
                    .then_inc(norm_ready, 1)

            normalise(0)
            normalise(1)
            for i in range(UNITS):
                if i % 2 == 0:
                    split_x1(dve, nc.vector, i)
                if i + 2 < UNITS:
                    normalise(i + 2)
            dve.sem_inc(g_free[0], 1)
            dve.sem_inc(sq2_ready, 1)

            def up(b):
                with dve.Fori(0, NB) as j:
                    g = w1_group(b, j)
                    group_splits(g)
                    dve.wait_ge(bank_free[NB - 1], bank_frees(g))
                    dve.wait_ge(f_ready, HEADS + NB * b + j)
                    nc.vector.tensor_tensor(pair[:, 1, :, :], pair[:, 0, :, :], pair[:, 0, :, :], ALU.mult)\
                        .then_inc(sq2_ready, 1)

            with dve.Fori(0, LAST_B) as b:
                up(b)
                dve.wait_ge(acc_ready, NB)
                with dve.Fori(0, NB) as j:
                    g = w2_group(b, j)
                    for i in range(SLOTS, UNITS):
                        split_lo(dve, g, i)
                    for i in range(SLOTS - 1):
                        split_lo(dve, g + 1, i)
                    for n in range(NB):
                        dve.wait_ge(bank_full, banks_full(g, n))
                        acc = mix[:, bass.ds(NB * j + n, 1), :]
                        nc.vector.tensor_tensor(acc, acc, bank[n][:, 0:N], ALU.add).then_inc(bank_free[n], 1)
                    split_lo(dve, g + 1, SLOTS - 1)
            up(LAST_B)

            def last_sum(j):
                for n in range(NB):
                    dve.wait_ge(bank_full, banks_full(w2_group(LAST_B, j), n))
                    nc.vector.tensor_tensor(stage[:, n, :], mix[:, bass.ds(NB * j + n, 1), :], bank[n][:, 0:N],
                                            ALU.add).then_inc(bank_free[n], 1)

            used = [NB + 1, NB, NB]
            full2 = [G_END[t] + used[t] for t in range(NTT)]
            g0 = w2_group(LAST_B, 0)
            for i in range(SLOTS, UNITS):
                split_lo(dve, g0, i)
            for i in range(SLOTS - 1):
                split_lo(dve, g0 + 1, i)
            last_sum(0)
            split_lo(dve, g0 + 1, SLOTS - 1)
            with dve.Fori(1, NB - 1) as j:
                for i in range(SLOTS, UNITS):
                    split_lo(dve, g0 + j, i)
                row_stats_of(j - 1, lambda t: full2[t] + j, NTT * (j - 1))
                for i in range(SLOTS - 1):
                    split_lo(dve, g0 + j + 1, i)
                last_sum(j)
                split_lo(dve, g0 + j + 1, SLOTS - 1)
            for i in range(SLOTS, UNITS):
                split_lo(dve, END_G, i)
            row_stats_of(NB - 2, lambda t: full2[t] + NB - 1, NTT * (NB - 2))
            last_sum(NB - 1)
            row_stats_of(NB - 1, lambda t: full2[t] + NB, NTT * (NB - 1))
            aggregate(2, lambda t: full2[t] + NB)
            dve.wait_ge(lnrow_landed, 32)
            for m, (t, c) in enumerate(DVE_PIECES):
                x = yrow[0:TT, t, c]
                nc.vector.scalar_tensor_tensor(out=x, in0=x, scalar=mv[0:TT, t, 0:1], in1=ln_w_row[0:TT, c],
                                               op0=ALU.subtract, op1=ALU.mult).then_inc(yw_ready, 1)
                if m == 0:
                    dve.wait_ge(row_scale, 4)
                dve.wait_ge(yw_ready, m + 1)
                nc.vector.scalar_tensor_tensor(out=x, in0=x, scalar=rstd[0:TT, t:t + 1], in1=ln_b_row[0:TT, c],
                                               op0=ALU.mult, op1=ALU.add).then_inc(yb_ready, 1)

        @block.gpsimd
        def _(pool):
            pstep = [0]

            def seq(ins):
                ins.then_inc(pool_seq, 1)
                pstep[0] += 1
                pool.wait_ge(pool_seq, pstep[0])

            seq(nc.gpsimd.memset(ident[:, :], 0.0))
            nc.gpsimd.affine_select(out=ident[:, :], in_=ident[:, :], compare_op=ALU.not_equal, fill=1.0, base=0,
                                    pattern=[[-1, P]], channel_multiplier=1).then_inc(ident_ready, 1)
            nc.gpsimd.memset(ones[:, :], 1.0)
            seq(nc.gpsimd.memset(minus_half[:, :], -0.5))
            for i, rows in enumerate([P, P, T - 2 * P]):
                pool.wait_ge(row_stats, i + 1)
                nc.gpsimd.tensor_tensor(rstd[0:rows, i:i + 1], var[0:rows, i:i + 1], minus_half[0:rows, 0:1], ALU.pow)\
                    .then_inc(row_pow, 1)
                if i < 2:
                    pool.wait_ge(row_pow, i + 1)
                    nc.gpsimd.tensor_tensor(nbias[0:rows, i:i + 1], neg_mean[0:rows, i:i + 1], rstd[0:rows, i:i + 1],
                                            ALU.mult).then_inc(row_scale, 1)
            for started in (*s0_stored, S_stored, tail_stored):
                pool.sem_inc(started, 1)
            for k in range(1, KT, 2):
                pool.wait_ge(x_hi_ready, k + 1)
                nc.gpsimd.tensor_tensor(x_lo[:, k, :], hf[:, k % HF_SLOTS, :], x_hi[:, k, :].bitcast(F32), ALU.subtract)\
                    .then_inc(x_lo_ready[1], 1)
            seq(nc.gpsimd.memset(mask[:, :, :], 0.0))
            nc.gpsimd.affine_select(out=mask[:, 0, :], in_=mask[:, 0, :], compare_op=ALU.not_equal, fill=1.0, base=0,
                                    pattern=[[-1, P]], channel_multiplier=1)
            rights = []
            for m, L in enumerate(LEVELS):
                right = mask[:, m + 1, :].rearrange("p (b l) -> p b l", l=2 * L)[:, :, L:2 * L]
                rights.append(right)
                last = nc.gpsimd.memset(right, 1.0)
            seq(last)
            for m, L in enumerate(LEVELS):
                last = nc.gpsimd.affine_select(out=rights[m], in_=rights[m], compare_op=ALU.is_ge, fill=0.0, base=0,
                                               pattern=[[-2 * L, P // (2 * L)], [0, L]], channel_multiplier=1)
            seq(last)
            for m, L in enumerate(LEVELS):
                last = nc.gpsimd.affine_select(out=rights[m], in_=rights[m], compare_op=ALU.is_ge, fill=0.0, base=L - 1,
                                               pattern=[[2 * L, P // (2 * L)], [0, L]], channel_multiplier=-1)
            seq(last)
            seq(nc.gpsimd.tensor_copy(mask2[0:48, :, :], mask[0:48, 0:5, 0:48]))
            nc.gpsimd.memset(mask2[0:48, 3:5, META:48], 0.0)
            groups = [segmask[32 * q:32 * q + 32, :] for q in range(3)]
            seq(nc.gpsimd.memset(segmask[:, :], 1.0))
            for rows in groups:
                last = nc.gpsimd.affine_select(out=rows, in_=rows, compare_op=ALU.is_ge, fill=0.0, base=0,
                                               pattern=[[-DSEQ, NSEQ]], channel_multiplier=1)
            seq(last)
            for rows in groups:
                last = nc.gpsimd.affine_select(out=rows, in_=rows, compare_op=ALU.is_ge, fill=0.0, base=DSEQ - 1,
                                               pattern=[[DSEQ, NSEQ]], channel_multiplier=-1)
            last.then_inc(masks_ready, 1)
            pool.wait_ge(masks_ready, 1)
            pool.wait_ge(const_ready, 1)
            pool.wait_ge(g_free[3], 1)

            def load_state(h, i):
                s = i % S0_SLOTS
                per = len(range(s, NSEQ, S0_SLOTS))
                pool.wait_ge(s0_stored[s], 16 * (per * h + i // S0_SLOTS) + 1)
                pool.dma_start(S0[:, s, :, :], state_gla[0, i, bass.ds(h, 1), :, :]
                               .rearrange("o (d p) v -> p (o d) v", p=P)).then_inc(s0_landed[s], 16)

            def select_keys(h, i):
                if i >= 2:
                    pool.wait_ge(g_full[2], g_filled(h, 2, f"d{i - 2}"))
                    alone(pool)
                nc.gpsimd.tensor_scalar(kms[:, i % 2, :, :], kstk[:, :, :], segmask[0:96, i:i + 1], None, ALU.mult)\
                    .then_inc(kms_ready, 1)

            def deviation(h, c, rows):
                pool.wait_ge(ss_ready, 3 * h + c + 1)
                alone(pool)
                nc.gpsimd.tensor_scalar(ms[0:rows, c:c + 1], ss[0:rows, c:c + 1], 1.0 / DV, EPS, ALU.mult, ALU.add)\
                    .then_inc(ms_ready, 1)
                pool.wait_ge(ms_ready, 3 * h + c + 1)
                nc.gpsimd.tensor_tensor(rs[0:rows, c:c + 1], ms[0:rows, c:c + 1], minus_half[0:rows, 0:1], ALU.pow)\
                    .then_inc(rs_ready, 1)

            with pool.Fori(0, HEADS) as h:
                pool.dma_start(wa2h[:, :], w_a2[0, :, bass.ds(h * DK, DK)]).then_inc(wa2h_landed, 16)
                for i in range(S0_SLOTS):
                    load_state(h, i)
                pool.wait_ge(eb_ready, h + 1)
                alone(pool)
                nc.gpsimd.tensor_copy(ebl[:, :, 0:2], eb[:, :, CHUNK - 1:2 * CHUNK:CHUNK])
                nc.gpsimd.tensor_copy(ebl[:, :, 2:11], eb[:, :, PROMPT - 1:T:DSEQ]).then_inc(ebl_ready, 1)
                pool.wait_ge(bank_free[NB - 1], bank_frees(HG * h + 1))

                def decay(lv, hi):
                    L = LEVELS[lv]
                    pool.wait_ge(exp_ready, 7 * h + lv + 1)
                    for d in range(DT):
                        x = lev[:, lv % 4, d, 0:hi].rearrange("p (b l) -> p b l", l=2 * L)
                        q = QK[:, d, 0:hi].rearrange("p (b l) -> p b l", l=2 * L)
                        k = QK[:, DT + d, 0:hi].rearrange("p (b l) -> p b l", l=2 * L)
                        nc.gpsimd.tensor_tensor(x[:, :, 0:L], x[:, :, 0:L], k[:, :, 0:L], ALU.mult)
                        last = nc.gpsimd.tensor_tensor(x[:, :, L:2 * L], x[:, :, L:2 * L], q[:, :, L:2 * L], ALU.mult)
                    last.then_inc(lev_ready, 1)

                for lv in range(3):
                    decay(lv, T)
                pool.wait_ge(kdecay_ready, h + 1)
                nc.gpsimd.tensor_tensor(kh[:, :, :], kh[:, :, :], QK[:, DT:2 * DT, :], ALU.mult).then_inc(qk_pool, 1)
                nc.gpsimd.tensor_tensor(qh[:, :, :], QK[:, 0:DT, CHUNK:2 * CHUNK], eb[:, :, CHUNK:2 * CHUNK], ALU.mult)\
                    .then_inc(qk_pool, 1)
                nc.gpsimd.tensor_tensor(q_dec[:, 0:DT * 48].rearrange("p (d c) -> p d c", c=48)[:, :, 0:META],
                                        QK[:, 0:DT, 2 * CHUNK:PROMPT],
                                        eb[:, :, 2 * CHUNK:PROMPT], ALU.mult).then_inc(qk_pool, 1)
                q = tmpA[:, 0:DT * DEC].rearrange("p (d t) -> p d t", t=DEC)
                nc.gpsimd.tensor_tensor(q, QK[:, 0:DT, PROMPT:T], eb[:, :, PROMPT:T], ALU.mult).then_inc(q_step, 1)
                pool.wait_ge(q_step, 2 * h + 1)
                alone(pool)
                m = NSEQ - 1

                def columns(d, at):
                    flat, step = q_parts[:, d, :, :].rearrange("p a b -> p (a b)"), QW + DSEQ
                    first, end = at + META, at + META + m * step
                    return (flat[:, first:end].rearrange("p (i c) -> p i c", c=step)[:, :, 0:DSEQ],
                            flat[:, end:end + DSEQ].rearrange("p (i c) -> p i c", c=DSEQ))

                pieces = []
                for d in range(DT):
                    qs = q[:, d, :].rearrange("p (i c) -> p i c", c=DSEQ)
                    pieces += zip((qs[:, 0:m, :], qs[:, m:NSEQ, :]), columns(d, 0), columns(d, Q_LO))
                for x, hi, lo in pieces:
                    last = nc.gpsimd.tensor_copy(hi, x)
                last.then_inc(q_step, 1)
                pool.wait_ge(q_step, 2 * h + 2)
                for x, hi, lo in pieces:
                    last = nc.gpsimd.tensor_tensor(lo, x, hi.bitcast(F32), ALU.subtract)
                last.then_inc(qk_pool, 1)
                decay(3, T)
                pool.wait_ge(qk_pool, 5 * h + 1)
                alone(pool)
                nc.gpsimd.tensor_copy(kst[:, :, 0:DEC], kh[:, :, PROMPT:T])
                nc.gpsimd.tensor_copy(kst[:, :, 2 * DEC:3 * DEC], kh[:, :, PROMPT:T]).then_inc(pool_head, 1)
                pool.wait_ge(pool_head, h + 1)
                nc.gpsimd.tensor_tensor(kst[:, :, DEC:2 * DEC], kh[:, :, PROMPT:T], kst[:, :, 0:DEC].bitcast(F32),
                                        ALU.subtract).then_inc(qk_pool, 1)
                pool.wait_ge(bank_free[NB - 1], bank_frees(HG * h + 2))
                alone(pool)
                nc.gpsimd.tensor_copy(vst[:, :, 0:DEC], V[:, :, PROMPT:T]).then_inc(vst_ready, 1)
                nc.gpsimd.tensor_copy(vst[:, :, DEC:2 * DEC], V[:, :, PROMPT:T]).then_inc(vst_ready, 1)
                pool.wait_ge(vst_ready, 3 * h + 2)
                nc.gpsimd.tensor_tensor(vst[:, :, 2 * DEC:3 * DEC], V[:, :, PROMPT:T], vst[:, :, 0:DEC].bitcast(F32),
                                        ALU.subtract).then_inc(vst_ready, 1)
                for lv in (4, 5, 6):
                    decay(lv, 2 * CHUNK)
                nc.gpsimd.tensor_copy(uD[:, :, :, 0:2], stT[:, bass.ds(NB * h, NB), :]
                                      .rearrange("p n (i c) -> p n i c", c=2)).then_inc(uD_ready, 1)
                pool.wait_ge(u_ready, h + 1)
                alone(pool)
                nc.gpsimd.tensor_copy(uD[:, :, :, 2:6], A[:, :, PROMPT:T].rearrange("p n (i c) -> p n i c", c=DSEQ))\
                    .then_inc(uD_ready, 1)
                nc.gpsimd.tensor_copy(tails[:, :, 0:2], A[:, :, PROMPT - 2:PROMPT])
                nc.gpsimd.tensor_copy(tails[:, :, 2:18].rearrange("p n (i c) -> p n i c", c=2),
                                      A[:, :, PROMPT:T].rearrange("p n (i c) -> p n i c", c=DSEQ)[:, :, :, 2:4])\
                    .then_inc(tails_ready, 1)
                pool.wait_ge(g_free[3], g_emptied(h, 3, "kst"))
                alone(pool)
                select_keys(h, 0)
                select_keys(h, 1)
                for j in (5, 6, 7):
                    if j == 7:
                        pool.wait_ge(bank_free[NB - 1], bank_frees(HG * h + 6))
                        nc.gpsimd.tensor_tensor(QK[:, :, 0:N], QK[:, :, 0:N], Fs[:, :, :], ALU.mult)\
                            .then_inc(silu_ready, 1)
                    for i in PIECE_SEQS[j]:
                        if i + 2 < NSEQ:
                            select_keys(h, i + 2)
                    deviation(h, j - 5, 48 if j == 7 else CHUNK)
                    for i in PIECE_SEQS[j]:
                        if i + S0_SLOTS < NSEQ:
                            load_state(h, i + S0_SLOTS)

            def inverse_deviation(m):
                pool.wait_ge(row_stats, m)
                nc.gpsimd.tensor_tensor(rstd[0:TT, :], var[0:TT, :], minus_half[0:TT, :], ALU.pow).then_inc(row_scale, 1)

            with pool.Fori(0, NB - 1) as j:
                pool.wait_ge(bank_free[NB - 1], bank_frees(WO_G + j))
                alone(pool)
                nc.gpsimd.tensor_copy(mix[:, bass.ds(NB * j, NB), :], stage[:, :, :]).then_inc(stage_copied, 1)
            inverse_deviation(4)
            pool.wait_ge(bank_free[NB - 1], bank_frees(WO_G + NB - 1))
            nc.gpsimd.tensor_copy(mix[:, KT - NB:KT, :], stage[:, :, :]).then_inc(stage_copied, 1)
            for s in range(S0_SLOTS):
                pool.wait_ge(s0_stored[s], 1 + 16 * HEADS * len(range(s, NSEQ, S0_SLOTS)))
            pool.wait_ge(tail_stored, 1 + 32 * HEADS)
            for row, src in ((ln_w_row, ln2_w), (ln_b_row, ln2_b)):
                pool.dma_start(row[0:TT, :], src[0:1, :].to_broadcast([TT, D])).then_inc(lnrow_landed, 16)
            for i in range(1, UNITS, 2):
                split_x1(pool, nc.gpsimd, i)
            for k in range(NB):
                pool.wait_ge(x1_ready[0], k + 1)
                pool.wait_ge(x1_ready[1], k + 1)
                x = mix[:, NB * k:NB * (k + 1), :]
                nc.gpsimd.tensor_scalar(x, x, ALPHA, None, ALU.mult).then_inc(acc_ready, 1)
            with pool.Fori(0, FB) as b:
                with pool.Fori(0, NB) as j:
                    pool.wait_ge(sq2_ready, NB * b + j + 2)
                    alone(pool)
                    f = bass.ds(NB * j, NB)
                    nc.gpsimd.tensor_copy(f_hi[:, f, :], pair[:, 1, :, :]).then_inc(fhi_ready, 1)
                    pool.wait_ge(fhi_ready, HEADS + NB * b + j + 1)
                    nc.gpsimd.tensor_tensor(f_lo[:, f, :], pair[:, 1, :, :], f_hi[:, f, :].bitcast(F32), ALU.subtract)\
                        .then_inc(f_ready, 1)
            inverse_deviation(5)
            pool.wait_ge(row_scale, 4)
            nc.gpsimd.tensor_tensor(nbias[0:TT, :], mv[0:TT, :, 0], rstd[0:TT, :], ALU.mult).then_inc(nbias_step, 1)
            pool.wait_ge(nbias_step, 1)
            nc.gpsimd.tensor_scalar(nbias[0:TT, :], nbias[0:TT, :], -1.0, None, ALU.mult).then_inc(nbias_ready, 1)
            t, c = POOL_PIECE
            y = yrow[0:TT, t, c]
            pool.wait_ge(lnrow_landed, 32)
            pool.wait_ge(yn_ready, 1)
            nc.gpsimd.tensor_tensor(y, y, ln_w_row[0:TT, c], ALU.mult).then_inc(pool_w, 1)
            pool.wait_ge(pool_w, 1)
            nc.gpsimd.tensor_tensor(y, y, ln_b_row[0:TT, c], ALU.add).then_inc(pool_piece_ready, 1)


_INS = ["x_prompt", "x_sample", "state_conv", "state_gla", "meta", "ln_in_w", "ln_in_b", "w_in", "conv_w", "w_a2",
        "b_a2", "gn_w", "w_o", "ln1_w", "ln1_b", "w1", "w2", "ln2_w", "ln2_b"]
_OUTS = [(1, SEQ, D), (NSEQ, DSEQ, D), (1, 1, CW - 1, D), (1, 1, HEADS, DK, DV), (1, NSEQ, CW - 1, D),
         (1, NSEQ, HEADS, DK, DV)]


def kernel(**inputs):
    import numpy as _np
    import concourse.bacc as _bacc
    from concourse.bass_utils import run_bass_kernel_spmd as _run

    nc = _bacc.Bacc("TRN2", target_bir_lowering=False, num_devices=1)
    arrays, args = {}, []
    for name in _INS:
        a = _np.ascontiguousarray(inputs[name])
        arrays[f"in_{name}"] = a
        args.append(nc.dram_tensor(f"in_{name}", a.shape, F32, kind="ExternalInput").ap())
    for i, shape in enumerate(_OUTS):
        args.append(nc.dram_tensor(f"out_{i}", shape, F32, kind="ExternalOutput").ap())
    build(nc, *args)
    r = _run(nc, [arrays], core_ids=[0])
    return tuple(r.results[0][f"out_{i}"] for i in range(len(_OUTS)))
```

```python
from contextlib import ExitStack

import concourse.bass as bass
from concourse import mybir

F32 = mybir.dt.float32
F32R = mybir.dt.float32r
BF16 = mybir.dt.bfloat16
ALU = mybir.AluOpType
ACT = mybir.ActivationFunctionType
AX_X = mybir.AxisListType.X

P = 128
D = 2048
KT = D // P
META, SEQ = 16, 256
NSEQ, DSEQ = 8, 4
DEC = NSEQ * DSEQ
PROMPT = META + SEQ
T = PROMPT + DEC
N = T - META
HEADS, DK, DV = 4, 256, 512
DT = DK // P
RANK = 16
FF = 4 * D
CW = 3
EPS = 1e-5
ALPHA = 2.0 ** 0.25
GW = 512
NB = GW // P
UK = 2
UNITS = KT // UK
SLOTS = 4
HG = 8
CHUNK = 128
CONV0 = META - (CW - 1)
EARLY = 2 * CHUNK - META
TT = 96
NTT = N // TT
FB = FF // D
CB, CC, CX, WQ, WK = 0, D, 2 * D, 3 * D, 3 * D + D // 2
WV = 4 * D
WG, WA, WGA, WGB = 5 * D, 6 * D, 6 * D + RANK, 7 * D + RANK
P_INW, P_INB, P_LW, P_LB, P_BA, P_GN, P_CW = 0, 16, 32, 48, 64, 72, 76
P_ALL = P_CW + CW * KT
LEVELS = [1, 2, 4, 8, 16, 32, 64]
USES = [
    ["z0", "lev_a0", "v0", "lev_b0", "o0", "o1", "o0T", "o1T", "tail"],
    ["z1", "lev_a1", "v1", "lev_b1", "d0", "d1", "d2", "s0", "d3", "d4", "d5", "s1", "d6", "d7", "s2"],
    ["lev_a2", "v2", "lev_b2", "d0", "d1", "d2", "s0", "d3", "d4", "d5", "s1", "d6", "d7", "s2"],
    ["kT", "vst", "kst", "o2", "o2T"],
]
BEFORE = [7, 6, 5, 1]
X_BANKS = 3
X_FIRST = [1, 1, 0]
HF_SLOTS = 4
WA_LO = 32
WA_W = WA_LO + RANK
S0_SLOTS = 3
PIECE_SEQS = {5: [0, 1, 2], 6: [3, 4, 5], 7: [6, 7]}
SPLIT_AFTER = [SLOTS, SLOTS + 1, SLOTS + 3]
READ_AFTER = [SLOTS - 1, SLOTS, SLOTS + 2]
UPDATE_AFTER = [SLOTS + 3, UNITS, UNITS + 2]
Q_LO = 64
QW = Q_LO + 48


def build(nc, x_prompt, x_sample, state_conv, state_gla, meta, ln_in_w, ln_in_b, w_in, conv_w,
          w_a2, b_a2, gn_w, w_o, ln1_w, ln1_b, w1, w2, ln2_w, ln2_b,
          y_prompt, y_sample, conv_prompt, gla_prompt, conv_sample, gla_sample):
    w_in, w_o, w1, w2 = w_in[0], w_o[0], w1[0], w2[0]
    with ExitStack() as ctx:
        scope = [ctx]

        def sb(name, shape, dt=F32):
            return scope[-1].enter_context(nc.sbuf_tensor(name, shape, dt))

        def sem(name):
            return ctx.enter_context(nc.semaphore(name))

        raw = sb("raw", [P, SLOTS, UK, GW])
        w_hi = sb("w_hi", [P, SLOTS, UK, GW], F32R)
        w_lo = sb("w_lo", [P, SLOTS, UK, GW], F32R)
        x_hi = sb("x_hi", [P, KT, T], F32R)
        x_lo = sb("x_lo", [P, KT, T], F32R)
        mix = sb("mix", [P, KT, N])
        ident = sb("ident", [P, P])
        ones = sb("ones", [P, P])
        params = sb("params", [P, P_ALL])
        stats = sb("stats", [P, NTT, KT // NB, 6])
        mv = sb("mv", [P, NTT, 2])
        var = sb("var", [P, NTT])
        neg_mean = sb("neg_mean", [P, NTT])
        rstd = sb("rstd", [P, NTT])
        nbias = sb("nbias", [P, NTT])
        minus_half = sb("minus_half", [P, NTT])
        stage = sb("stage", [P, NB, N])
        consts = ExitStack()
        scope.append(consts)
        mask = sb("mask", [P, 8, P], BF16)
        mask2 = sb("mask2", [P, 5, 48], BF16)
        segmask = sb("segmask", [P, NSEQ])
        carry = sb("carry", [P, T], BF16)
        a1T = sb("a1T", [RANK, T])
        stT = sb("stT", [P, KT, NSEQ * 2])
        q_dec = sb("q_dec", [P, (DT - 1) * 48 + QW])
        q_parts = sb("q_parts", [P, DT, NSEQ, QW], F32R)

        def phase(alloc):
            with ExitStack() as inner:
                scope.append(inner)
                got = alloc()
                scope.pop()
            return got

        def start_buffers():
            return (sb("xrow", [P, 3, D]), sb("wa1", [P, KT, P]), sb("wa1_parts", [P, KT, WA_W], F32R),
                    sb("a1_low", [RANK, T]), sb("hf", [P, HF_SLOTS, T]), sb("prow", [P, P]), sb("strow", [16, D]),
                    sb("stats_in", [P, 2, 4, 6]), sb("unused", [P, D]), sb("sums", [P, 2]))

        xrow, wa1, wa1_parts, a1_low, hf, prow, strow, stats_in, unused, sums = phase(start_buffers)

        def head_buffers():
            return dict(
                lev=sb("lev", [P, 4, DT, T]), eb=sb("eb", [P, DT, T]), kh=sb("kh", [P, DT, T]),
                bT=sb("bT", [P, DT, T]), qh=sb("qh", [P, DT, CHUNK]), prod=sb("prod", [P, 4, CHUNK]),
                ktok=sb("ktok", [P, 2, DT, P]), kst=sb("kst", [P, DT, 96], F32R), vst=sb("vst", [P, NB, 96], F32R),
                V=sb("V", [P, NB, T]), F=sb("F", [P, NB, N]), kt2=sb("kt2", [16, DT, P]),
                kstk=sb("kstk", [96, DT, P]), kms=sb("kms", [96, 2, DT, P], F32R), tmpA=sb("tmpA", [P, CHUNK]),
                wa2h=sb("wa2h", [RANK, DK]),
                onT=sb("onT", [P, NB, N]), QK=sb("QK", [P, NB, T]), A=sb("A", [P, NB, T]), B=sb("B", [P, NB, T]),
                vtok=sb("vtok", [P, 3, DV]), vstk=sb("vstk", [96, DV], F32R), att=sb("att", [P, 3, CHUNK]),
                S=sb("S", [P, DT, DV]), S0=sb("S0", [P, S0_SLOTS, DT, DV]), uD=sb("uD", [P, NB, NSEQ, 6]),
                tails=sb("tails", [P, NB, 18]), ebl=sb("ebl", [P, DT, 11]),
                ss=sb("ss", [P, 3]), rs=sb("rs", [P, 3]), ms=sb("ms", [P, 3]))

        hb = phase(head_buffers)
        lev, eb, kh, bT, qh, prod, ktok, kst, vst = (hb[k] for k in "lev eb kh bT qh prod ktok kst vst".split())
        V, Fs, kt2, kstk, kms, tmpA, wa2h, onT, QK = (hb[k] for k in "V F kt2 kstk kms tmpA wa2h onT QK".split())
        A, B, vtok, vstk, att, S, S0, uD = (hb[k] for k in "A B vtok vstk att S S0 uD".split())
        tails, ebl, ss, rs, ms = (hb[k] for k in "tails ebl ss rs ms".split())
        junk = prod[:, :, :].rearrange("p a b -> p (a b)")
        tailrow = ktok[0:18, :, :, :].rearrange("p a b c -> p (a b c)")

        def state_parts():
            return sb("s_hi", [P, 2, DT, DV], F32R), sb("s_lo", [P, 2, DT, DV], F32R)

        def o2_parts():
            return sb("o2_low", [48, DV]), sb("o2_sum", [48, DV])

        def tail_buffers():
            return (sb("f_hi", [P, KT, N], F32R), sb("f_lo", [P, KT, N], F32R),
                    sb("pair", [P, 2, NB, N]), sb("diag", [P, 2, NTT, TT]), sb("yrow", [P, NTT, D]),
                    sb("ln_w_row", [P, D]), sb("ln_b_row", [P, D]))

        s_hi, s_lo = phase(state_parts)
        o2_low, o2_sum = phase(o2_parts)
        scope.pop()
        consts.close()
        f_hi, f_lo, pair, diag, yrow, ln_w_row, ln_b_row = phase(tail_buffers)

        bank = [ctx.enter_context(nc.psum_tensor(f"bank{n}", [P, 512], F32)) for n in range(NB)]
        gbank = [ctx.enter_context(nc.psum_tensor(f"gbank{n}", [P, 512], F32)) for n in range(4)]

        raw_landed = [sem(f"raw_landed{s}") for s in range(SLOTS)]
        k_landed = [sem(f"k_landed{s}") for s in range(SLOTS)]
        hi_ready = sem("hi_ready")
        lo_ready = sem("lo_ready")
        units_used = sem("units_used")
        bank_full = sem("bank_full")
        bank_free = [sem(f"bank_free{n}") for n in range(NB)]
        g_full = [sem(f"g_full{n}") for n in range(4)]
        g_free = [sem(f"g_free{n}") for n in range(4)]
        x_landed = [sem(f"x_landed{i}") for i in range(3)]
        x_half_landed = [sem(f"x_half_landed{i}") for i in range(2)]
        prow_landed = sem("prow_landed")
        st_landed = sem("st_landed")
        wa1_landed = sem("wa1_landed")
        row_stats = sem("row_stats")
        row_pow = sem("row_pow")
        row_scale = sem("row_scale")
        row_done = sem("row_done")
        middle_rows_done = sem("middle_rows_done")
        sums_ready = sem("sums_ready")
        var_ready = sem("var_ready")
        const_ready = sem("const_ready")
        ident_ready = sem("ident_ready")
        x_hi_ready = sem("x_hi_ready")
        x_lo_ready = [sem("x_lo_ready_even"), sem("x_lo_ready_odd")]
        wa1_split = sem("wa1_split")
        a1_low_ready = sem("a1_low_ready")
        pool_seq = sem("pool_seq")
        pool_head = sem("pool_head")
        masks_ready = sem("masks_ready")
        dve_step = sem("dve_step")
        act_step = sem("act_step")
        b_ready = sem("b_ready")
        dist_ready = sem("dist_ready")
        exp_ready = sem("exp_ready")
        eb_ready = sem("eb_ready")
        kd_ready = sem("kd_ready")
        kdecay_ready = sem("kdecay_ready")
        lev_ready = sem("lev_ready")
        wa2h_landed = sem("wa2h_landed")
        q_step = sem("q_step")
        s_hi_ready = sem("s_hi_ready")
        s_lo_ready = sem("s_lo_ready")
        s_read = sem("s_read")
        o2_low_ready = sem("o2_low_ready")
        o2_sum_ready = sem("o2_sum_ready")
        qk_pool = sem("qk_pool")
        ebl_ready = sem("ebl_ready")
        vst_ready = sem("vst_ready")
        kms_ready = sem("kms_ready")
        tails_ready = sem("tails_ready")
        u_ready = sem("u_ready")
        uD_ready = sem("uD_ready")
        conv_done = sem("conv_done")
        cb_used = sem("cb_used")
        ga_used = sem("ga_used")
        silu_ready = sem("silu_ready")
        gated_ready = sem("gated_ready")
        ss_ready = sem("ss_ready")
        ms_ready = sem("ms_ready")
        rs_ready = sem("rs_ready")
        att_ready = sem("att_ready")
        sc1_ready = sem("sc1_ready")
        s0_landed = [sem(f"s0_landed{s}") for s in range(S0_SLOTS)]
        s0_stored = [sem(f"s0_stored{s}") for s in range(S0_SLOTS)]
        S_final = sem("S_final")
        S_stored = sem("S_stored")
        m_ready = sem("m_ready")
        tail_stored = sem("tail_stored")
        fhi_ready = sem("fhi_ready")
        f_ready = sem("f_ready")
        x_staged = sem("x_staged")
        stage_copied = sem("stage_copied")
        diag_ready = sem("diag_ready")
        norm_ready = sem("norm_ready")
        aff_ready = sem("aff_ready")
        x1hi_ready = sem("x1hi_ready")
        x1_ready = [sem("x1_ready_even"), sem("x1_ready_odd")]
        acc_ready = sem("acc_ready")
        sq2_ready = sem("sq2_ready")
        yrow_copied = sem("yrow_copied")
        lnrow_landed = sem("lnrow_landed")
        yn_ready = sem("yn_ready")
        yw_ready = sem("yw_ready")
        yb_ready = sem("yb_ready")
        out_stored = sem("out_stored")

        nbias_step = sem("nbias_step")
        nbias_ready = sem("nbias_ready")
        pool_w = sem("pool_w")
        pool_piece_ready = sem("pool_piece_ready")
        waits_alone = sem("waits_alone")

        def banks_full(g, n):
            return NB * g + n + 1

        def bank_frees(g):
            return g + 2

        def landed(g, i):
            return 16 * (2 * g + 1 + i // SLOTS)

        def g_index(h, k, use):
            return BEFORE[k] + len(USES[k]) * h + USES[k].index(use)

        def g_filled(h, k, use):
            return g_index(h, k, use) + 1

        def g_emptied(h, k, use):
            return g_index(h, k, use) + 1

        def g_available(h, k, use):
            return g_index(h, k, use)

        G_END = [BEFORE[k] + len(USES[k]) * HEADS for k in range(4)]
        WO_G, FF_G = HG * HEADS, HG * HEADS + NB
        LAST_B = FB - 1

        def w1_group(b, j):
            return FF_G + 2 * NB * b + j

        def w2_group(b, j):
            return FF_G + 2 * NB * b + NB + j

        END_G = w2_group(LAST_B, NB - 1)

        def alone(engine):
            engine.sem_inc(waits_alone, 1)

        PIECES = [(t, slice(q * GW, (q + 1) * GW)) for t in range(NTT) for q in range(D // GW)]
        DVE_PIECES, POOL_PIECES = PIECES[:-4], PIECES[-4:]

        def split_hi(act, g, i, with_k=None):
            s = i % SLOTS
            act.wait_ge(raw_landed[s], landed(g, i))
            if with_k is not None:
                act.wait_ge(k_landed[s], 16 * (2 * with_k + 1 + i // SLOTS))
            if i >= SLOTS:
                act.wait_ge(units_used, (UNITS - 1) * g + i - SLOTS + 1)
            elif not (isinstance(g, int) and g == 0):
                if i < SLOTS - 1:
                    act.wait_ge(units_used, (UNITS - 1) * (g - 1) + i + SLOTS + 1)
                else:
                    act.wait_ge(bank_full, banks_full(g - 1, NB - 1))
            nc.scalar.activation(w_hi[:, s, :, :], raw[:, s, :, :], ACT.Copy).then_inc(hi_ready, 1)

        def split_lo(dve, g, i):
            s = i % SLOTS
            dve.wait_ge(hi_ready, UNITS * g + i + 1)
            nc.vector.tensor_tensor(w_lo[:, s, :, :], raw[:, s, :, :], w_hi[:, s, :, :].bitcast(F32),
                                    ALU.subtract).then_inc(lo_ready, 1)

        def dense_group(pe, g, a_hi, a_lo, cols, operand=None, between=None, after=None, second=None):
            for i in range(UNITS):
                s = i % SLOTS
                pe.wait_ge(lo_ready, SLOTS + UNITS * g + i + 1)
                if operand is not None:
                    pe.wait_ge(*operand(i))
                for n in range(NB):
                    if i == 0:
                        pe.wait_ge(bank_free[n], bank_frees(g - 1))
                    c0, c1 = cols[n]
                    out = bank[n][:, 0:c1 - c0]
                    for kk in range(UK):
                        kt = UK * i + kk
                        if kt == 1 and n == 0 and second is not None:
                            pe.wait_ge(*second)
                        wh, wl = w_hi[:, s, kk, n * P:(n + 1) * P], w_lo[:, s, kk, n * P:(n + 1) * P]
                        nc.tensor.matmul(out, wh, a_hi[:, kt, c0:c1], start=(kt == 0), stop=False)
                        nc.tensor.matmul(out, wh, a_lo[:, kt, c0:c1], start=False, stop=False)
                        last = nc.tensor.matmul(out, wl, a_hi[:, kt, c0:c1], start=False, stop=(kt == KT - 1))
                    if i == UNITS - 1:
                        last.then_inc(bank_full, 1)
                if i < UNITS - 1:
                    last.then_inc(units_used, 1)
                if i == SLOTS - 1 and between is not None:
                    between()
                if after is not None:
                    after(i)

        NORM_STEPS = [(0, 1), (1, 2)] + [(k, k + UK) for k in range(UK, KT, UK)]

        def unit_of(step):
            return NORM_STEPS[step][0] // UK

        def x1_count(i):
            return x1_ready[i % 2], (i // 2 + 1 if i % 2 else i // 2 + (1 if i == 0 else 2))

        def split_x1(engine, ops, i):
            kk = slice(*NORM_STEPS[i])
            engine.wait_ge(x1hi_ready, i + 1)
            ops.tensor_tensor(x_lo[:, kk, META:T], mix[:, kk, :], x_hi[:, kk, META:T].bitcast(F32), ALU.subtract)\
                .then_inc(x1_ready[unit_of(i) % 2], 1)

        ALL, OUT, MIX = [(0, T)] * NB, [(META, T)] * NB, [(0, N)] * NB
        CONV = [(CONV0, T)] * NB
        GROUP_COLS = [CONV, OUT[:DT] + ALL[DT:], ALL, CONV, OUT, OUT, OUT, OUT]

        def transpose(out, in_, rows):
            return nc.tensor.transpose(out, in_, ident[0:rows, 0:rows])

        def row_transposes(pe, first, g):
            for n in range(NB):
                pe.wait_ge(bank_free[n], bank_frees(g))
                for t in range(NTT):
                    if n == 0:
                        pe.wait_ge(g_free[t], first(t))
                    last = transpose(gbank[t][0:TT, n * P:(n + 1) * P], stage[:, n, t * TT:(t + 1) * TT], P)
                    if n == NB - 1:
                        last.then_inc(g_full[t], 1)

        block = ctx.enter_context(nc.Block())

        @block.sync
        def _(sp):
            sp.dma_start(xrow[0:META, 2, :], x_prompt[0, 2 * P - META:SEQ, :]).then_inc(x_landed[2], 16)
            sp.dma_start(xrow[META:META + DEC, 2, :], x_sample.rearrange("a b d -> (a b) d")).then_inc(x_landed[2], 16)
            sp.dma_start(xrow[0:META, 0, :], meta).then_inc(x_landed[0], 16)
            sp.dma_start(xrow[META:P, 0, 0:D // 2], x_prompt[0, 0:P - META, 0:D // 2]).then_inc(x_landed[0], 16)
            sp.dma_start(xrow[META:P, 0, D // 2:D], x_prompt[0, 0:P - META, D // 2:D]).then_inc(x_half_landed[0], 16)
            sp.dma_start(xrow[:, 1, 0:D // 2], x_prompt[0, P - META:2 * P - META, 0:D // 2]).then_inc(x_landed[1], 16)
            sp.dma_start(xrow[:, 1, D // 2:D], x_prompt[0, P - META:2 * P - META, D // 2:D]).then_inc(x_half_landed[1], 16)
            for src, at, rows in [(ln_in_w, P_INW, 16), (ln_in_b, P_INB, 16), (ln1_w[0], P_LW, 16), (ln1_b[0], P_LB, 16),
                                  (b_a2[0], P_BA, 8), (gn_w[0], P_GN, 4)]:
                sp.dma_start(prow[at:at + rows, :], src.rearrange("(r c) -> r c", c=P)).then_inc(prow_landed, 16)
            sp.dma_start(prow[P_CW:P_ALL, :], conv_w[0].rearrange("w (r c) -> (w r) c", c=P)).then_inc(prow_landed, 16)
            sp.dma_start(wa1[:, :, :], w_in[:, WA:WA + P].rearrange("(k p) c -> p k c", p=P)).then_inc(wa1_landed, 16)

            def load_unit(u, slot, src):
                sp.wait_ge(lo_ready, u + 1)
                alone(sp)
                sp.dma_start(raw[:, slot, :, :], src.rearrange("(k p) c -> p k c", p=P))\
                    .then_inc(raw_landed[slot], 16)

            def load_group(g, w, row0, col):
                for i in range(UNITS):
                    load_unit(UNITS * g + i, i % SLOTS, w[bass.ds(row0 + i * UK * P, UK * P), bass.ds(col, GW)])

            with sp.Fori(0, HEADS) as h:
                for j, first in enumerate([CC, None, WV, CX, CB, WGA, WG, WGB]):
                    if first is not None:
                        load_group(HG * h + j, w_in, 0, first + h * GW)
                        continue
                    for i in range(UNITS):
                        s, rows = i % SLOTS, slice(i * UK * P, (i + 1) * UK * P)
                        sp.wait_ge(lo_ready, UNITS * (HG * h + j) + i + 1)
                        sp.dma_start(raw[:, s, :, 0:DK], w_in[rows, bass.ds(WQ + h * DK, DK)]
                                     .rearrange("(k p) c -> p k c", p=P)).then_inc(raw_landed[s], 16)
                        sp.dma_start(raw[:, s, :, DK:GW], w_in[rows, bass.ds(WK + h * DK, DK)]
                                     .rearrange("(k p) c -> p k c", p=P)).then_inc(k_landed[s], 16)
            with sp.Fori(0, NB) as j:
                load_group(WO_G + j, w_o, 0, j * GW)
            with sp.Fori(0, FB) as b:
                with sp.Fori(0, NB) as j:
                    load_group(w1_group(b, j), w1, 0, b * D + j * GW)
                with sp.Fori(0, NB) as j:
                    load_group(w2_group(b, j), w2, b * D, j * GW)
            order = [0, 1, 2, 8, 3, 4, 9, 5, 6, 10, 7, 11]
            for m, (t, c) in ((m, PIECES[m]) for m in order):
                if (t, c) in POOL_PIECES:
                    sp.wait_ge(pool_piece_ready, POOL_PIECES.index((t, c)) + 1)
                else:
                    sp.wait_ge(yb_ready, m + 1)
                a, e = t * TT, (t + 1) * TT
                n_prompt = min(e, SEQ) - a
                sp.dma_start(y_prompt[0, a:a + n_prompt, c], yrow[0:n_prompt, t, c]).then_inc(out_stored, 16)
                if n_prompt < TT:
                    sp.dma_start(y_sample.rearrange("a b d -> (a b) d")[:, c],
                                 yrow[n_prompt:TT, t, c]).then_inc(out_stored, 16)
            sp.wait_ge(out_stored, 16 * (D // GW) * (NTT + 1))
            for s in range(S0_SLOTS):
                sp.wait_ge(s0_stored[s], 1 + 16 * HEADS * len(range(s, NSEQ, S0_SLOTS)))
            sp.wait_ge(S_stored, 1 + 16 * HEADS)
            sp.wait_ge(tail_stored, 1 + 32 * HEADS)

        @block.tensor
        def _(pe):
            pe.wait_ge(ident_ready, 1)
            pe.wait_ge(prow_landed, 16 * 7)
            transpose(gbank[0][:, 0:P_ALL], prow[0:P_ALL, :], P_ALL).then_inc(g_full[0], 1)
            pe.wait_ge(st_landed, 16)
            for k in range(KT):
                last = transpose(gbank[1][:, 16 * k:16 * k + 16], strow[:, k * P:(k + 1) * P], 16)
            last.then_inc(g_full[1], 1)
            for k in range(KT + HF_SLOTS):
                if k < KT:
                    n = k % X_BANKS
                    if X_FIRST[n] + k // X_BANKS > 0:
                        pe.wait_ge(g_free[n], X_FIRST[n] + k // X_BANKS)
                    for i, rows in enumerate([P, P, T - 2 * P]):
                        if k == 0:
                            pe.wait_ge(*[(row_done, 1), (middle_rows_done, 1), (row_done, 2)][i])
                        last = transpose(gbank[n][:, i * P:i * P + rows], xrow[0:rows, i, k * P:(k + 1) * P], rows)
                    last.then_inc(g_full[n], 1)
                if k >= HF_SLOTS:
                    kt = k - HF_SLOTS
                    if kt == 0:
                        pe.wait_ge(wa1_split, 2)
                    pe.wait_ge(x_lo_ready[kt % 2], kt // 2 + 1)
                    high = (gbank[3][0:RANK, 0:T], wa1_parts[:, kt, 0:RANK], x_lo[:, kt, :])
                    both = (gbank[3][0:WA_W, 0:T], wa1_parts[:, kt, :], x_hi[:, kt, :])
                    if kt == 0:
                        nc.tensor.matmul(*both, start=True, stop=False)
                        nc.tensor.matmul(*high, start=False, stop=False)
                    else:
                        nc.tensor.matmul(*high, start=False, stop=False)
                        last = nc.tensor.matmul(*both, start=False, stop=(kt == KT - 1))
            last.then_inc(g_full[3], 1)

            def level(h, k, c, c0, w, entries, use):
                pe.wait_ge(g_free[k], g_available(h, k, use))
                for m, buf in enumerate(entries):
                    out = gbank[k][0:w, m * w:(m + 1) * w]
                    for d in range(DT):
                        ks = QK[:, DT + d, c0:c0 + w] if buf is None else lev[:, buf, d, c0:c0 + w]
                        qs = QK[:, d, c0:c0 + w] if buf is None else ks
                        last = nc.tensor.matmul(out, ks, qs, start=(d == 0), stop=(d == DT - 1))
                return last

            def large_levels(c):
                for buf, L in enumerate(LEVELS[4:]):
                    for r in range(0, CHUNK, 2 * L):
                        for d in range(DT):
                            x = lev[:, buf, d, c * CHUNK + r:c * CHUNK + r + 2 * L]
                            last = nc.tensor.matmul(gbank[c][r:r + L, r + L:r + 2 * L], x[:, 0:L], x[:, L:2 * L],
                                                    start=(d == 0), stop=(d == DT - 1))
                return last

            def state_update(h, use, keys, vals):
                for d in range(DT):
                    pe.wait_ge(g_free[1 + d], g_available(h, 1 + d, use))
                    nc.tensor.matmul(gbank[1 + d][:, :], keys[:, d, :], vals, start=True, stop=True)\
                        .then_inc(g_full[1 + d], 1)

            def seq_read(h, i):
                if i == 0:
                    pe.wait_ge(g_free[3], g_available(h, 3, "o2"))
                    alone(pe)
                pe.wait_ge(s_lo_ready, NSEQ * h + i + 1)
                for d in range(DT):
                    nc.tensor.matmul(gbank[3][0:QW, :], q_parts[:, d, i, :], s_hi[:, i % 2, d, :],
                                     start=(i == 0 and d == 0), stop=False)
                for d in range(DT):
                    last = nc.tensor.matmul(gbank[3][0:48, :], q_parts[:, d, i, 0:48], s_lo[:, i % 2, d, :],
                                            start=False, stop=False)
                last.then_inc(s_read, 1)

            def rows_to_features(h, k, use, src, rows):
                pe.wait_ge(g_free[k], g_available(h, k, use))
                alone(pe)
                for n in range(NB):
                    last = transpose(src[0](n), src[1](n), rows)
                last.then_inc(g_full[k], 1)

            def o_transposed(h, c):
                rows_to_features(h, 0, f"o{c}T", (lambda n: gbank[0][:, n * P:(n + 1) * P],
                                                  lambda n: vtok[:, c, n * P:(n + 1) * P]), P)

            def last_chunk(h):
                nc.tensor.matmul(gbank[3][0:48, :], att[0:48, 2, 0:48], vtok[0:48, 2, :], start=False, stop=False)
                for d in range(DT):
                    w = QW if d == DT - 1 else 48
                    last = nc.tensor.matmul(gbank[3][0:w, :], q_dec[:, d * 48:d * 48 + w], S[:, d, :],
                                            start=False, stop=(d == DT - 1))
                last.then_inc(g_full[3], 1)

            def sequences(h, j):
                if j not in PIECE_SEQS:
                    return None

                def after(unit):
                    if unit in READ_AFTER:
                        m = READ_AFTER.index(unit)
                        if m < len(PIECE_SEQS[j]):
                            seq_read(h, PIECE_SEQS[j][m])
                            seq_write(h, PIECE_SEQS[j][m])
                    if j == 7:
                        if unit == 0:
                            o_transposed(h, 0)
                        if unit == 2:
                            o_transposed(h, 1)
                        if unit == 4:
                            pe.wait_ge(tails_ready, h + 1)
                            rows_to_features(h, 0, "tail", (lambda n: gbank[0][0:18, n * P:(n + 1) * P],
                                                            lambda n: tails[:, n, :]), P)
                        if unit == 5:
                            last_chunk(h)
                        if unit == 6:
                            state_update(h, "s2", kt2, vtok[0:16, 2, :])
                return after

            def seq_write(h, i):
                pe.wait_ge(kms_ready, NSEQ * h + i + 1)
                state_update(h, f"d{i}", kms[:, i % 2, :, :], vstk[:, :])

            with pe.Fori(0, HEADS) as h:
                for j in range(HG):
                    dense_group(pe, HG * h + j, x_hi, x_lo, GROUP_COLS[j], after=sequences(h, j))
                    if j == 0:
                        pe.wait_ge(wa2h_landed, 16 * (h + 1))
                        for d in range(DT):
                            pe.wait_ge(g_free[d], g_available(h, d, f"z{d}"))
                            nc.tensor.matmul(gbank[d][:, 0:T], wa2h[:, d * P:(d + 1) * P], a1T[:, :],
                                             start=True, stop=True).then_inc(g_full[d], 1)
                    if j == 2:
                        pe.wait_ge(lev_ready, 7 * h + 3)
                        for c in range(2):
                            level(h, c, c, c * CHUNK, CHUNK, [None, 0, 1, 2], f"lev_a{c}").then_inc(g_full[c], 1)
                        level(h, 2, 2, 2 * CHUNK, 48, [None, 0, 1, 2], "lev_a2").then_inc(g_full[2], 1)
                        pe.wait_ge(qk_pool, 5 * h + 4)
                        pe.wait_ge(g_free[3], g_available(h, 3, "kT"))
                        for c in range(2):
                            for d in range(DT):
                                m = c * DT + d
                                last = transpose(gbank[3][:, m * P:(m + 1) * P],
                                                 kh[:, d, c * CHUNK:(c + 1) * CHUNK], P)
                        last.then_inc(g_full[3], 1)
                    if j == 3:
                        for c, w in enumerate([CHUNK, CHUNK, 48]):
                            pe.wait_ge(g_free[c], g_available(h, c, f"v{c}"))
                            alone(pe)
                            for n in range(NB):
                                last = transpose(gbank[c][0:w, n * P:(n + 1) * P], V[:, n, c * CHUNK:c * CHUNK + w], P)
                            last.then_inc(g_full[c], 1)
                        pe.wait_ge(vst_ready, 3 * h + 3)
                        pe.wait_ge(g_free[3], g_available(h, 3, "vst"))
                        for n in range(NB):
                            last = transpose(gbank[3][0:96, n * P:(n + 1) * P], vst[:, n, :].bitcast(F32), P)
                        last.then_inc(g_full[3], 1)
                    if j == 4:
                        pe.wait_ge(lev_ready, 7 * h + 7)
                        for c in range(2):
                            level(h, c, c, c * CHUNK, CHUNK, [3], f"lev_b{c}")
                            large_levels(c).then_inc(g_full[c], 1)
                        level(h, 2, 2, 2 * CHUNK, 48, [3], "lev_b2")
                        for d in range(DT):
                            last = transpose(gbank[2][0:16, P + d * P:P + (d + 1) * P],
                                             kh[:, d, 2 * CHUNK:PROMPT], P)
                        last.then_inc(g_full[2], 1)
                        pe.wait_ge(qk_pool, 5 * h + 5)
                        pe.wait_ge(g_free[3], g_available(h, 3, "kst"))
                        for d in range(DT):
                            last = transpose(gbank[3][0:96, d * P:(d + 1) * P], kst[:, d, :].bitcast(F32), P)
                        last.then_inc(g_full[3], 1)
                    if j == 5:
                        pe.wait_ge(att_ready, 3 * h + 3)
                        pe.wait_ge(g_free[0], g_available(h, 0, "o0"))
                        nc.tensor.matmul(gbank[0][:, :], att[:, 0, :], vtok[:, 0, :], start=True, stop=True)\
                            .then_inc(g_full[0], 1)
                        state_update(h, "s0", ktok[:, 0, :, :], vtok[:, 0, :])
                    if j == 6:
                        pe.wait_ge(g_free[0], g_available(h, 0, "o1"))
                        nc.tensor.matmul(gbank[0][:, :], att[:, 1, :], vtok[:, 1, :], start=True, stop=False)
                        for d in range(DT):
                            last = nc.tensor.matmul(gbank[0][:, :], qh[:, d, :], S[:, d, :], start=False,
                                                    stop=(d == DT - 1))
                        last.then_inc(g_full[0], 1)
                        state_update(h, "s1", ktok[:, 1, :, :], vtok[:, 1, :])
                    if j == 7:
                        rows_to_features(h, 3, "o2T", (lambda n: gbank[3][:, n * 48:(n + 1) * 48],
                                                       lambda n: o2_low[:, n * P:(n + 1) * P]), 48)

            mix_part = lambda i: (f_ready, i // 2 + 1)
            dense_group(pe, WO_G, f_hi, f_lo, MIX, mix_part)
            with pe.Fori(1, NB) as j:
                dense_group(pe, WO_G + j, f_hi, f_lo, MIX, mix_part,
                            between=lambda: row_transposes(pe, lambda t: G_END[t] + j - 1, WO_G + j - 1))
            row_transposes(pe, lambda t: G_END[t] + NB - 1, WO_G + NB - 1)
            for m, k in enumerate([3, 0]):
                pe.wait_ge(diag_ready, m + 1)
                pe.wait_ge(g_free[k], G_END[3] if k == 3 else G_END[0] + NB)
                for t in range(NTT):
                    last = nc.tensor.matmul(gbank[k][:, t * TT:(t + 1) * TT], ones[0:TT, :], diag[0:TT, m, t, :],
                                            start=True, stop=True)
                last.then_inc(g_full[k], 1)

            def up(b):
                with pe.Fori(0, NB) as j:
                    dense_group(pe, w1_group(b, j), x_hi, x_lo, OUT, x1_count, second=(x1_ready[0], 2))

            def down_part(b):
                return lambda i: (f_ready, HEADS + NB * b + i // 2 + 1)

            with pe.Fori(0, LAST_B) as b:
                up(b)
                with pe.Fori(0, NB) as j:
                    dense_group(pe, w2_group(b, j), f_hi, f_lo, MIX, down_part(b))
            up(LAST_B)
            dense_group(pe, w2_group(LAST_B, 0), f_hi, f_lo, MIX, down_part(LAST_B))
            used = [NB + 1, NB, NB]
            with pe.Fori(1, NB) as j:
                dense_group(pe, w2_group(LAST_B, j), f_hi, f_lo, MIX, down_part(LAST_B),
                            between=lambda: row_transposes(pe, lambda t: G_END[t] + used[t] + j - 1,
                                                           w2_group(LAST_B, j - 1)))
            row_transposes(pe, lambda t: G_END[t] + used[t] + NB - 1, END_G)

        @block.scalar
        def _(act):
            act.dma_start(strow[:, :], state_conv[0].rearrange("a b d -> (a b) d")).then_inc(st_landed, 16)

            last_rows = xrow[0:T - 2 * P, 2, :]
            act.wait_ge(x_landed[2], 32)
            nc.scalar.activation(unused[0:T - 2 * P, :], last_rows, ACT.Copy, accum_out=sums[0:T - 2 * P, 0:1])\
                .then_inc(sums_ready, 1)
            act.wait_ge(sums_ready, 1)
            nc.scalar.activation(neg_mean[0:T - 2 * P, 2:3], sums[0:T - 2 * P, 0:1], ACT.Copy, scale=-1.0 / D)\
                .then_inc(sums_ready, 1)
            act.wait_ge(sums_ready, 2)
            nc.scalar.activation(unused[0:T - 2 * P, :], last_rows, ACT.Square, bias=neg_mean[0:T - 2 * P, 2:3],
                                 accum_out=sums[0:T - 2 * P, 1:2]).then_inc(sums_ready, 1)

            def normalise_rows(i, rows, count):
                act.wait_ge(row_scale, count)
                nc.scalar.activation(xrow[0:rows, i, :], xrow[0:rows, i, :], ACT.Identity, bias=nbias[0:rows, i:i + 1],
                                     scale=rstd[0:rows, i:i + 1]).then_inc(row_done, 1)

            normalise_rows(0, P, 1)
            act.wait_ge(g_full[0], 1)
            nc.scalar.activation(params[:, :], gbank[0][:, 0:P_ALL], ACT.Copy).then_inc(g_free[0], 1)
            normalise_rows(2, T - 2 * P, 2)
            act.wait_ge(g_full[1], 1)
            nc.scalar.activation(stT[:, :, :], gbank[1][:, 0:16 * KT], ACT.Copy).then_inc(g_free[1], 1)
            act.wait_ge(wa1_landed, 16)
            act.wait_ge(const_ready, 1)
            nc.scalar.activation(wa1_parts[:, :, 0:RANK], wa1[:, :, 0:RANK], ACT.Copy).then_inc(wa1_split, 1)
            act.wait_ge(g_free[0], 1)
            for k in range(KT):
                n = k % X_BANKS
                act.wait_ge(g_full[n], X_FIRST[n] + k // X_BANKS + 1)
                if k >= HF_SLOTS:
                    act.wait_ge(x_lo_ready[k % 2], (k - HF_SLOTS) // 2 + 1)
                nc.scalar.activation(hf[:, k % HF_SLOTS, :], gbank[n][:, 0:T], ACT.Identity,
                                     bias=params[:, P_INB + k:P_INB + k + 1],
                                     scale=params[:, P_INW + k:P_INW + k + 1]).then_inc(g_free[n], 1)
                if k in (KT // 2, KT - 1):
                    split_hi(act, 0, k // (KT - 1))
            for i in range(2, SLOTS):
                split_hi(act, 0, i)
            act.wait_ge(g_full[3], 1)
            nc.scalar.activation(a1_low[:, :], gbank[3][WA_LO:WA_W, 0:T], ACT.Copy).then_inc(a1_low_ready, 1)

            def evacuate(g, dst, func, scale=1.0):
                for n in range(NB):
                    act.wait_ge(bank_full, banks_full(g, n))
                    nc.scalar.activation(dst(n), bank[n][:, 0:dst(n).shape[-1]], func,
                                         scale=(scale if n < DT else 1.0)).then_inc(bank_free[n], 1)

            def normalise(h, c, k, use, rows, summed=None):
                o = gbank[k] if summed is None else summed
                act.wait_ge(g_full[k], g_filled(h, k, use))
                nc.scalar.activation(junk[0:rows, :], o[0:rows, :], ACT.Square,
                                     accum_out=ss[0:rows, c:c + 1]).then_inc(ss_ready, 1)
                act.wait_ge(rs_ready, 3 * h + c + 1)
                if summed is None:
                    act.wait_ge(g_full[2], g_filled(h, 2, f"s{c}"))
                dst = vtok[0:rows, c, :] if summed is None else o2_low[:, :]
                nc.scalar.activation(dst, o[0:rows, :], ACT.Copy,
                                     scale=rs[0:rows, c:c + 1]).then_inc(g_free[k], 1)

            def rows_back(h, k, use, w, skip, at):
                act.wait_ge(g_full[k], g_filled(h, k, use))
                for n in range(NB):
                    last = nc.scalar.activation(onT[:, n, at:at + w - skip], gbank[k][:, n * w + skip:(n + 1) * w],
                                                ACT.Copy, scale=params[:, P_GN + n:P_GN + n + 1])
                last.then_inc(g_free[k], 1)

            def exp_level(h, lv):
                act.wait_ge(dist_ready, 7 * h + lv + 1)
                nc.scalar.activation(lev[:, lv, :, :], lev[:, lv, :, :], ACT.Exp, scale=1.0 / 16).then_inc(exp_ready, 1)

            def state_hi(h, i):
                s = i % S0_SLOTS
                act.wait_ge(s0_landed[s], 16 * (len(range(s, NSEQ, S0_SLOTS)) * h + i // S0_SLOTS + 1))
                if i >= 2:
                    act.wait_ge(s_read, NSEQ * h + i - 1)
                nc.scalar.activation(s_hi[:, i % 2, :, :], S0[:, s, :, :], ACT.Copy).then_inc(s_hi_ready, 1)

            def store_state(h, i):
                s = i % S0_SLOTS
                act.wait_ge(g_free[2], g_emptied(h, 2, f"d{i}"))
                act.dma_start(gla_sample[0, i, bass.ds(h, 1), :, :].rearrange("o (d p) v -> p (o d) v", p=P),
                              S0[:, s, :, :]).then_inc(s0_stored[s], 16)

            def merged_hi(k):
                act.wait_ge(m_ready, HEADS if k == HEADS - 1 else HEADS - 1)
                nc.scalar.activation(f_hi[:, NB * k:NB * (k + 1), :], mix[:, NB * k:NB * (k + 1), :], ACT.Copy)\
                    .then_inc(fhi_ready, 1)

            def head(h, final=False):
                for j in range(HG):
                    g = HG * h + j
                    for i in range(SLOTS, UNITS):
                        split_hi(act, g, i, with_k=(h if j == 1 else None))
                        if j in PIECE_SEQS and i in SPLIT_AFTER[:len(PIECE_SEQS[j])]:
                            state_hi(h, PIECE_SEQS[j][SPLIT_AFTER.index(i)])
                        if j == 7 and i == SLOTS + 1:
                            rows_back(h, 0, "o0T", CHUNK, META, 0)
                        if j == 7 and i == SLOTS + 3:
                            rows_back(h, 0, "o1T", CHUNK, 0, CHUNK - META)
                        if j == 1 and i > SLOTS:
                            exp_level(h, i - SLOTS - 1)
                        if j == 3 and i < 7:
                            lv = i - SLOTS
                            act.wait_ge(dist_ready, 7 * h + 4 + lv + 1)
                            nc.scalar.activation(lev[:, lv, :, 0:2 * CHUNK], lev[:, lv, :, 0:2 * CHUNK], ACT.Exp,
                                                 scale=1.0 / 16).then_inc(exp_ready, 1)
                    for i in range(SLOTS - 1):
                        split_hi(act, g + 1, i, with_k=(h if j == 0 else None))
                        if j == 7 and i == 1:
                            act.wait_ge(g_full[0], g_filled(h, 0, "tail"))
                            nc.scalar.activation(tailrow, gbank[0][0:18, :], ACT.Copy).then_inc(g_free[0], 1)
                        if final and j == 7 and i == 2:
                            merged_hi(0)
                        if j == 7 and i == 1:
                            act.wait_ge(g_full[3], g_filled(h, 3, "o2"))
                            nc.scalar.activation(o2_low[:, :], gbank[3][Q_LO:QW, :], ACT.Copy).then_inc(o2_low_ready, 1)
                            for seq in PIECE_SEQS[j]:
                                store_state(h, seq)
                            act.wait_ge(o2_sum_ready, h + 1)
                            normalise(h, 2, 3, "o2", 48, o2_sum)
                        if j == 1 and i == 0:
                            exp_level(h, 3)
                        if j == 1 and i == 1:
                            nc.scalar.activation(eb[:, :, :], bT[:, :, :], ACT.Exp, scale=1.0 / 16).then_inc(eb_ready, 1)
                        if j == 1 and i == 2:
                            act.wait_ge(kd_ready, h + 1)
                            nc.scalar.activation(kh[:, :, :], kh[:, :, :], ACT.Exp, scale=1.0 / 16)\
                                .then_inc(kdecay_ready, 1)
                    if j == 0:
                        evacuate(g, lambda n: A[:, n, CONV0:T], ACT.Copy)
                    if j == 1:
                        nc.scalar.activation(QK[:, 0:DT, 0:META], ones[:, 0:DT * META], ACT.Copy, scale=0.0)
                        evacuate(g, lambda n: QK[:, n, META if n < DT else 0:T], ACT.Copy, scale=float(DK) ** -0.5)
                    if j == 2:
                        evacuate(g, lambda n: V[:, n, :], ACT.Copy)
                    if j == 3:
                        evacuate(g, lambda n: B[:, n, CONV0:T], ACT.Copy)
                    if j == 4:
                        act.wait_ge(vst_ready, 3 * h + 3)
                        evacuate(g, lambda n: V[:, n, 0:N], ACT.Copy)
                    if j == 5:
                        act.wait_ge(conv_done, h + 1)
                        act.wait_ge(tails_ready, h + 1)
                        evacuate(g, lambda n: A[:, n, 0:N], ACT.Sigmoid)
                    if j == 6:
                        for n in range(NB):
                            act.wait_ge(bank_full, banks_full(g, n))
                            nc.scalar.activation(Fs[:, n, :], bank[n][:, 0:N], ACT.Sigmoid)
                            nc.scalar.activation(QK[:, n, 0:N], bank[n][:, 0:N], ACT.Copy).then_inc(bank_free[n], 1)
                    if j == 7:
                        act.wait_ge(ga_used, h + 1)
                        evacuate(g, lambda n: A[:, n, 0:N], ACT.Sigmoid)
                    split_hi(act, g + 1, SLOTS - 1, with_k=(h if j == 0 else None))
                    if final and j == 7:
                        merged_hi(1)
                    if j == 0:
                        for d in range(DT):
                            act.wait_ge(g_full[d], g_filled(h, d, f"z{d}"))
                            nc.scalar.activation(lev[:, 2, d, :], gbank[d][:, 0:T], ACT.Identity,
                                                 bias=params[:, bass.ds(P_BA + DT * h + d, 1)]).then_inc(g_free[d], 1)
                        act.wait_ge(g_free[1], g_emptied(h, 1, "z1"))
                        nc.scalar.activation(lev[:, 3, :, :], lev[:, 2, :, :], ACT.Abs).then_inc(act_step, 1)
                        act.wait_ge(act_step, 3 * h + 1)
                        nc.scalar.activation(lev[:, 3, :, :], lev[:, 3, :, :], ACT.Exp, scale=-1.0).then_inc(act_step, 1)
                        act.wait_ge(act_step, 3 * h + 2)
                        nc.scalar.activation(lev[:, 3, :, :], lev[:, 3, :, :], ACT.Ln, bias=ones[:, 0:1])\
                            .then_inc(act_step, 1)
                    if j == 2:
                        act.wait_ge(tail_stored, 32 * h + 1)
                        act.wait_ge(g_full[3], g_filled(h, 3, "kT"))
                        nc.scalar.activation(ktok[:, :, :, :], gbank[3][:, :], ACT.Copy).then_inc(g_free[3], 1)
                    if j == 3:
                        for c, w in enumerate([CHUNK, CHUNK, 48]):
                            act.wait_ge(g_full[c], g_filled(h, c, f"v{c}"))
                            nc.scalar.activation(vtok[0:w, c, :], gbank[c][0:w, :], ACT.Copy).then_inc(g_free[c], 1)
                        act.wait_ge(g_full[3], g_filled(h, 3, "vst"))
                        nc.scalar.activation(vstk[:, :], gbank[3][0:96, :], ACT.Copy).then_inc(g_free[3], 1)
                    if j == 4:
                        act.wait_ge(g_full[3], g_filled(h, 3, "kst"))
                        nc.scalar.activation(kstk[:, :, :], gbank[3][0:96, 0:DK], ACT.Copy).then_inc(g_free[3], 1)
                    if j in (5, 6):
                        for i in PIECE_SEQS[j]:
                            store_state(h, i)
                        normalise(h, j - 5, 0, f"o{j - 5}", CHUNK)
                    if j == 7:
                        act.wait_ge(g_free[2], g_emptied(h, 2, "s2"))
                        act.dma_start(gla_prompt[0, 0, bass.ds(h, 1), :, :].rearrange("o (d p) v -> p (o d) v", p=P),
                                      S[:, :, :]).then_inc(S_stored, 16)
                        act.wait_ge(g_free[0], g_emptied(h, 0, "tail"))
                        act.dma_start(conv_prompt[0, 0, :, bass.ds(h * GW, GW)], tailrow[0:2]).then_inc(tail_stored, 16)
                        act.dma_start(conv_sample[0].rearrange("i c d -> (i c) d")[:, bass.ds(h * GW, GW)],
                                      tailrow[2:18]).then_inc(tail_stored, 16)
                        rows_back(h, 3, "o2T", 48, 0, 2 * CHUNK - META)

            def group_splits(g, first):
                for i in range(first, UNITS):
                    split_hi(act, g, i)
                for i in range(SLOTS - 1):
                    split_hi(act, g + 1, i)

            def next_splits(g):
                for i in range(SLOTS - 1, SLOTS + 1):
                    split_hi(act, g + 1, i)

            with act.Fori(0, HEADS - 1) as h:
                head(h)
            head(HEADS - 1, final=True)
            for k in range(2, HEADS):
                merged_hi(k)
            with act.Fori(0, NB) as j:
                group_splits(WO_G + j, SLOTS)
                split_hi(act, WO_G + j + 1, SLOTS - 1)
            for i, (a, e) in enumerate(NORM_STEPS):
                act.wait_ge(norm_ready, i + 1)
                for f in range(a, e):
                    last = nc.scalar.activation(mix[:, f, :], mix[:, f, :], ACT.Identity,
                                                bias=params[:, P_LB + f:P_LB + f + 1],
                                                scale=params[:, P_LW + f:P_LW + f + 1])
                last.then_inc(aff_ready, 1)
                act.wait_ge(aff_ready, i + 1)
                nc.scalar.activation(x_hi[:, a:e, META:T], mix[:, a:e, :], ACT.Copy).then_inc(x1hi_ready, 1)
                if unit_of(i) == UNITS - 4:
                    split_hi(act, FF_G, SLOTS)

            def relu_group(g):
                for n in range(NB):
                    act.wait_ge(bank_full, banks_full(g, n))
                    nc.scalar.activation(pair[:, 0, n, :], bank[n][:, 0:N], ACT.Relu).then_inc(bank_free[n], 1)

            def up(b):
                with act.Fori(0, NB) as j:
                    g = w1_group(b, j)
                    group_splits(g, SLOTS + 1)
                    act.wait_ge(sq2_ready, NB * b + j + 1)
                    relu_group(g)
                    next_splits(g)

            with act.Fori(0, LAST_B) as b:
                up(b)
                with act.Fori(0, NB) as j:
                    group_splits(w2_group(b, j), SLOTS + 1)
                    next_splits(w2_group(b, j))
            up(LAST_B)

            def rows_out(first, m):
                for t in range(NTT):
                    act.wait_ge(g_full[t], first(t))
                    nc.scalar.activation(yrow[0:TT, t, bass.ds(m * GW, GW)], gbank[t][0:TT, :], ACT.Copy)\
                        .then_inc(yrow_copied, 1)

            used = [NB + 1, NB, NB]
            full0 = [G_END[t] + used[t] for t in range(NTT)]
            group_splits(w2_group(LAST_B, 0), SLOTS + 1)
            split_hi(act, w2_group(LAST_B, 1), SLOTS - 1)
            with act.Fori(1, NB - 1) as j:
                g = w2_group(LAST_B, j)
                for i in range(SLOTS, UNITS):
                    split_hi(act, g, i)
                rows_out(lambda t: full0[t] + j, j - 1)
                for i in range(SLOTS):
                    split_hi(act, g + 1, i)
            for i in range(SLOTS, UNITS):
                split_hi(act, END_G, i)
            rows_out(lambda t: full0[t] + NB - 1, NB - 2)
            rows_out(lambda t: full0[t] + NB, NB - 1)
            act.wait_ge(nbias_ready, 1)
            for t, c in POOL_PIECES:
                nc.scalar.activation(yrow[0:TT, t, c], yrow[0:TT, t, c], ACT.Identity,
                                     bias=nbias[0:TT, t:t + 1], scale=rstd[0:TT, t:t + 1]).then_inc(yn_ready, 1)

        @block.vector
        def _(dve):
            dve.sem_inc(lo_ready, SLOTS)
            for n in range(NB):
                dve.sem_inc(bank_free[n], 1)
            nc.vector.memset(carry[:, :], 1.0).then_inc(dve_step, 1)
            dve.wait_ge(dve_step, 1)
            for c in (0, CHUNK, 2 * CHUNK):
                nc.vector.memset(carry[:, c:c + 1], 0.0)
            nc.vector.memset(carry[:, PROMPT:T:DSEQ], 0.0)
            nc.vector.memset(wa1_parts[:, :, :].bitcast(F32), 0.0)
            nc.vector.memset(q_parts[:, :, :, :].bitcast(F32), 0.0)
            nc.vector.memset(q_dec[:, :], 0.0).then_inc(const_ready, 1)

            for i, rows in enumerate([P, P]):
                dve.wait_ge(x_landed[i], 16 if i == 1 else 32)
                for q in range(4):
                    if q == 2:
                        dve.wait_ge(x_half_landed[i], 16)
                    last = nc.vector.bn_stats(stats_in[0:rows, i, q, :], xrow[0:rows, i, q * 512:(q + 1) * 512])
                last.then_inc(dve_step, 1)
                dve.wait_ge(dve_step, 2 * i + 2)
                nc.vector.bn_aggr(mv[0:rows, i, :], stats_in[0:rows, i, :, :].rearrange("p q s -> p (q s)"))\
                    .then_inc(dve_step, 1)
                dve.wait_ge(dve_step, 2 * i + 3)
                nc.vector.tensor_scalar(var[0:rows, i:i + 1], mv[0:rows, i, 1:2], EPS, None, ALU.add)
                nc.vector.tensor_scalar(neg_mean[0:rows, i:i + 1], mv[0:rows, i, 0:1], -1.0, None, ALU.mult)\
                    .then_inc(row_stats, 1)
            dve.wait_ge(row_pow, 3)
            nc.vector.tensor_scalar(xrow[:, 1, :], xrow[:, 1, :], mv[:, 1, 0:1], rstd[:, 1:2], ALU.subtract, ALU.mult)\
                .then_inc(middle_rows_done, 1)
            for k in range(KT):
                n = k % X_BANKS
                dve.wait_ge(g_free[n], X_FIRST[n] + k // X_BANKS + 1)
                nc.vector.tensor_copy(x_hi[:, k, :], hf[:, k % HF_SLOTS, :]).then_inc(x_hi_ready, 1)
                if k % 2 == 0:
                    dve.wait_ge(x_hi_ready, k + 1)
                    nc.vector.tensor_tensor(x_lo[:, k, :], hf[:, k % HF_SLOTS, :], x_hi[:, k, :].bitcast(F32),
                                            ALU.subtract).then_inc(x_lo_ready[0], 1)
                if k == 0:
                    dve.wait_ge(wa1_split, 1)
                    nc.vector.tensor_tensor(wa1_parts[:, :, WA_LO:WA_W], wa1[:, :, 0:RANK],
                                            wa1_parts[:, :, 0:RANK].bitcast(F32), ALU.subtract).then_inc(wa1_split, 1)
            for i in range(SLOTS):
                split_lo(dve, 0, i)
            dve.wait_ge(a1_low_ready, 1)
            nc.vector.tensor_tensor(a1T[:, :], gbank[3][0:RANK, 0:T], a1_low[:, :], ALU.add).then_inc(g_free[3], 1)
            dve.wait_ge(g_free[3], 1)

            def halves(ap, lo, hi, L):
                return ap[:, :, lo:hi].rearrange("p d (b l) -> p d b l", l=2 * L)

            def distance(h, lv, L, hi):
                out, b = halves(lev[:, lv % 4, :, :], 0, hi, L), halves(bT, 0, hi, L)
                nb = hi // (2 * L)
                ref = b[:, :, :, L - 1:L].to_broadcast([P, DT, nb, 2 * L])
                nc.vector.tensor_tensor(out, b, ref, ALU.subtract).then_inc(dve_step, 1)

            def negative(lv, hi):
                x = lev[:, lv, :, 0:hi]
                return nc.vector.scalar_tensor_tensor(out=x, in0=x, scalar=-1.0, in1=x, op0=ALU.mult, op1=ALU.min)

            def small_levels(h, k, use, w, msk):
                if k > 0:
                    dve.wait_ge(sc1_ready, 3 * h + k)
                dve.wait_ge(g_full[k], g_filled(h, k, use))
                pr = prod[0:w, :, :].rearrange("p a b -> p (a b)")[:, 0:4 * w].rearrange("p (a b) -> p a b", b=w)
                nc.vector.tensor_tensor(pr, gbank[k][0:w, 0:4 * w].rearrange("p (a b) -> p a b", b=w), msk, ALU.mult)\
                    .then_inc(g_free[k], 1)
                dve.wait_ge(g_free[k], g_emptied(h, k, use))
                nc.vector.tensor_reduce(out=att[0:w, k, 0:w], in_=pr.rearrange("p a b -> p b a"), axis=AX_X, op=ALU.add)\
                    .then_inc(sc1_ready, 1)

            def large_levels(h, c):
                if c > 0:
                    dve.wait_ge(att_ready, 3 * h + c)
                dve.wait_ge(g_full[c], g_filled(h, c, f"lev_b{c}"))
                nc.vector.tensor_tensor(tmpA[:, :], gbank[c][:, 0:CHUNK], mask[:, 4, :], ALU.mult).then_inc(g_free[c], 1)
                dve.wait_ge(g_free[c], g_emptied(h, c, f"lev_b{c}"))
                dve.wait_ge(sc1_ready, 3 * h + 3)
                nc.vector.tensor_tensor(att[:, c, :], att[:, c, :], tmpA[:, :], ALU.add).then_inc(att_ready, 1)

            def state_lo(h, i):
                dve.wait_ge(s_hi_ready, NSEQ * h + i + 1)
                nc.vector.tensor_tensor(s_lo[:, i % 2, :, :], S0[:, i % S0_SLOTS, :, :],
                                        s_hi[:, i % 2, :, :].bitcast(F32), ALU.subtract).then_inc(s_lo_ready, 1)

            def seq_state(h, i):
                if i == 0:
                    dve.wait_ge(ebl_ready, h + 1)
                s = i % S0_SLOTS
                for d in range(DT):
                    dve.wait_ge(g_full[1 + d], g_filled(h, 1 + d, f"d{i}"))
                    nc.vector.scalar_tensor_tensor(out=S0[:, s, d, :], in0=S0[:, s, d, :],
                                                   scalar=ebl[:, d, 3 + i:4 + i], in1=gbank[1 + d][:, :],
                                                   op0=ALU.mult, op1=ALU.add).then_inc(g_free[1 + d], 1)

            def prompt_state(h, c):
                for d in range(DT):
                    dve.wait_ge(g_full[1 + d], g_filled(h, 1 + d, f"s{c}"))
                    if c == 0:
                        if d == 0:
                            dve.wait_ge(S_stored, 16 * h + 1)
                        nc.vector.tensor_copy(S[:, d, :], gbank[1 + d][:, :]).then_inc(g_free[1 + d], 1)
                    else:
                        nc.vector.scalar_tensor_tensor(out=S[:, d, :], in0=S[:, d, :], scalar=ebl[:, d, c:c + 1],
                                                       in1=gbank[1 + d][:, :], op0=ALU.mult, op1=ALU.add)\
                            .then_inc(g_free[1 + d], 1)

            STEP0 = 5
            HS = 7 + 2 * NB + 4

            def merged_lo(k):
                dve.wait_ge(fhi_ready, k + 1)
                kk = slice(NB * k, NB * (k + 1))
                nc.vector.tensor_tensor(f_lo[:, kk, :], mix[:, kk, :], f_hi[:, kk, :].bitcast(F32), ALU.subtract)\
                    .then_inc(f_ready, 1)

            def head(h, final=False):
                step = [0]

                def link(ins):
                    ins.then_inc(dve_step, 1)
                    step[0] += 1
                    dve.wait_ge(dve_step, STEP0 + HS * h + step[0])

                for j in range(HG):
                    g = HG * h + j
                    for i in range(SLOTS, UNITS):
                        split_lo(dve, g, i)
                        if j in PIECE_SEQS and i in SPLIT_AFTER[:len(PIECE_SEQS[j])]:
                            state_lo(h, PIECE_SEQS[j][SPLIT_AFTER.index(i)])
                        if j in PIECE_SEQS and i == UPDATE_AFTER[0]:
                            seq_state(h, PIECE_SEQS[j][0])
                        if j == 1:
                            lv = i - SLOTS
                            distance(h, lv, LEVELS[lv], T)
                            step[0] += 1
                            dve.wait_ge(dve_step, STEP0 + HS * h + step[0])
                            negative(lv, T).then_inc(dist_ready, 1)
                        if j == 3 and i < 7:
                            lv = 4 + i - SLOTS
                            if i == SLOTS:
                                dve.wait_ge(g_full[3], g_filled(h, 3, "kT"))
                            distance(h, lv, LEVELS[lv], 2 * CHUNK)
                            step[0] += 1
                            dve.wait_ge(dve_step, STEP0 + HS * h + step[0])
                            negative(lv - 4, 2 * CHUNK).then_inc(dist_ready, 1)
                        if j == 4 and i == SLOTS:
                            dve.wait_ge(bank_free[NB - 1], bank_frees(g - 1))
                            nc.vector.tensor_tensor(A[:, :, CONV0:T], A[:, :, CONV0:T], B[:, :, CONV0:T], ALU.mult)\
                                .then_inc(u_ready, 1)
                        if j == 4 and i > SLOTS:
                            if i == SLOTS + 1:
                                dve.wait_ge(u_ready, h + 1)
                                dve.wait_ge(uD_ready, 2 * h + 2)
                            for n in ([0], [1, 2], [3])[i - SLOTS - 1]:
                                for t in range(CW):
                                    w = params[:, bass.ds(P_CW + KT * t + NB * h + n, 1)]
                                    off = CONV0 + t
                                    y, yd = B[:, n, 0:SEQ], B[:, n, SEQ:N].rearrange("p (i t) -> p i t", t=DSEQ)
                                    u, ud = A[:, n, off:off + SEQ], uD[:, n, :, t:t + DSEQ]
                                    if t == 0:
                                        nc.vector.tensor_scalar(y, u, w, None, ALU.mult)
                                        last = nc.vector.tensor_scalar(yd, ud, w, None, ALU.mult)
                                    else:
                                        nc.vector.scalar_tensor_tensor(out=y, in0=u, scalar=w, in1=y,
                                                                       op0=ALU.mult, op1=ALU.add)
                                        last = nc.vector.scalar_tensor_tensor(out=yd, in0=ud, scalar=w, in1=yd,
                                                                              op0=ALU.mult, op1=ALU.add)
                                    if t < CW - 1:
                                        link(last)
                                    elif n == NB - 1:
                                        last.then_inc(conv_done, 1)
                        if j == 5 and i == SLOTS:
                            dve.wait_ge(bank_free[NB - 1], bank_frees(g - 1))
                            dve.wait_ge(conv_done, h + 1)
                            nc.vector.tensor_tensor(B[:, :, 0:N], B[:, :, 0:N], V[:, :, 0:N], ALU.mult)\
                                .then_inc(cb_used, 1)
                        if j == 6 and i == SLOTS:
                            dve.wait_ge(bank_free[NB - 1], bank_frees(g - 1))
                            dve.wait_ge(cb_used, h + 1)
                            nc.vector.tensor_tensor(B[:, :, 0:N], B[:, :, 0:N], A[:, :, 0:N], ALU.mult)\
                                .then_inc(ga_used, 1)
                    for i in range(SLOTS):
                        if j == 7 and i == SLOTS - 1:
                            dve.wait_ge(silu_ready, h + 1)
                            dve.wait_ge(bank_free[NB - 1], bank_frees(g))
                            nc.vector.tensor_tensor(QK[:, :, 0:N], QK[:, :, 0:N], A[:, :, 0:N], ALU.mult)\
                                .then_inc(gated_ready, 1)
                        split_lo(dve, g + 1, i)
                        if j == 7 and i == 1:
                            dve.wait_ge(o2_low_ready, h + 1)
                            nc.vector.tensor_tensor(o2_sum[:, :], gbank[3][0:48, :], o2_low[:, :], ALU.add)\
                                .then_inc(o2_sum_ready, 1)
                        if j == 7 and i == 2:
                            if final:
                                merged_lo(0)
                            prompt_state(h, 2)
                        if j in PIECE_SEQS and UNITS + i in UPDATE_AFTER[:len(PIECE_SEQS[j])]:
                            seq_state(h, PIECE_SEQS[j][UPDATE_AFTER.index(UNITS + i)])
                        if j == 1 and i == 0:
                            b0, k0 = bT[:, :, 0:2 * CHUNK], kh[:, :, 0:2 * CHUNK]
                            v = b0.rearrange("p d (c t) -> p d c t", t=CHUNK)
                            nc.vector.tensor_tensor(k0.rearrange("p d (c t) -> p d c t", t=CHUNK),
                                                    v[:, :, :, CHUNK - 1:CHUNK].to_broadcast([P, DT, 2, CHUNK]), v,
                                                    ALU.subtract)
                            v = bT[:, :, 2 * CHUNK:PROMPT]
                            nc.vector.tensor_tensor(kh[:, :, 2 * CHUNK:PROMPT],
                                                    v[:, :, META - 1:META].to_broadcast([P, DT, META]), v, ALU.subtract)
                            v = bT[:, :, PROMPT:T].rearrange("p d (c t) -> p d c t", t=DSEQ)
                            nc.vector.tensor_tensor(kh[:, :, PROMPT:T].rearrange("p d (c t) -> p d c t", t=DSEQ),
                                                    v[:, :, :, DSEQ - 1:DSEQ].to_broadcast([P, DT, NSEQ, DSEQ]), v,
                                                    ALU.subtract).then_inc(kd_ready, 1)
                    if j == 0:
                        dve.wait_ge(act_step, 3 * h + 3)
                        link(nc.vector.scalar_tensor_tensor(out=lev[:, 2, :, :], in0=lev[:, 2, :, :], scalar=0.0,
                                                            in1=lev[:, 3, :, :], op0=ALU.min, op1=ALU.subtract))
                        for d in range(DT):
                            last = nc.vector.tensor_tensor_scan(bT[:, d, :], carry[:, :], lev[:, 2, d, :],
                                                                0.0, ALU.mult, ALU.add)
                        last.then_inc(b_ready, 1)
                        dve.wait_ge(b_ready, h + 1)
                    if j == 2:
                        dve.wait_ge(masks_ready, 1)
                        for c in range(2):
                            small_levels(h, c, f"lev_a{c}", CHUNK, mask[:, 0:4, :])
                        small_levels(h, 2, "lev_a2", 48, mask2[0:48, 0:4, :])
                    if j == 4:
                        for c in range(2):
                            large_levels(h, c)
                        dve.wait_ge(g_full[2], g_filled(h, 2, "lev_b2"))
                        dve.wait_ge(att_ready, 3 * h + 2)
                        link(nc.vector.tensor_tensor(tmpA[0:48, 0:48], gbank[2][0:48, 0:48], mask2[0:48, 4, :], ALU.mult))
                        nc.vector.tensor_tensor(att[0:48, 2, 0:48], att[0:48, 2, 0:48], tmpA[0:48, 0:48], ALU.add)\
                            .then_inc(att_ready, 1)
                        nc.vector.tensor_copy(kt2[:, :, :], gbank[2][0:16, P:P + DK]).then_inc(g_free[2], 1)
                    if j in (5, 6):
                        prompt_state(h, j - 5)
                    if j == 7:
                        if final:
                            merged_lo(1)
                        for a, e, of, k in ((0, EARLY, "o1T", 0), (EARLY, N, "o2T", 3)):
                            dve.wait_ge(g_free[k], g_emptied(h, k, of))
                            if a == 0:
                                dve.wait_ge(gated_ready, h + 1)
                            link(nc.vector.tensor_tensor(onT[:, :, a:e], onT[:, :, a:e], QK[:, :, a:e], ALU.mult))
                            last = nc.vector.tensor_tensor(mix[:, bass.ds(NB * h, NB), a:e], onT[:, :, a:e],
                                                           B[:, :, a:e], ALU.add)
                        last.then_inc(m_ready, 1)
                assert step[0] == HS

            with dve.Fori(0, HEADS - 1) as h:
                head(h)
            head(HEADS - 1, final=True)
            for k in range(2, HEADS):
                if k == HEADS - 1:
                    dve.wait_ge(tail_stored, 1 + 32 * HEADS)
                merged_lo(k)

            def group_splits(g, end=SLOTS):
                for i in range(SLOTS + 1, UNITS):
                    split_lo(dve, g, i)
                for i in range(end):
                    split_lo(dve, g + 1, i)

            def row_stats_of(m, first, copied=None):
                for t in range(NTT):
                    dve.wait_ge(g_full[t], first(t))
                    if copied is not None:
                        dve.wait_ge(yrow_copied, copied + t + 1)
                    nc.vector.bn_stats(stats[0:TT, t, bass.ds(m, 1), :], gbank[t][0:TT, :]).then_inc(g_free[t], 1)

            AFTER = STEP0 + HS * HEADS

            def residual(j):
                for n in range(NB):
                    dve.wait_ge(bank_full, banks_full(WO_G + j, n))
                    nc.vector.scalar_tensor_tensor(out=stage[:, n, :], in0=stage[:, n, :], scalar=ALPHA,
                                                   in1=bank[n][:, 0:N], op0=ALU.mult, op1=ALU.add)\
                        .then_inc(bank_free[n], 1)

            def stage_x(j):
                f = bass.ds(NB * j, NB)
                nc.vector.tensor_tensor(stage[:, :, :], x_hi[:, f, META:T].bitcast(F32), x_lo[:, f, META:T].bitcast(F32),
                                        ALU.add).then_inc(x_staged, 1)

            full1 = [G_END[t] for t in range(NTT)]
            for i in range(SLOTS, UNITS):
                split_lo(dve, WO_G, i)
            stage_x(0)
            for i in range(SLOTS - 1):
                split_lo(dve, WO_G + 1, i)
            dve.wait_ge(x_staged, 1)
            residual(0)
            with dve.Fori(1, NB) as j:
                for i in range(SLOTS - 1, UNITS):
                    split_lo(dve, WO_G + j, i)
                row_stats_of(j - 1, lambda t: full1[t] + j)
                dve.wait_ge(stage_copied, j)
                stage_x(j)
                for i in range(SLOTS - 1):
                    split_lo(dve, WO_G + j + 1, i)
                dve.wait_ge(x_staged, j + 1)
                residual(j)
            row_stats_of(NB - 1, lambda t: full1[t] + NB)

            n_link = [0]

            def chain(ins):
                ins.then_inc(dve_step, 1)
                n_link[0] += 1
                dve.wait_ge(dve_step, AFTER + n_link[0])

            def aggregate(free_count):
                for t in range(NTT):
                    dve.wait_ge(g_free[t], free_count(t))
                    last = nc.vector.bn_aggr(mv[0:TT, t, :], stats[0:TT, t, :, :].rearrange("p q s -> p (q s)"))
                chain(last)
                nc.vector.tensor_scalar(var[0:TT, :], mv[0:TT, :, 1], EPS, None, ALU.add).then_inc(row_stats, 1)

            aggregate(lambda t: G_END[t] + NB)
            for t in range(NTT):
                last = nc.vector.tensor_scalar(diag[0:TT, 0, t, :], ident[0:TT, 0:TT], mv[0:TT, t, 0:1], None, ALU.mult)
            last.then_inc(diag_ready, 1)
            dve.wait_ge(row_scale, 3)
            for t in range(NTT):
                last = nc.vector.tensor_scalar(diag[0:TT, 1, t, :], ident[0:TT, 0:TT], rstd[0:TT, t:t + 1], None, ALU.mult)
            last.then_inc(diag_ready, 1)
            split_lo(dve, FF_G, SLOTS - 1)
            dve.wait_ge(g_full[3], G_END[3] + 1)
            dve.wait_ge(g_full[0], G_END[0] + NB + 1)

            def normalise(i):
                a, e = NORM_STEPS[i]
                dve.wait_ge(stage_copied, max(a // NB + 1, NB - 1))
                x = mix[:, a:e, :]
                chain(nc.vector.tensor_tensor(x, x, gbank[3][:, None, 0:N].to_broadcast([P, e - a, N]), ALU.subtract))
                nc.vector.tensor_tensor(x, x, gbank[0][:, None, 0:N].to_broadcast([P, e - a, N]), ALU.mult)\
                    .then_inc(norm_ready, 1)

            normalise(0)
            normalise(1)
            for i in range(len(NORM_STEPS)):
                if unit_of(i) % 2 == 0:
                    split_x1(dve, nc.vector, i)
                if i == 1:
                    normalise(2)
                if 0 < i < len(NORM_STEPS) - 2:
                    normalise(i + 2)
                if unit_of(i) == UNITS - 3:
                    split_lo(dve, FF_G, SLOTS)
            dve.sem_inc(g_free[0], 1)
            dve.sem_inc(sq2_ready, 1)

            def up(b):
                with dve.Fori(0, NB) as j:
                    g = w1_group(b, j)
                    group_splits(g)
                    dve.wait_ge(bank_free[NB - 1], bank_frees(g))
                    dve.wait_ge(f_ready, HEADS + NB * b + j)
                    nc.vector.tensor_tensor(pair[:, 1, :, :], pair[:, 0, :, :], pair[:, 0, :, :], ALU.mult)\
                        .then_inc(sq2_ready, 1)
                    split_lo(dve, g + 1, SLOTS)

            with dve.Fori(0, LAST_B) as b:
                up(b)
                dve.wait_ge(acc_ready, NB)
                with dve.Fori(0, NB) as j:
                    g = w2_group(b, j)
                    group_splits(g, SLOTS - 1)
                    for n in range(NB):
                        dve.wait_ge(bank_full, banks_full(g, n))
                        acc = mix[:, bass.ds(NB * j + n, 1), :]
                        nc.vector.tensor_tensor(acc, acc, bank[n][:, 0:N], ALU.add).then_inc(bank_free[n], 1)
                    for i in range(SLOTS - 1, SLOTS + 1):
                        split_lo(dve, g + 1, i)
            up(LAST_B)

            def last_sum(j):
                for n in range(NB):
                    dve.wait_ge(bank_full, banks_full(w2_group(LAST_B, j), n))
                    nc.vector.tensor_tensor(stage[:, n, :], mix[:, bass.ds(NB * j + n, 1), :], bank[n][:, 0:N],
                                            ALU.add).then_inc(bank_free[n], 1)

            used = [NB + 1, NB, NB]
            full2 = [G_END[t] + used[t] for t in range(NTT)]
            g0 = w2_group(LAST_B, 0)
            group_splits(g0, SLOTS - 1)
            last_sum(0)
            split_lo(dve, g0 + 1, SLOTS - 1)
            with dve.Fori(1, NB - 1) as j:
                for i in range(SLOTS, UNITS):
                    split_lo(dve, g0 + j, i)
                row_stats_of(j - 1, lambda t: full2[t] + j, NTT * (j - 1))
                for i in range(SLOTS - 1):
                    split_lo(dve, g0 + j + 1, i)
                last_sum(j)
                split_lo(dve, g0 + j + 1, SLOTS - 1)
            for i in range(SLOTS, UNITS):
                split_lo(dve, END_G, i)
            row_stats_of(NB - 2, lambda t: full2[t] + NB - 1, NTT * (NB - 2))
            last_sum(NB - 1)
            row_stats_of(NB - 1, lambda t: full2[t] + NB, NTT * (NB - 1))
            aggregate(lambda t: full2[t] + NB)
            dve.wait_ge(lnrow_landed, 32)
            for m in range(len(DVE_PIECES) + 1):
                if m < len(DVE_PIECES):
                    t, c = DVE_PIECES[m]
                    x = yrow[0:TT, t, c]
                    nc.vector.scalar_tensor_tensor(out=x, in0=x, scalar=mv[0:TT, t, 0:1], in1=ln_w_row[0:TT, c],
                                                   op0=ALU.subtract, op1=ALU.mult).then_inc(yw_ready, 1)
                if m > 0:
                    if m == 1:
                        dve.wait_ge(row_scale, 4)
                    dve.wait_ge(yw_ready, m)
                    t, c = DVE_PIECES[m - 1]
                    x = yrow[0:TT, t, c]
                    nc.vector.scalar_tensor_tensor(out=x, in0=x, scalar=rstd[0:TT, t:t + 1], in1=ln_b_row[0:TT, c],
                                                   op0=ALU.mult, op1=ALU.add).then_inc(yb_ready, 1)

        @block.gpsimd
        def _(pool):
            pstep = [0]

            def seq(ins):
                ins.then_inc(pool_seq, 1)
                pstep[0] += 1
                pool.wait_ge(pool_seq, pstep[0])

            seq(nc.gpsimd.memset(ident[:, :], 0.0))
            nc.gpsimd.affine_select(out=ident[:, :], in_=ident[:, :], compare_op=ALU.not_equal, fill=1.0, base=0,
                                    pattern=[[-1, P]], channel_multiplier=1).then_inc(ident_ready, 1)
            nc.gpsimd.memset(ones[:, :], 1.0)
            seq(nc.gpsimd.memset(minus_half[:, :], -0.5))
            for m, (i, rows) in enumerate([(0, P), (2, T - 2 * P), (1, P)]):
                if i == 2:
                    pool.wait_ge(sums_ready, 3)
                    nc.gpsimd.tensor_scalar(var[0:rows, 2:3], sums[0:rows, 1:2], 1.0 / D, EPS, ALU.mult, ALU.add)\
                        .then_inc(var_ready, 1)
                    pool.wait_ge(var_ready, 1)
                else:
                    pool.wait_ge(row_stats, i + 1)
                nc.gpsimd.tensor_tensor(rstd[0:rows, i:i + 1], var[0:rows, i:i + 1], minus_half[0:rows, 0:1], ALU.pow)\
                    .then_inc(row_pow, 1)
                if i != 1:
                    pool.wait_ge(row_pow, m + 1)
                    nc.gpsimd.tensor_tensor(nbias[0:rows, i:i + 1], neg_mean[0:rows, i:i + 1], rstd[0:rows, i:i + 1],
                                            ALU.mult).then_inc(row_scale, 1)
            for started in (*s0_stored, S_stored, tail_stored):
                pool.sem_inc(started, 1)
            for k in range(1, KT, 2):
                pool.wait_ge(x_hi_ready, k + 1)
                nc.gpsimd.tensor_tensor(x_lo[:, k, :], hf[:, k % HF_SLOTS, :], x_hi[:, k, :].bitcast(F32), ALU.subtract)\
                    .then_inc(x_lo_ready[1], 1)
            seq(nc.gpsimd.memset(mask[:, :, :], 0.0))
            nc.gpsimd.affine_select(out=mask[:, 0, :], in_=mask[:, 0, :], compare_op=ALU.not_equal, fill=1.0, base=0,
                                    pattern=[[-1, P]], channel_multiplier=1)
            rights = []
            for m, L in enumerate(LEVELS):
                right = mask[:, m + 1, :].rearrange("p (b l) -> p b l", l=2 * L)[:, :, L:2 * L]
                rights.append(right)
                last = nc.gpsimd.memset(right, 1.0)
            seq(last)
            for m, L in enumerate(LEVELS):
                last = nc.gpsimd.affine_select(out=rights[m], in_=rights[m], compare_op=ALU.is_ge, fill=0.0, base=0,
                                               pattern=[[-2 * L, P // (2 * L)], [0, L]], channel_multiplier=1)
            seq(last)
            for m, L in enumerate(LEVELS):
                last = nc.gpsimd.affine_select(out=rights[m], in_=rights[m], compare_op=ALU.is_ge, fill=0.0, base=L - 1,
                                               pattern=[[2 * L, P // (2 * L)], [0, L]], channel_multiplier=-1)
            seq(last)
            seq(nc.gpsimd.tensor_copy(mask2[0:48, :, :], mask[0:48, 0:5, 0:48]))
            nc.gpsimd.memset(mask2[0:48, 3:5, META:48], 0.0)
            seq(nc.gpsimd.tensor_tensor(mask[:, 4, :], mask[:, 4, :], mask[:, 5, :], ALU.add))
            seq(nc.gpsimd.tensor_tensor(mask[:, 6, :], mask[:, 6, :], mask[:, 7, :], ALU.add))
            seq(nc.gpsimd.tensor_tensor(mask[:, 4, :], mask[:, 4, :], mask[:, 6, :], ALU.add))
            groups = [segmask[32 * q:32 * q + 32, :] for q in range(3)]
            seq(nc.gpsimd.memset(segmask[:, :], 1.0))
            for rows in groups:
                last = nc.gpsimd.affine_select(out=rows, in_=rows, compare_op=ALU.is_ge, fill=0.0, base=0,
                                               pattern=[[-DSEQ, NSEQ]], channel_multiplier=1)
            seq(last)
            for rows in groups:
                last = nc.gpsimd.affine_select(out=rows, in_=rows, compare_op=ALU.is_ge, fill=0.0, base=DSEQ - 1,
                                               pattern=[[DSEQ, NSEQ]], channel_multiplier=-1)
            last.then_inc(masks_ready, 1)
            pool.wait_ge(masks_ready, 1)
            pool.wait_ge(const_ready, 1)
            pool.wait_ge(g_free[3], 1)

            def load_state(h, i):
                s = i % S0_SLOTS
                per = len(range(s, NSEQ, S0_SLOTS))
                pool.wait_ge(s0_stored[s], 16 * (per * h + i // S0_SLOTS) + 1)
                pool.dma_start(S0[:, s, :, :], state_gla[0, i, bass.ds(h, 1), :, :]
                               .rearrange("o (d p) v -> p (o d) v", p=P)).then_inc(s0_landed[s], 16)

            def select_keys(h, i):
                if i >= 2:
                    pool.wait_ge(g_full[2], g_filled(h, 2, f"d{i - 2}"))
                    alone(pool)
                nc.gpsimd.tensor_scalar(kms[:, i % 2, :, :], kstk[:, :, :], segmask[0:96, i:i + 1], None, ALU.mult)\
                    .then_inc(kms_ready, 1)

            def deviation(h, c, rows):
                pool.wait_ge(ss_ready, 3 * h + c + 1)
                alone(pool)
                nc.gpsimd.tensor_scalar(ms[0:rows, c:c + 1], ss[0:rows, c:c + 1], 1.0 / DV, EPS, ALU.mult, ALU.add)\
                    .then_inc(ms_ready, 1)
                pool.wait_ge(ms_ready, 3 * h + c + 1)
                nc.gpsimd.tensor_tensor(rs[0:rows, c:c + 1], ms[0:rows, c:c + 1], minus_half[0:rows, 0:1], ALU.pow)\
                    .then_inc(rs_ready, 1)

            with pool.Fori(0, HEADS) as h:
                pool.dma_start(wa2h[:, :], w_a2[0, :, bass.ds(h * DK, DK)]).then_inc(wa2h_landed, 16)
                for i in range(S0_SLOTS):
                    load_state(h, i)
                pool.wait_ge(eb_ready, h + 1)
                alone(pool)
                nc.gpsimd.tensor_copy(ebl[:, :, 0:2], eb[:, :, CHUNK - 1:2 * CHUNK:CHUNK])
                nc.gpsimd.tensor_copy(ebl[:, :, 2:11], eb[:, :, PROMPT - 1:T:DSEQ]).then_inc(ebl_ready, 1)
                pool.wait_ge(bank_free[NB - 1], bank_frees(HG * h + 1))

                def decay(lv, hi):
                    L = LEVELS[lv]
                    pool.wait_ge(exp_ready, 7 * h + lv + 1)
                    for d in range(DT):
                        x = lev[:, lv % 4, d, 0:hi].rearrange("p (b l) -> p b l", l=2 * L)
                        q = QK[:, d, 0:hi].rearrange("p (b l) -> p b l", l=2 * L)
                        k = QK[:, DT + d, 0:hi].rearrange("p (b l) -> p b l", l=2 * L)
                        nc.gpsimd.tensor_tensor(x[:, :, 0:L], x[:, :, 0:L], k[:, :, 0:L], ALU.mult)
                        last = nc.gpsimd.tensor_tensor(x[:, :, L:2 * L], x[:, :, L:2 * L], q[:, :, L:2 * L], ALU.mult)
                    last.then_inc(lev_ready, 1)

                for lv in range(3):
                    decay(lv, T)
                pool.wait_ge(kdecay_ready, h + 1)
                nc.gpsimd.tensor_tensor(kh[:, :, :], kh[:, :, :], QK[:, DT:2 * DT, :], ALU.mult).then_inc(qk_pool, 1)
                nc.gpsimd.tensor_tensor(qh[:, :, :], QK[:, 0:DT, CHUNK:2 * CHUNK], eb[:, :, CHUNK:2 * CHUNK], ALU.mult)\
                    .then_inc(qk_pool, 1)
                nc.gpsimd.tensor_tensor(q_dec[:, 0:DT * 48].rearrange("p (d c) -> p d c", c=48)[:, :, 0:META],
                                        QK[:, 0:DT, 2 * CHUNK:PROMPT],
                                        eb[:, :, 2 * CHUNK:PROMPT], ALU.mult).then_inc(qk_pool, 1)
                q = tmpA[:, 0:DT * DEC].rearrange("p (d t) -> p d t", t=DEC)
                nc.gpsimd.tensor_tensor(q, QK[:, 0:DT, PROMPT:T], eb[:, :, PROMPT:T], ALU.mult).then_inc(q_step, 1)
                pool.wait_ge(q_step, 2 * h + 1)
                alone(pool)
                m = NSEQ - 1

                def columns(d, at):
                    flat, step = q_parts[:, d, :, :].rearrange("p a b -> p (a b)"), QW + DSEQ
                    first, end = at + META, at + META + m * step
                    return (flat[:, first:end].rearrange("p (i c) -> p i c", c=step)[:, :, 0:DSEQ],
                            flat[:, end:end + DSEQ].rearrange("p (i c) -> p i c", c=DSEQ))

                pieces = []
                for d in range(DT):
                    qs = q[:, d, :].rearrange("p (i c) -> p i c", c=DSEQ)
                    pieces += zip((qs[:, 0:m, :], qs[:, m:NSEQ, :]), columns(d, 0), columns(d, Q_LO))
                for x, hi, lo in pieces:
                    last = nc.gpsimd.tensor_copy(hi, x)
                last.then_inc(q_step, 1)
                pool.wait_ge(q_step, 2 * h + 2)
                for x, hi, lo in pieces:
                    last = nc.gpsimd.tensor_tensor(lo, x, hi.bitcast(F32), ALU.subtract)
                last.then_inc(qk_pool, 1)
                decay(3, T)
                pool.wait_ge(qk_pool, 5 * h + 1)
                alone(pool)
                nc.gpsimd.tensor_copy(kst[:, :, 0:DEC], kh[:, :, PROMPT:T])
                nc.gpsimd.tensor_copy(kst[:, :, 2 * DEC:3 * DEC], kh[:, :, PROMPT:T]).then_inc(pool_head, 1)
                pool.wait_ge(pool_head, h + 1)
                nc.gpsimd.tensor_tensor(kst[:, :, DEC:2 * DEC], kh[:, :, PROMPT:T], kst[:, :, 0:DEC].bitcast(F32),
                                        ALU.subtract).then_inc(qk_pool, 1)
                pool.wait_ge(bank_free[NB - 1], bank_frees(HG * h + 2))
                alone(pool)
                nc.gpsimd.tensor_copy(vst[:, :, 0:DEC], V[:, :, PROMPT:T]).then_inc(vst_ready, 1)
                nc.gpsimd.tensor_copy(vst[:, :, DEC:2 * DEC], V[:, :, PROMPT:T]).then_inc(vst_ready, 1)
                pool.wait_ge(vst_ready, 3 * h + 2)
                nc.gpsimd.tensor_tensor(vst[:, :, 2 * DEC:3 * DEC], V[:, :, PROMPT:T], vst[:, :, 0:DEC].bitcast(F32),
                                        ALU.subtract).then_inc(vst_ready, 1)
                for lv in (4, 5, 6):
                    decay(lv, 2 * CHUNK)
                nc.gpsimd.tensor_copy(uD[:, :, :, 0:2], stT[:, bass.ds(NB * h, NB), :]
                                      .rearrange("p n (i c) -> p n i c", c=2)).then_inc(uD_ready, 1)
                pool.wait_ge(u_ready, h + 1)
                alone(pool)
                nc.gpsimd.tensor_copy(uD[:, :, :, 2:6], A[:, :, PROMPT:T].rearrange("p n (i c) -> p n i c", c=DSEQ))\
                    .then_inc(uD_ready, 1)
                nc.gpsimd.tensor_copy(tails[:, :, 0:2], A[:, :, PROMPT - 2:PROMPT])
                nc.gpsimd.tensor_copy(tails[:, :, 2:18].rearrange("p n (i c) -> p n i c", c=2),
                                      A[:, :, PROMPT:T].rearrange("p n (i c) -> p n i c", c=DSEQ)[:, :, :, 2:4])\
                    .then_inc(tails_ready, 1)
                pool.wait_ge(g_free[3], g_emptied(h, 3, "kst"))
                alone(pool)
                select_keys(h, 0)
                select_keys(h, 1)
                for j in (5, 6, 7):
                    if j == 7:
                        pool.wait_ge(bank_free[NB - 1], bank_frees(HG * h + 6))
                        nc.gpsimd.tensor_tensor(QK[:, :, 0:N], QK[:, :, 0:N], Fs[:, :, :], ALU.mult)\
                            .then_inc(silu_ready, 1)
                    for i in PIECE_SEQS[j]:
                        if i + 2 < NSEQ:
                            select_keys(h, i + 2)
                    deviation(h, j - 5, 48 if j == 7 else CHUNK)
                    for i in PIECE_SEQS[j]:
                        if i + S0_SLOTS < NSEQ:
                            load_state(h, i + S0_SLOTS)

            def inverse_deviation(m):
                pool.wait_ge(row_stats, m)
                nc.gpsimd.tensor_tensor(rstd[0:TT, :], var[0:TT, :], minus_half[0:TT, :], ALU.pow).then_inc(row_scale, 1)

            with pool.Fori(0, NB - 1) as j:
                pool.wait_ge(bank_free[NB - 1], bank_frees(WO_G + j))
                alone(pool)
                nc.gpsimd.tensor_copy(mix[:, bass.ds(NB * j, NB), :], stage[:, :, :]).then_inc(stage_copied, 1)
            inverse_deviation(3)
            pool.wait_ge(bank_free[NB - 1], bank_frees(WO_G + NB - 1))
            nc.gpsimd.tensor_copy(mix[:, KT - NB:KT, :], stage[:, :, :]).then_inc(stage_copied, 1)
            for s in range(S0_SLOTS):
                pool.wait_ge(s0_stored[s], 1 + 16 * HEADS * len(range(s, NSEQ, S0_SLOTS)))
            pool.wait_ge(tail_stored, 1 + 32 * HEADS)
            for row, src in ((ln_w_row, ln2_w), (ln_b_row, ln2_b)):
                pool.dma_start(row[0:TT, :], src[0:1, :].to_broadcast([TT, D])).then_inc(lnrow_landed, 16)
            for i in range(len(NORM_STEPS)):
                if unit_of(i) % 2:
                    split_x1(pool, nc.gpsimd, i)
            for k in range(NB):
                pool.wait_ge(x1_ready[0], k + 2)
                pool.wait_ge(x1_ready[1], k + 1)
                x = mix[:, NB * k:NB * (k + 1), :]
                nc.gpsimd.tensor_scalar(x, x, ALPHA, None, ALU.mult).then_inc(acc_ready, 1)
            with pool.Fori(0, FB) as b:
                with pool.Fori(0, NB) as j:
                    pool.wait_ge(sq2_ready, NB * b + j + 2)
                    alone(pool)
                    f = bass.ds(NB * j, NB)
                    nc.gpsimd.tensor_copy(f_hi[:, f, :], pair[:, 1, :, :]).then_inc(fhi_ready, 1)
                    pool.wait_ge(fhi_ready, HEADS + NB * b + j + 1)
                    nc.gpsimd.tensor_tensor(f_lo[:, f, :], pair[:, 1, :, :], f_hi[:, f, :].bitcast(F32), ALU.subtract)\
                        .then_inc(f_ready, 1)
            inverse_deviation(4)
            pool.wait_ge(row_scale, 4)
            nc.gpsimd.tensor_tensor(nbias[0:TT, :], mv[0:TT, :, 0], rstd[0:TT, :], ALU.mult).then_inc(nbias_step, 1)
            pool.wait_ge(nbias_step, 1)
            nc.gpsimd.tensor_scalar(nbias[0:TT, :], nbias[0:TT, :], -1.0, None, ALU.mult).then_inc(nbias_ready, 1)
            pool.wait_ge(lnrow_landed, 32)
            for m, (t, c) in enumerate(POOL_PIECES):
                y = yrow[0:TT, t, c]
                pool.wait_ge(yn_ready, m + 1)
                nc.gpsimd.tensor_tensor(y, y, ln_w_row[0:TT, c], ALU.mult).then_inc(pool_w, 1)
                pool.wait_ge(pool_w, m + 1)
                nc.gpsimd.tensor_tensor(y, y, ln_b_row[0:TT, c], ALU.add).then_inc(pool_piece_ready, 1)


_INS = ["x_prompt", "x_sample", "state_conv", "state_gla", "meta", "ln_in_w", "ln_in_b", "w_in", "conv_w", "w_a2",
        "b_a2", "gn_w", "w_o", "ln1_w", "ln1_b", "w1", "w2", "ln2_w", "ln2_b"]
_OUTS = [(1, SEQ, D), (NSEQ, DSEQ, D), (1, 1, CW - 1, D), (1, 1, HEADS, DK, DV), (1, NSEQ, CW - 1, D),
         (1, NSEQ, HEADS, DK, DV)]


def kernel(**inputs):
    import numpy as _np
    import concourse.bacc as _bacc
    from concourse.bass_utils import run_bass_kernel_spmd as _run

    nc = _bacc.Bacc("TRN2", target_bir_lowering=False, num_devices=1)
    arrays, args = {}, []
    for name in _INS:
        a = _np.ascontiguousarray(inputs[name])
        arrays[f"in_{name}"] = a
        args.append(nc.dram_tensor(f"in_{name}", a.shape, F32, kind="ExternalInput").ap())
    for i, shape in enumerate(_OUTS):
        args.append(nc.dram_tensor(f"out_{i}", shape, F32, kind="ExternalOutput").ap())
    build(nc, *args)
    r = _run(nc, [arrays], core_ids=[0])
    return tuple(r.results[0][f"out_{i}"] for i in range(len(_OUTS)))
```
